# Optimizing a Trainium2 kernel written in Bass

```python
import numpy as np
import jax, jax.numpy as jnp
from jax import lax

D_MODEL = 1024
BATCH = 1
SEQ = 256
DEPTH = 2

GRID_W = 64
CTX_LEN = 256
M_HEADS = 4
M_DQK = 128
M_DV = 256
M_CHUNK = 64
M_QK = M_HEADS * M_DQK
M_V = M_HEADS * M_DV
M_GATES = 2 * 2 * M_HEADS
A_HEADS = 8
A_KV_HEADS = 2
A_GROUP = A_HEADS // A_KV_HEADS
A_HD = 128
A_Q = A_HEADS * A_HD
A_KV = A_KV_HEADS * A_HD
Q_BLOCK = 128
ROPE_THETA = 10000.0
C_WIDTH = D_MODEL
CONV_K = 3
D_FF = 4 * D_MODEL
N_MOD = 6
EPS = 1e-6
COL_SIZES = (M_QK, M_QK, M_V, M_V, M_GATES, A_Q, A_KV, A_KV, C_WIDTH, C_WIDTH, C_WIDTH, D_MODEL, D_MODEL, D_MODEL)
IN_COLS = sum(COL_SIZES)

kernel_name = 'hybrid_mlstm_gqa_shortconv_prefix_block'

def rms_norm(x, g):
    xf = x.astype(jnp.float32)
    y = xf * lax.rsqrt(jnp.mean(xf * xf, axis=-1, keepdims=True) + EPS)
    return (y * g).astype(x.dtype)

def modulate(x, shift, scale):
    return x * (1 + scale) + shift

def heads(t, n):
    return t.reshape(*t.shape[:-1], n, t.shape[-1] // n)

def split_columns(z):
    return jnp.split(z, np.cumsum(COL_SIZES)[:-1].tolist(), axis=-1)

def axial_rope_tables(n_tokens):
    rows = n_tokens // GRID_W
    row_idx = jnp.repeat(jnp.arange(rows), GRID_W)
    col_idx = jnp.tile(jnp.arange(GRID_W), rows)
    n_freq = A_HD // 4
    inv_freq = ROPE_THETA ** (-jnp.arange(n_freq, dtype=jnp.float32) / n_freq)
    pos = jnp.stack([row_idx, col_idx], axis=-1).astype(jnp.float32)
    ang = pos[:, :, None] * inv_freq
    return jnp.cos(ang), jnp.sin(ang)

def apply_rope(x, cos, sin):
    b, s, h, d = x.shape
    xr = x.astype(jnp.float32).reshape(b, s, h, 2, 2, d // 4)
    x1, x2 = xr[..., 0, :], xr[..., 1, :]
    cs = cos[None, :, None]
    sn = sin[None, :, None]
    out = jnp.stack([x1 * cs - x2 * sn, x1 * sn + x2 * cs], axis=-2)
    return out.reshape(b, s, h, d).astype(x.dtype)

def mlstm_scan(q, k, v, log_i, log_f, state):
    b, h, s, _ = q.shape
    dv = v.shape[-1]
    nc = s // M_CHUNK

    def chunks(t):
        return jnp.moveaxis(t.reshape(b, h, nc, M_CHUNK, *t.shape[3:]), 2, 0)

    tri = jnp.tril(jnp.ones((M_CHUNK, M_CHUNK), dtype=bool))

    def step(carry, inp):
        c_mat, n_vec, m = carry
        qc, kc, vc, ic, fc = inp
        bcum = jnp.cumsum(fc, axis=-1)
        d = jnp.where(tri, bcum[..., :, None] - bcum[..., None, :] + ic[..., None, :], -jnp.inf)
        inter = bcum + m[..., None]
        m_t = jnp.maximum(inter, jnp.max(d, axis=-1))
        w_intra = jnp.exp(d - m_t[..., None])
        w_inter = jnp.exp(inter - m_t)
        s_qk = jnp.einsum('bhtd,bhsd->bhts', qc, kc) * w_intra
        num = jnp.einsum('bhts,bhsv->bhtv', s_qk, vc) + w_inter[..., None] * jnp.einsum('bhtd,bhdv->bhtv', qc, c_mat)
        den = jnp.sum(s_qk, axis=-1) + w_inter * jnp.einsum('bhtd,bhd->bht', qc, n_vec)
        h_out = num / jnp.maximum(jnp.abs(den), jnp.exp(-m_t))[..., None]
        b_last = bcum[..., -1]
        g = b_last[..., None] - bcum + ic
        m_new = jnp.maximum(b_last + m, jnp.max(g, axis=-1))
        w_g = jnp.exp(g - m_new[..., None])
        w_c = jnp.exp(b_last + m - m_new)
        c_new = w_c[..., None, None] * c_mat + jnp.einsum('bhs,bhsd,bhsv->bhdv', w_g, kc, vc)
        n_new = w_c[..., None] * n_vec + jnp.einsum('bhs,bhsd->bhd', w_g, kc)
        return (c_new, n_new, m_new), h_out

    state, hs = lax.scan(step, state, (chunks(q), chunks(k), chunks(v), chunks(log_i), chunks(log_f)))
    return state, jnp.moveaxis(hs, 0, 2).reshape(b, h, s, dv)

def mlstm_inputs(parts, gate_b):
    mq, mk, mv, mg = parts[0], parts[1], parts[2], parts[4]
    bsz, n = mq.shape[:2]

    def hm(t):
        return jnp.swapaxes(heads(t, M_HEADS), 1, 2).astype(jnp.float32)

    gates = (mg.reshape(bsz, n, 2, 2, M_HEADS).astype(jnp.float32) + gate_b).transpose(0, 2, 3, 4, 1)
    return hm(mq) * (M_DQK ** -0.5), hm(mk), hm(mv), gates

def mlstm_bidirectional(q_l, k_l, v_l, g_l, q_c, k_c, v_c, g_c):
    bsz = q_l.shape[0]
    init = (jnp.zeros((bsz, M_HEADS, M_DQK, M_DV), jnp.float32),
            jnp.zeros((bsz, M_HEADS, M_DQK), jnp.float32),
            jnp.zeros((bsz, M_HEADS), jnp.float32))
    outs = []
    for direction in range(2):
        rev = (lambda t: jnp.flip(t, axis=2)) if direction == 1 else (lambda t: t)

        def run(q, k, v, g, state):
            return mlstm_scan(rev(q), rev(k), rev(v), rev(g[:, direction, 0]),
                              rev(jax.nn.log_sigmoid(g[:, direction, 1])), state)

        ctx_state, h_c = run(q_c, k_c, v_c, g_c, init)
        _, h_l = run(q_l, k_l, v_l, g_l, ctx_state)
        outs.append((rev(h_l), rev(h_c)))
    return outs[0][0] + outs[1][0], outs[0][1] + outs[1][1]

def mlstm_output(h, o_pre, gain):
    h = jnp.swapaxes(h, 1, 2)
    h = h * lax.rsqrt(jnp.mean(h * h, axis=-1, keepdims=True) + EPS)
    h = h.reshape(*h.shape[:2], M_V) * gain
    return (h * jax.nn.sigmoid(o_pre.astype(jnp.float32))).astype(o_pre.dtype)

def gqa_attend(q, k, v):
    s = jnp.einsum('bqhgd,bkhd->bhgqk', q, k).astype(jnp.float32) * (A_HD ** -0.5)
    p = jax.nn.softmax(s, axis=-1).astype(v.dtype)
    return jnp.einsum('bhgqk,bkhd->bqhgd', p, v)

def latent_attention(q, k_all, v_all):
    b, s = q.shape[:2]
    nb = s // Q_BLOCK
    qb = jnp.moveaxis(q.reshape(b, nb, Q_BLOCK, A_KV_HEADS, A_GROUP, A_HD), 1, 0)
    out = lax.map(lambda blk: gqa_attend(blk, k_all, v_all), qb)
    return jnp.moveaxis(out, 0, 1).reshape(b, s, A_Q)

def context_attention(q, k, v):
    b, n = q.shape[:2]
    return gqa_attend(q.reshape(b, n, A_KV_HEADS, A_GROUP, A_HD), k, v).reshape(b, n, A_Q)

def attn_q(parts, q_g):
    return rms_norm(heads(parts[5], A_HEADS), q_g)

def attn_kv(parts, k_g):
    return rms_norm(heads(parts[6], A_KV_HEADS), k_g), heads(parts[7], A_KV_HEADS)

def short_conv(u, w):
    up = jnp.pad(u, ((0, 0), (1, 1), (0, 0)))
    return w[0] * up[:, :-2] + w[1] * up[:, 1:-1] + w[2] * up[:, 2:]

def conv_branch(parts, w):
    u, gate_b, gate_c = parts[8], parts[9], parts[10]
    return gate_b * short_conv(gate_c * u, w)

def merge_branches(y_m, y_a, y_c, parts, w_pm, w_pa, w_pc, w_o):
    ga, gb, gc = parts[11], parts[12], parts[13]
    merged = (jax.nn.sigmoid(ga) * (y_m @ w_pm) + jax.nn.sigmoid(gb) * (y_a @ w_pa)
              + jax.nn.sigmoid(gc) * (y_c @ w_pc))
    return merged @ w_o

def squared_relu_mlp(h, w_up, w_down):
    return jnp.square(jax.nn.relu(h @ w_up)) @ w_down

def setup_inputs(seed: int = 0) -> dict:
    key = jax.random.key(seed)
    ks = jax.random.split(key, 24)
    nrm = jax.random.normal
    f32 = jnp.float32
    ib = 0.1 * nrm(ks[8], (DEPTH, 2, 1, M_HEADS), f32)
    fb = 3.0 + jnp.linspace(0.0, 3.0, M_HEADS, dtype=f32)[None, None, None, :] + 0.1 * nrm(ks[9], (DEPTH, 2, 1, M_HEADS), f32)
    return {
        'x': nrm(ks[0], (BATCH, SEQ, D_MODEL), f32),
        'c': nrm(ks[1], (BATCH, D_MODEL), f32),
        'ctx': nrm(ks[2], (BATCH, CTX_LEN, D_MODEL), f32),
        'c_ctx': nrm(ks[3], (D_MODEL,), f32),
        'w_ada': nrm(ks[4], (DEPTH, D_MODEL, N_MOD * D_MODEL), f32) * (0.5 * D_MODEL ** -0.5),
        'b_ada': 0.02 * nrm(ks[5], (DEPTH, N_MOD * D_MODEL), f32),
        'norm1': 1.0 + 0.05 * nrm(ks[6], (DEPTH, D_MODEL), f32),
        'norm2': 1.0 + 0.05 * nrm(ks[7], (DEPTH, D_MODEL), f32),
        'w_in': nrm(ks[10], (DEPTH, D_MODEL, IN_COLS), f32) * D_MODEL ** -0.5,
        'mlstm_gate_b': jnp.concatenate([ib, fb], axis=2),
        'mlstm_norm': 1.0 + 0.05 * nrm(ks[11], (DEPTH, M_V), f32),
        'q_norm': 1.0 + 0.05 * nrm(ks[12], (DEPTH, A_HD), f32),
        'k_norm': 1.0 + 0.05 * nrm(ks[13], (DEPTH, A_HD), f32),
        'conv_w': nrm(ks[14], (DEPTH, CONV_K, C_WIDTH), f32) * CONV_K ** -0.5,
        'w_proj_m': nrm(ks[15], (DEPTH, M_V, D_MODEL), f32) * M_V ** -0.5,
        'w_proj_a': nrm(ks[16], (DEPTH, A_Q, D_MODEL), f32) * A_Q ** -0.5,
        'w_proj_c': nrm(ks[17], (DEPTH, C_WIDTH, D_MODEL), f32) * C_WIDTH ** -0.5,
        'w_out': nrm(ks[18], (DEPTH, D_MODEL, D_MODEL), f32) * D_MODEL ** -0.5,
        'w_up': nrm(ks[19], (DEPTH, D_MODEL, D_FF), f32) * D_MODEL ** -0.5,
        'w_down': nrm(ks[20], (DEPTH, D_FF, D_MODEL), f32) * D_FF ** -0.5,
        'final_norm': 1.0 + 0.05 * nrm(ks[21], (D_MODEL,), f32),
    }

def reference(x, c, ctx, c_ctx, w_ada, b_ada, norm1, norm2, w_in, mlstm_gate_b, mlstm_norm, q_norm, k_norm,
              conv_w, w_proj_m, w_proj_a, w_proj_c, w_out, w_up, w_down, final_norm):
    cos, sin = axial_rope_tables(x.shape[1])
    for layer in range(DEPTH):
        need_ctx = layer < DEPTH - 1
        mod_l = jax.nn.silu(c) @ w_ada[layer] + b_ada[layer]
        mod_c = jax.nn.silu(c_ctx) @ w_ada[layer] + b_ada[layer]
        sh1, sc1, g1, sh2, sc2, g2 = jnp.split(mod_l[:, None, :], N_MOD, axis=-1)
        csh1, csc1, cg1, csh2, csc2, cg2 = jnp.split(mod_c, N_MOD, axis=-1)

        p_l = split_columns(modulate(rms_norm(x, norm1[layer]), sh1, sc1) @ w_in[layer])
        p_c = split_columns(modulate(rms_norm(ctx, norm1[layer]), csh1, csc1) @ w_in[layer])

        mq_l, mk_l, mv_l, mg_l = mlstm_inputs(p_l, mlstm_gate_b[layer])
        mq_c, mk_c, mv_c, mg_c = mlstm_inputs(p_c, mlstm_gate_b[layer])
        hm_l, hm_c = mlstm_bidirectional(mq_l, mk_l, mv_l, mg_l, mq_c, mk_c, mv_c, mg_c)
        ym_l = mlstm_output(hm_l, p_l[3], mlstm_norm[layer])

        aq_l = apply_rope(attn_q(p_l, q_norm[layer]), cos, sin)
        ak_l, av_l = attn_kv(p_l, k_norm[layer])
        ak_l = apply_rope(ak_l, cos, sin)
        ak_c, av_c = attn_kv(p_c, k_norm[layer])
        ya_l = latent_attention(aq_l, jnp.concatenate([ak_c, ak_l], axis=1), jnp.concatenate([av_c, av_l], axis=1))

        yc_l = conv_branch(p_l, conv_w[layer])

        x = x + g1 * merge_branches(ym_l, ya_l, yc_l, p_l, w_proj_m[layer], w_proj_a[layer], w_proj_c[layer], w_out[layer])
        x = x + g2 * squared_relu_mlp(modulate(rms_norm(x, norm2[layer]), sh2, sc2), w_up[layer], w_down[layer])

        if need_ctx:
            ym_c = mlstm_output(hm_c, p_c[3], mlstm_norm[layer])
            ya_c = context_attention(attn_q(p_c, q_norm[layer]), ak_c, av_c)
            yc_c = conv_branch(p_c, conv_w[layer])
            ctx = ctx + cg1 * merge_branches(ym_c, ya_c, yc_c, p_c, w_proj_m[layer], w_proj_a[layer], w_proj_c[layer], w_out[layer])
            ctx = ctx + cg2 * squared_relu_mlp(modulate(rms_norm(ctx, norm2[layer]), csh2, csc2), w_up[layer], w_down[layer])
    return rms_norm(x, final_norm)


_drawn_inputs = setup_inputs


def setup_inputs(seed=0):
    import zlib

    import numpy as np

    out = dict(_drawn_inputs(seed))
    spreads = {}
    factors = {'mlstm_norm': 8.0, 'q_norm': 8.0, 'k_norm': 8.0}
    for name, (base, spread) in spreads.items():
        noise = np.random.default_rng([zlib.crc32(name.encode()), seed]).standard_normal(out[name].shape)
        drawn = base * np.exp(spread * noise) if base else spread * noise
        out[name] = __import__('jax').numpy.asarray(drawn.astype(out[name].dtype))
    for name, factor in factors.items():
        out[name] = (out[name] * factor).astype(out[name].dtype)
    return out
```

```python
from contextlib import ExitStack

import numpy as np

import concourse.bass as bass
from concourse import mybir

F32 = mybir.dt.float32
F32R = mybir.dt.float32r
ALU = mybir.AluOpType
ACT = mybir.ActivationFunctionType
AX = mybir.AxisListType.X

P = 128
D = 1024
KT = D // P
DEPTH = 2
CTX = 256
LAT = 256
TOK = CTX + LAT
TT = TOK // P
GRID_W = 64
MH, MQK, MV = 4, 128, 256
AH, AKV, AHD = 8, 2, 128
CONV_K = 3
FF = 4 * D
PC = 256
NB = PC // P
NC = D // PC
EPS = 1e-6
ROPE_THETA = 10000.0
RAW = 3
KP = 5

SIZES = dict(mq=512, mk=512, mv=1024, mo=1024, mg=16, aq=1024, ak=256, av=256, cu=D, cb=D, cc=D, g0=D, g1=D, g2=D)
COL, _at = {}, 0
for _n, _s in SIZES.items():
    COL[_n] = _at
    _at += _s

ROW_ADA, ROW_N1, ROW_N2, ROW_MN, ROW_CONV, ROW_QN, ROW_KN = 0, 48, 56, 64, 72, 96, 97
ROWS = 98
BACK = [1, 0, 3, 2]


def make_constants():
    ident = np.eye(P, dtype=np.float32)
    rot = np.zeros((P, P), np.float32)
    for m in range(P):
        if m % 64 < 32:
            rot[m + 32, m] = -1.0
        else:
            rot[m - 32, m] = 1.0
    nf = AHD // 4
    inv = (np.float32(ROPE_THETA) ** (-np.arange(nf, dtype=np.float32) / np.float32(nf))).astype(np.float32)
    t = np.arange(LAT)
    pos = np.stack([t // GRID_W, t % GRID_W]).astype(np.float32)
    d = np.arange(P)
    ang = (pos[d // 64][:, :] * inv[d % 32][:, None]).astype(np.float32)
    sel = np.zeros((P, 4, 8), np.float32)
    for g in range(2):
        for dr in range(2):
            for h in range(MH):
                sel[dr * 8 + g * 4 + h, g * 2 + dr, dr * 4 + h] = 1.0
    return np.concatenate([ident, rot, np.cos(ang), np.sin(ang), sel.reshape(P, 32)], axis=1).astype(np.float32)


CONST_COLS = P + P + LAT + LAT + 32


def spans(l, d, s):
    if d == 0:
        out = [(P * s, TOK)]
    elif s < CTX // P:
        out = [(0, P * (s + 1)), (CTX, TOK)]
    else:
        out = [(CTX, P * (s + 1))]
    if l == DEPTH - 1:
        out = [(max(a, CTX), b) for a, b in out if b > CTX]
    if len(out) == 2 and out[0][1] == out[1][0]:
        out = [(out[0][0], out[1][1])]
    return out


def packed(l, d):
    at, res = 0, []
    for s in range(TT):
        row = []
        for a, b in spans(l, d, s):
            row.append((a, b, at))
            at += b - a
        res.append(row)
    return res


EPW = 1280


def make_plan():
    plan = []

    def panel(kind, l, c, b=0):
        plan.append(dict(k="panel", kind=kind, l=l, c=c, b=b))

    def step(k, l, **kw):
        plan.append(dict(k=k, l=l, **kw))

    def ada(l, a, b):
        for c in range(a, b):
            panel("ada", l, c)

    ada(0, 0, 8)
    for l in range(DEPTH):
        more = l < DEPTH - 1
        step("ss", l, n=1)
        if l:
            ada(l, 4, 8)
        step("spread", l, n=1)
        step("apply", l, n=1)
        step("gate_tok", l)
        panel("mk", l, 0)
        step("gate_rows", l)
        panel("mk", l, 1)
        step("gate_sel", l)
        panel("mq", l, 0)
        panel("mq", l, 1)
        step("gate_cols", l)
        for h in range(MH):
            panel("mv", l, h)
        for h in range(MH):
            step("weigh", l, h=h)
            panel("mo", l, h)
            ada(l, 8 + h, 9 + h)
            step("value", l, h=h)
            step("turn", l, h=h)
        stream = [("ak", 0), ("aq", 0), ("aq", 1), ("aq", 2), ("aq", 3), ("av", 0), ("gate", 0), ("proj", 0)]
        for j, (kind, c) in enumerate(stream):
            panel(kind, l, c)
            if j >= 3:
                step("qrot", l, j=j - 3)
            if 2 <= j <= 6:
                step("qbc", l, j=j - 2)
            if 1 <= j <= 5:
                step("qss", l, j=j - 1)
        seq = [("gate", c // 2, 0) if c % 2 == 0 else ("proj", c // 2, 0) for c in range(2, 8)]
        for i in range(AH + 2):
            if i < 6:
                panel(seq[i][0], l, seq[i][1], 0)
                ada(l, 12 + i, 13 + i)
            elif i == 6:
                ada(l, 18, 19)
                panel("gate", l, 0, 1)
            elif i == 7:
                ada(l, 19, 20)
                if more:
                    ada(l + 1, 0, 1)
            elif more:
                ada(l + 1, i - 7, i - 6)
            if i >= 2:
                step("attend", l, h=i - 2)
            if 1 <= i <= AH:
                step("probs", l, h=i - 1)
            if i < AH:
                step("scores", l, h=i)
        for j in range(4):
            step("ysplit", l, j=j)
        for c in range(NC):
            if c:
                panel("gate", l, c, 1)
            panel("proj", l, c, 1)
        for c in range(NC):
            panel("cc", l, c)
            panel("cu", l, c)
            panel("cb", l, c)
            if more and c == 0:
                ada(l + 1, 3, 4)
        for c in range(NC):
            panel("gate", l, c, 2)
            if c == NC - 1:
                for j in range(NC - 1):
                    step("msplit", l, j=j)
            panel("proj", l, c, 2)
        step("msplit", l, j=NC - 1)
        for c in range(NC):
            panel("wo", l, c)
        step("ss", l, n=2)
        ada(l, 20, 24)
        step("spread", l, n=2)
        step("apply", l, n=2)
        for g in range(FF // D):
            for c in range(NC):
                panel("up", l, c, g)
            for c in range(NC):
                panel("down", l, c, g)
    step("ss", DEPTH, n=1)
    step("spread", DEPTH, n=1)
    step("final", DEPTH)

    p = s = 0
    uses = [0, 0, 0, 0]
    for st in plan:
        if st["k"] == "panel":
            st["p"] = p
            p += 1
            if st["kind"] != "ada":
                st["s"] = s
                s += 1
        st["u"] = {}

    def use(st, name, bank):
        st["u"][name] = (bank, uses[bank])
        uses[bank] += 1

    start = dict(k="start", l=0, u={})
    for name in range(3):
        use(start, f"par{name}", name)
    for kt in range(KT):
        use(start, f"x{kt}", kt % 4)
    for st in plan:
        k = st["k"]
        if k == "ss":
            use(st, "ss", 3)
        elif k == "spread":
            use(st, "r", 2)
        elif k == "gate_tok":
            use(st, "g", 0)
        elif k == "gate_rows":
            use(st, "g", 1)
        elif k == "gate_sel":
            use(st, "i", 2)
            use(st, "f", 3)
        elif k == "gate_cols":
            use(st, "g", 0)
        elif k == "weigh":
            use(st, "m0", 3)
            use(st, "m1", 2)
            use(st, "s0", 0)
            use(st, "s1", 1)
            use(st, "s2", 3)
        elif k == "value":
            for tt in range(TT) if st["l"] < DEPTH - 1 else range(CTX // P, TT):
                for d in range(2):
                    use(st, (tt, d), (2 * tt + d) % 4)
        elif k == "turn":
            use(st, 0, 0)
            use(st, 1, 1)
        elif k == "qss":
            use(st, 0, 3)
        elif k == "qbc":
            use(st, 0, 0)
            use(st, 1, 1)
        elif k == "qrot":
            use(st, 0, 2)
        elif k in ("scores", "probs"):
            for b in range(3 if st["l"] < DEPTH - 1 else 2):
                use(st, b, b)
        elif k == "attend":
            use(st, 0, 3)
        elif k == "final":
            for i in range(4):
                use(st, i, i)
    return [start] + plan, p, s


PLAN, NPANELS, NSPLIT = make_plan()
PANELS = [st for st in PLAN if st["k"] == "panel"]


def panel_no(kind, l, c, b=0):
    return next(st["p"] for st in PANELS if (st["kind"], st["l"], st["c"], st["b"]) == (kind, l, c, b))


def trunk(nc, x, c, ctx_in, c_ctx, w_ada, b_ada, norm1, norm2, w_in, gate_b, mnorm, qnorm, knorm, conv_w,
          w_pm, w_pa, w_pc, w_out, w_up, w_down, fnorm, consts, out):
    ctx = ExitStack()
    with ctx:
        place = {}
        base = (nc.sbuf_base + 63) // 64 * 64

        def at(name, shape, dt, offset):
            return nc.alloc_sbuf_tensor_at(name, shape, dt, offset=base + offset)

        K16 = KT * TOK * 4
        o = 0
        xT = at("xT", [P, KT, TOK], F32, o); o += K16
        hH = at("hH", [P, KT, TOK], F32R, o); o += K16
        hL = at("hL", [P, KT, TOK], F32R, o); o += K16
        raw = at("raw", [P, RAW, KT, PC], F32, o); o += RAW * KT * PC * 4
        wH = at("wH", [P, 2, KT, PC], F32R, o); o += 2 * KT * PC * 4
        wL = at("wL", [P, 2, KT, PC], F32R, o); o += 2 * KT * PC * 4
        Y = o
        yH = at("yH", [P, KT, TOK], F32R, o); o += K16
        yL = at("yL", [P, KT, TOK], F32R, o); o += K16
        names = ["g_rows", "g_back", "f_pre", "f_neg", "f_exp", "log_f", "F_run", "a_run", "e_run"]
        rows = {n: at(n, [16, TOK], F32, Y + i * TOK * 4) for i, n in enumerate(names)}
        rows["a_back"] = at("a_back", [16, TOK], F32, Y + 9 * TOK * 4)
        rows["e_back"] = at("e_back", [16, TOK], F32, Y + 10 * TOK * 4)
        rows["ones"] = at("ones_row", [16, TOK], F32, Y + 11 * TOK * 4)
        rows["M_run"] = at("M_run", [16, TOK], F32, Y + 14 * TOK * 4)
        rows["M_back"] = at("M_back", [16, TOK], F32, Y + 15 * TOK * 4)
        G = o
        merged = at("merged", [P, KT, TOK], F32, o); o += K16
        x_in = at("x_in", [P, TT, D], F32, G)
        qk = at("qk", [P, MH, 2, TOK], F32, G)
        hM = at("hM", [P, MH, TT, MV], F32, G)
        T = o
        vaug = at("vaug", [P, TT, MH, MV + 1], F32, T)
        EP = at("EP", [P, 2, EPW], F32, T + 16448)
        sig_o = at("sig_o", [P, 2, NB, TOK], F32, T + 26688)
        y_tmp = at("y_tmp", [P, NB, TOK], F32, T + 34944)
        junk = at("junk", [P, MV], F32, T + 39040)
        g_tok = at("g_tok", [P, TT, 16], F32, T + 40064)
        g_col = at("g_col", [P, 4, TT, 8], F32, T + 40320)
        mstat = at("mstat", [P, TT, 6], F32, T + 40832)
        mss = at("mss", [P, TT], F32, T + 40960)
        mrs = at("mrs", [P, TT], F32, T + 41024)
        w_gate = at("w_gate", [P, KT, 16], F32, T + 41088)
        wgH = at("wgH", [P, KT, 16], F32R, T + 41600)
        wgL = at("wgL", [P, KT, 16], F32R, T + 42112)
        gb = at("gb", [8, 2], F32, T + 42624)
        v_a = at("v_a", [P, TT, PC], F32, T)
        k_a = at("k_a", [P, NB, TOK], F32, T + 4096)
        q_a = at("q_a", [P, AH, TOK], F32, T + 8192)
        pr = at("pr", [P, 6 * 256], F32, T + 24576)
        prT = at("prT", [P, 6 * 256], F32, T + 30720)
        q_sq = at("q_sq", [P, NB, TOK], F32, T + 30720)
        q_t = at("q_t", [P, NB, LAT], F32, T + 40960)
        c_sb = at("c_sb", [P, NB, TOK], F32, T)
        c_u = at("c_u", [P, NB, 2, LAT + 2], F32, T + 4096)
        c_acc = at("c_acc", [P, NB, 2, LAT], F32, T + 8256)
        n_sq = at("n_sq", [P, 2, TOK], F32, T)
        n_t = at("n_t", [P, 2, TOK], F32, T + 6144)
        n_h = at("n_h", [P, 4, TOK], F32, T + 10240)
        f_out = at("f_out", [P, 2, D], F32, T + 20480)
        par_rows = [at(f"par_rows{i}", [P, P], F32, T + 30720 + 512 * i) for i in range(3)]
        o = T + 43008
        gs = at("gs", [P, NB, TOK], F32, o); o += NB * TOK * 4
        con = at("con", [P, CONST_COLS], F32, o); o += (CONST_COLS * 4 + 31) // 32 * 32
        small = at("small", [P, 32], F32, o); o += 128
        mean_d, mean_h, eps = small[:, 0:1], small[:, 1:2], small[:, 2:3]
        n_sd, n_rs = small[:, 4:8], small[:, 8:12]
        q_sd, q_rs = small[:, 16:24], small[:, 24:32]
        pars = [at(f"pars{i}", [P, P], F32, o + 512 * i) for i in range(3)]; o += 1536
        modT = at("modT", [P, 2, 48, 2], F32, o); o += 768
        c2 = at("c2", [P, KT, 2], F32, o); o += 64
        c2e = at("c2e", [P, KT, 2], F32, o); o += 64
        gain = at("gain", [P, KT, 2], F32, o); o += 64
        amax = at("amax", [P, 4], F32, o); o += 32
        anb = at("anb", [P, 4], F32, o); o += 32
        asum = at("asum", [P, 4], F32, o); o += 32
        ars = at("ars", [P, 4], F32, o); o += 32

        ident, rot = con[:, 0:P], con[:, P:2 * P]
        ropeC, ropeS = con[:, 2 * P:2 * P + LAT], con[:, 2 * P + LAT:2 * P + 2 * LAT]
        sel = con[:, 2 * P + 2 * LAT:CONST_COLS].rearrange("p (g m) -> p g m", g=4)

        pp = ctx.enter_context(nc.psum_tensor("pp", [P, 2, NB, TOK], F32))
        pc = ctx.enter_context(nc.psum_tensor("pc", [P, 4, TOK], F32))

        def sem(name):
            return ctx.enter_context(nc.semaphore(name))

        s_small = sem("small_loaded")
        s_x = sem("x_loaded")
        s_wg = sem("gate_weights_loaded")
        s_raw = [sem(f"raw_loaded{i}") for i in range(RAW)]
        s_out = sem("out_stored")
        wH_ready = sem("weights_high_ready")
        wL_ready = sem("weights_rest_ready")
        panel_done = sem("panel_done")
        slot_free = [sem(f"slot_free{i}") for i in range(2)]
        full = [sem(f"bank_full{i}") for i in range(4)]
        free = [sem(f"bank_free{i}") for i in range(4)]
        s_const = sem("constants_ready")
        s_silu = sem("silu_ready")
        s_cexp = sem("c_exp_ready")
        s_xt = sem("x_turned")
        s_par = sem("params_ready")
        x_ready = sem("x_pair_ready")
        sd_ready = sem("deviation_ready")
        rs_ready = sem("reciprocal_ready")
        qsd_ready = sem("q_deviation_ready")
        qrs_ready = sem("q_reciprocal_ready")
        mrs_ready = sem("h_deviation_ready")
        ot_ready = sem("h_turned_scaled")
        wLv_ready = sem("weights_rest_vector_ready")
        sq_ready = sem("squares_ready")
        sq_used = sem("squares_used")
        hf_ready = sem("h_float_ready")
        hH_ready = sem("h_high_ready")
        h_ready = sem("h_ready")
        y_ready = sem("y_ready")
        yf_ready = sem("y_float_ready")
        yH_ready = sem("y_high_ready")
        wgH_ready = sem("gate_w_high_ready")
        wg_ready = sem("gate_w_ready")
        g_ready = sem("gates_tok_ready")
        gr_ready = sem("gates_rows_ready")
        fneg_ready = sem("f_neg_ready")
        fln_ready = sem("f_ln_ready")
        erow_ready = sem("e_row_ready")
        eexp_ready = sem("e_exp_ready")
        cols_in = sem("gate_cols_inputs")
        gc_ready = sem("gate_cols_ready")
        mqk_ready = sem("mqk_ready")
        mv_ready = sem("mv_ready")
        E_ready = sem("E_ready")
        P_ready = sem("P_ready")
        mask_ready = sem("mask_ready")
        hraw_ready = sem("h_out_ready")
        hss_ready = sem("h_ss_ready")
        hn_ready = sem("h_norm_ready")
        so_exp = sem("sig_o_exp_ready")
        aqk_in = sem("aqk_copied")
        qsq_ready = sem("q_squares_ready")
        qn_ready = sem("q_normed")
        qk_ready = sem("qk_roped")
        av_ready = sem("av_ready")
        nb_ready = sem("neg_max_ready")
        p_exp = sem("p_exp_ready")
        p_ready = sem("p_scaled")
        pT_ready = sem("pT_ready")
        ya_ready = sem("ya_ready")
        gate_exp = sem("gate_exp_ready")
        mt_ready = sem("merge_term_ready")
        m_ready = sem("merged_ready")
        cc_ready = sem("cc_copied")
        cu_ready = sem("cu_ready")
        cpad = sem("conv_pad_zeroed")
        c1_ready = sem("conv_first_tap")
        up_ready = sem("up_relu_ready")
        f_ready = sem("final_rows_ready")
        vones = sem("value_ones")
        orow = sem("ones_row_ready")

        def cols(l):
            return slice(0, TOK) if l < DEPTH - 1 else slice(CTX, TOK)

        def halves(l):
            return [(slice(CTX, TOK), 0)] + ([(slice(0, CTX), 1)] if l < DEPTH - 1 else [])

        def panel_source(st):
            kind, l, c, b = st["kind"], st["l"], st["c"], st["b"]
            if kind == "ada":
                w, at_ = w_ada[l], 0
            elif kind in COL:
                w, at_ = w_in[l], COL[kind]
            elif kind == "gate":
                w, at_ = w_in[l], COL[f"g{b}"]
            elif kind == "proj":
                w, at_ = (w_pm, w_pa, w_pc)[b][l], 0
            elif kind == "wo":
                w, at_ = w_out[l], 0
            elif kind == "up":
                w, at_ = w_up[l], b * D
            else:
                w, at_ = w_down[l][b * D:(b + 1) * D, :], 0
            return w.rearrange("(k p) n -> p k n", p=P)[:, :, at_ + c * PC:at_ + (c + 1) * PC]

        y_no, h_no = {}, {}
        n_y = n_h_ = n_x = 0
        x_no = {}
        for st in PLAN:
            k, l = st["k"], st["l"]
            if k == "turn":
                y_no[l, "m", st["h"]] = n_y; n_y += 1
            elif k == "ysplit":
                y_no[l, "a", st["j"]] = n_y; n_y += 1
            elif k == "panel" and st["kind"] == "cb":
                y_no[l, "c", st["c"]] = n_y; n_y += 1
            elif k == "panel" and st["kind"] == "up":
                y_no[l, "up", st["b"], st["c"]] = n_y; n_y += 1
            elif k == "apply":
                h_no[l, st["n"]] = n_h_; n_h_ += KT
            elif k == "msplit":
                h_no[l, "m", st["j"]] = n_h_; n_h_ += 1
            elif k == "panel" and st["kind"] in ("wo", "down"):
                x_no[l, st["kind"], st["b"], st["c"]] = n_x; n_x += 1

        taken = [no for key, no in sorted(y_no.items(), key=lambda kv: kv[1]) if key[1] != "a"]
        yf_of = {no: i for i, no in enumerate(taken)}

        def x_needed(st):
            l, n = st["l"], st["n"]
            if l == 0 and n == 1:
                return 0
            if n == 2:
                return x_no[l, "wo", 0, NC - 1] + 1
            return x_no[l - 1, "down", FF // D - 1, NC - 1] + 1

        def operand(st):
            kind, l, c, b = st["kind"], st["l"], st["c"], st["b"]
            if kind == "proj":
                br = "mac"[b]
                return yH, yL, y_ready, lambda kt: y_no[l, br, kt // 2] + 1
            if kind == "wo":
                return hH, hL, h_ready, lambda kt: h_no[l, "m", kt // 2] + 1
            if kind == "down":
                return yH, yL, y_ready, lambda kt: y_no[l, "up", b, kt // 2] + 1
            n = 2 if kind == "up" else 1
            return hH, hL, h_ready, lambda kt: h_no[l, n] + kt + 1

        def next_panel(st):
            p = st["p"] + 1
            return PANELS[p] if p < NPANELS and "s" in PANELS[p] else None

        def raw_arrived(eng, p):
            eng.wait_ge(s_raw[p % RAW], 16 * (p // RAW + 1))

        def bank(eng, u, what=None):
            b, n = u
            eng.wait_ge(full[b], n + 1)
            return pc[:, b, :]

        n_fin = KT * 2 * DEPTH
        dchain = sem("vector_chain")

        def spans_tt(l):
            return list(range(TT)) if l < DEPTH - 1 else list(range(CTX // P, TT))

        def norm_tiles(st):
            only_latent = st["l"] == DEPTH or (st["l"] == DEPTH - 1 and st["n"] == 2)
            return range(CTX // P, TT) if only_latent else range(TT)

        block = ctx.enter_context(nc.Block())

        @block.sync
        def _(sp):
            sp.dma_start(con[:, :], consts).then_inc(s_small, 16)
            for l in range(DEPTH):
                pr_ = par_rows[l]
                for row, src, n in ((ROW_ADA, b_ada[l], 48), (ROW_N1, norm1[l], 8), (ROW_N2, norm2[l], 8),
                                    (ROW_MN, mnorm[l], 8), (ROW_QN, qnorm[l], 1), (ROW_KN, knorm[l], 1)):
                    sp.dma_start(pr_[row:row + n, :], src.rearrange("(r q) -> r q", q=P)).then_inc(s_small, 16)
                sp.dma_start(pr_[ROW_CONV:ROW_CONV + 24, :],
                             conv_w[l].rearrange("k (r q) -> (k r) q", q=P)).then_inc(s_small, 16)
            sp.dma_start(par_rows[2][0:8, :], c.rearrange("a (r q) -> (a r) q", q=P)).then_inc(s_small, 16)
            sp.dma_start(par_rows[2][8:16, :], c_ctx.rearrange("(r q) -> r q", q=P)).then_inc(s_small, 16)
            sp.dma_start(par_rows[2][16:24, :], fnorm.rearrange("(r q) -> r q", q=P)).then_inc(s_small, 16)
            sp.dma_start(x_in[:, 0:2, :], ctx_in[0].rearrange("(t p) d -> p t d", p=P)).then_inc(s_x, 16)
            sp.dma_start(x_in[:, 2:4, :], x[0].rearrange("(t p) d -> p t d", p=P)).then_inc(s_x, 16)
            for st in PLAN:
                if st["k"] == "gate_tok":
                    l = st["l"]
                    if l:
                        sp.wait_ge(panel_done, panel_no("down", l - 1, NC - 1, FF // D - 1) + 1)
                    else:
                        sp.wait_ge(s_par, 3)
                    sp.dma_start(w_gate[:, :, :], w_in[l].rearrange("(k p) n -> p k n", p=P)[
                        :, :, COL["mg"]:COL["mg"] + 16]).then_inc(s_wg, 16)
                    for g in range(2):
                        for dr in range(2):
                            sp.dma_start(gb[dr * 4:dr * 4 + 4, g:g + 1],
                                         gate_b[l, dr, g].rearrange("(h a) -> h a", a=1)).then_inc(s_wg, 16)
                if st["k"] != "panel":
                    continue
                p = st["p"]
                if p >= RAW:
                    old = PANELS[p - RAW]
                    if "s" in old:
                        sp.wait_ge(wL_ready, old["s"] + 1)
                        sp.wait_ge(wLv_ready, old["s"] + 1)
                    else:
                        sp.wait_ge(panel_done, old["p"] + 1)
                sp.dma_start(raw[:, p % RAW, :, :], panel_source(st)).then_inc(s_raw[p % RAW], 16)
            ov = out[0].rearrange("(t p) d -> p t d", p=P)
            for tt in range(2):
                sp.wait_ge(f_ready, tt + 1)
                sp.dma_start(ov[:, tt, :], f_out[:, tt, :]).then_inc(s_out, 16)
            sp.wait_ge(s_out, 32)

        @block.tensor
        def _(pe):
            def claim(u):
                b, n = u
                if n:
                    pe.wait_ge(free[b], n)
                return pc[:, b, :]

            def filled(ins, u):
                ins.then_inc(full[u[0]], 1)

            def run_panel(st):
                p, kind, l = st["p"], st["kind"], st["l"]
                slot = p % 2
                if p >= 2:
                    pe.wait_ge(slot_free[slot], p // 2)
                if kind == "ada":
                    raw_arrived(pe, p)
                    if p == 0:
                        pe.wait_ge(s_silu, 1)
                    for b in range(NB):
                        for kt in range(KT):
                            last = pe.matmul(pp[:, slot, b, 0:2], raw[:, p % RAW, kt, b * P:(b + 1) * P], c2[:, kt, :],
                                             start=kt == 0, stop=kt == KT - 1)
                    last.then_inc(panel_done, 1)
                    return
                ws = st["s"] % 2
                pe.wait_ge(wL_ready, st["s"] + 1)
                pe.wait_ge(wLv_ready, st["s"] + 1)
                hi, lo, ready, need = operand(st)
                if kind in ("mv", "av"):
                    pe.wait_ge(ready, need(KT - 1))
                    for tt in range(TT):
                        dst = pp[:, slot, tt // 2, (tt % 2) * PC:(tt % 2 + 1) * PC]
                        ts_ = slice(tt * P, (tt + 1) * P)
                        for kt in range(KT):
                            pe.matmul(dst, hi[:, kt, ts_], wH[:, ws, kt, :], start=kt == 0, stop=False)
                            pe.matmul(dst, hi[:, kt, ts_], wL[:, ws, kt, :], start=False, stop=False)
                            last = pe.matmul(dst, lo[:, kt, ts_], wH[:, ws, kt, :], start=False, stop=kt == KT - 1)
                    last.then_inc(panel_done, 1)
                    return
                ts_ = slice(0, TOK) if kind in ("mk", "ak") else cols(l)
                seen = 0
                for kt in range(KT):
                    if need(kt) > seen:
                        seen = need(kt)
                        pe.wait_ge(ready, seen)
                    for b in range(NB):
                        dst = pp[:, slot, b, ts_]
                        w = slice(b * P, (b + 1) * P)
                        pe.matmul(dst, wH[:, ws, kt, w], hi[:, kt, ts_], start=kt == 0, stop=False)
                        pe.matmul(dst, wH[:, ws, kt, w], lo[:, kt, ts_], start=False, stop=False)
                        last = pe.matmul(dst, wL[:, ws, kt, w], hi[:, kt, ts_], start=False, stop=kt == KT - 1)
                last.then_inc(panel_done, 1)

            n_norm = 0
            for st in PLAN:
                k, l, u = st["k"], st["l"], st["u"]
                if k == "panel":
                    run_panel(st)
                elif k == "start":
                    pe.wait_ge(s_small, 16 * (1 + 7 * DEPTH + 3))
                    for i in range(3):
                        n = ROWS if i < 2 else 24
                        b = claim(u[f"par{i}"])
                        filled(pe.transpose(b[:, 0:n], par_rows[i][0:n, :], ident[0:n, 0:n]), u[f"par{i}"])
                    pe.wait_ge(s_x, 32)
                    for kt in range(KT):
                        b = claim(u[f"x{kt}"])
                        for tt in range(TT):
                            last = pe.transpose(b[:, tt * P:(tt + 1) * P], x_in[:, tt, kt * P:(kt + 1) * P], ident)
                        filled(last, u[f"x{kt}"])
                elif k == "ss":
                    b = claim(u["ss"])
                    if n_norm == 0:
                        pe.wait_ge(s_const, 3)
                    for kt in range(KT):
                        pe.wait_ge(sq_ready, n_norm * KT + kt + 1)
                        tts = norm_tiles(st)
                        for tt in tts:
                            last = pe.matmul(b[:, tt:tt + 1], n_sq[:, kt % 2, tt * P:(tt + 1) * P], mean_d,
                                             start=kt == 0 and tt == tts[0], stop=kt == KT - 1, skip_group_check=True)
                        if kt < KT - 1:
                            last.then_inc(sq_used, 1)
                    filled(last, u["ss"])
                    n_norm += 1
                elif k == "spread":
                    b = claim(u["r"])
                    pe.wait_ge(rs_ready, n_norm)
                    for tt in norm_tiles(st):
                        last = pe.matmul(b[:, tt * P:(tt + 1) * P], n_rs[:, tt:tt + 1].to_broadcast([P, P]), ident,
                                         start=True, stop=True)
                    filled(last, u["r"])
                elif k == "gate_tok":
                    b = claim(u["g"])
                    pe.wait_ge(wg_ready, l + 1)
                    pe.wait_ge(h_ready, h_no[l, 1] + KT)
                    for tt in range(TT):
                        for kt in range(KT):
                            dst, hs = b[:, tt * 16:(tt + 1) * 16], slice(tt * P, (tt + 1) * P)
                            pe.matmul(dst, hH[:, kt, hs], wgH[:, kt, :], start=kt == 0, stop=False)
                            pe.matmul(dst, hH[:, kt, hs], wgL[:, kt, :], start=False, stop=False)
                            last = pe.matmul(dst, hL[:, kt, hs], wgH[:, kt, :], start=False, stop=kt == KT - 1)
                    filled(last, u["g"])
                elif k == "gate_rows":
                    b = claim(u["g"])
                    pe.wait_ge(g_ready, l + 1)
                    for tt in range(TT):
                        last = pe.transpose(b[0:16, tt * P:(tt + 1) * P], g_tok[:, tt, :], ident)
                    filled(last, u["g"])
                elif k == "gate_sel":
                    pe.wait_ge(gr_ready, 3 * l + 3)
                    for name, g in (("i", 0), ("f", 1)):
                        b = claim(u[name])
                        pe.matmul(b[0:8, :], sel[0:16, 2 * g, :], rows["g_rows"][:, :], start=True, stop=False)
                        last = pe.matmul(b[0:8, :], sel[0:16, 2 * g + 1, :], rows["g_back"][:, :], start=False, stop=True)
                        filled(last, u[name])
                elif k == "gate_cols":
                    b = claim(u["g"])
                    pe.wait_ge(cols_in, 4 * l + 4)
                    for i, name in enumerate(("a_run", "a_back", "e_run", "e_back")):
                        for tt in range(TT):
                            c0 = (i * TT + tt) * 8
                            last = pe.matmul(b[:, c0:c0 + 8], rows[name][0:8, tt * P:(tt + 1) * P], ident[0:8, 0:8],
                                             start=True, stop=True)
                    filled(last, u["g"])
                elif k == "weigh":
                    h = st["h"]
                    for d in range(2):
                        b = claim(u[f"m{d}"])
                        src = rows["M_run" if d == 0 else "M_back"]
                        r = d * MH + h
                        last = pe.matmul(b[:, :], ident[0:8, r:r + 1].to_broadcast([8, P]), src[0:8, :], start=True, stop=True)
                        filled(last, u[f"m{d}"])
                    pe.wait_ge(mqk_ready, 4 * l + 4)
                    for s in range(2):
                        b = claim(u[f"s{s}"])
                        filled(pe.matmul(b[:, cols(l)], qk[:, h, 1, s * P:(s + 1) * P], qk[:, h, 0, cols(l)],
                                         start=True, stop=True), u[f"s{s}"])
                    b = claim(u["s2"])
                    for s in range(2, 4):
                        last = pe.matmul(b[:, (s - 2) * LAT:(s - 1) * LAT], qk[:, h, 1, s * P:(s + 1) * P],
                                         qk[:, h, 0, CTX:TOK], start=True, stop=True)
                    filled(last, u["s2"])
                elif k == "value":
                    h = st["h"]
                    n = l * MH + h + 1
                    pe.wait_ge(P_ready, n)
                    pe.wait_ge(mask_ready, n)
                    pe.wait_ge(mv_ready, MH * l + h + 1)
                    pe.wait_ge(vones, l + 1)
                    for tt in sorted({key[0] for key in u}):
                        for d in range(2):
                            b = claim(u[tt, d])
                            terms = [(s, off + tt * P - a) for s, row in enumerate(packed(l, d)) for a, e, off in row
                                     if a <= tt * P < e]
                            for i, (s, off) in enumerate(terms):
                                last = pe.matmul(b[:, 0:MV + 1], EP[:, d, off:off + P], vaug[:, s, h, :],
                                                 start=i == 0, stop=i == len(terms) - 1)
                            filled(last, u[tt, d])
                elif k == "turn":
                    h = st["h"]
                    tts = range(TT) if l < DEPTH - 1 else range(CTX // P, TT)
                    pe.wait_ge(hn_ready, l * MH + h + 1)
                    for j in range(2):
                        b = claim(u[j])
                        for tt in tts:
                            last = pe.transpose(b[:, tt * P:(tt + 1) * P], hM[:, h, tt, j * P:(j + 1) * P], ident)
                        filled(last, u[j])
                elif k == "qss":
                    j = st["j"]
                    ts_ = slice(0, TOK) if j == 0 else cols(l)
                    pe.wait_ge(qsq_ready, l * 5 + j + 1)
                    b = claim(u[0])
                    for b_ in range(NB):
                        for tt in range(ts_.start // P, TT):
                            last = pe.matmul(b[:, b_ * TT + tt:b_ * TT + tt + 1], q_sq[:, b_, tt * P:(tt + 1) * P], mean_h,
                                             start=True, stop=True)
                    filled(last, u[0])
                elif k == "qbc":
                    j = st["j"]
                    pe.wait_ge(qrs_ready, l * 5 + j + 1)
                    for b_ in range(NB):
                        b = claim(u[b_])
                        for tt in range(0 if j == 0 else cols(l).start // P, TT):
                            n = b_ * TT + tt
                            last = pe.matmul(b[:, tt * P:(tt + 1) * P], q_rs[:, n:n + 1].to_broadcast([P, P]), ident,
                                             start=True, stop=True)
                        filled(last, u[b_])
                elif k == "qrot":
                    j = st["j"]
                    pe.wait_ge(qn_ready, l * 5 + j + 1)
                    b = claim(u[0])
                    for b_ in range(NB):
                        src = k_a[:, b_, CTX:TOK] if j == 0 else q_a[:, 2 * (j - 1) + b_, CTX:TOK]
                        last = pe.matmul(b[:, b_ * LAT:(b_ + 1) * LAT], rot, src, start=True, stop=True)
                    filled(last, u[0])
                elif k == "scores":
                    h = st["h"]
                    kv = h // (AH // AKV)
                    pe.wait_ge(qk_ready, l * 5 + h // 2 + 2)
                    for i in range(2):
                        b = claim(u[i])
                        filled(pe.matmul(b[:, :], q_a[:, h, CTX + i * P:CTX + (i + 1) * P], k_a[:, kv, :],
                                         start=True, stop=True), u[i])
                    if 2 in u:
                        b = claim(u[2])
                        for i in range(2):
                            last = pe.matmul(b[:, i * CTX:(i + 1) * CTX], q_a[:, h, i * P:(i + 1) * P], k_a[:, kv, 0:CTX],
                                             start=True, stop=True)
                        filled(last, u[2])
                elif k == "probs":
                    h = st["h"]
                    pe.wait_ge(p_ready, l * AH + h + 1)
                    for i in range(2):
                        b = claim(u[i])
                        for kt in range(2 * i, 2 * i + 2):
                            for qt in range(2):
                                last = pe.transpose(b[:, (kt % 2) * 256 + qt * P:(kt % 2) * 256 + (qt + 1) * P],
                                                    pr[:, qt * TOK + kt * P:qt * TOK + (kt + 1) * P], ident)
                        filled(last, u[i])
                    if 2 in u:
                        b = claim(u[2])
                        for kt in range(2):
                            for qt in range(2):
                                last = pe.transpose(b[:, kt * 256 + qt * P:kt * 256 + (qt + 1) * P],
                                                    pr[:, 2 * TOK + qt * CTX + kt * P:2 * TOK + qt * CTX + (kt + 1) * P],
                                                    ident)
                        filled(last, u[2])
                elif k == "attend":
                    h = st["h"]
                    kv = h // (AH // AKV)
                    pe.wait_ge(pT_ready, l * AH + h + 1)
                    if h == 0:
                        pe.wait_ge(av_ready, l + 1)
                    b = claim(u[0])
                    if l < DEPTH - 1:
                        for kt in range(2):
                            pe.matmul(b[:, 0:CTX], v_a[:, kt, kv * P:(kv + 1) * P],
                                      prT[:, 2 * TOK + kt * 256:2 * TOK + (kt + 1) * 256], start=kt == 0, stop=kt == 1)
                    for kt in range(4):
                        last = pe.matmul(b[:, CTX:TOK], v_a[:, kt, kv * P:(kv + 1) * P], prT[:, kt * 256:(kt + 1) * 256],
                                         start=kt == 0, stop=kt == 3)
                    filled(last, u[0])
                elif k == "final":
                    for i in range(4):
                        b = claim(u[i])
                        pe.wait_ge(hf_ready, n_fin + 4 * (i % 2) + 4)
                        tt, half = i // 2, i % 2
                        for kt in range(4 * half, 4 * half + 4):
                            last = pe.transpose(b[:, (kt % 4) * P:(kt % 4 + 1) * P],
                                                xT[:, kt, CTX + tt * P:CTX + (tt + 1) * P], ident)
                        filled(last, u[i])

        @block.scalar
        def _(act):
            def split(st):
                p, s = st["p"], st["s"]
                raw_arrived(act, p)
                if s >= 2:
                    act.wait_ge(panel_done, [q["p"] for q in PANELS if q.get("s") == s - 2][0] + 1)
                act.activation(wH[:, s % 2, :, :], raw[:, p % RAW, :, :], ACT.Copy).then_inc(wH_ready, 1)

            def y_high(no, src, kts, ts_):
                act.wait_ge(yf_ready, yf_of[no] + 1)
                act.activation(yH[:, kts, ts_], src, ACT.Copy).then_inc(yH_ready, 1)

            n_norm = n_hf = n_m = 0
            if "s" in PANELS[0]:
                split(PANELS[0])
            for st in PLAN:
                k, l, u = st["k"], st["l"], st["u"]
                if k == "start":
                    act.wait_ge(s_par, 3)
                    act.activation(c2e[:, :, :], c2[:, :, :], ACT.Exp, scale=-1.0).then_inc(s_cexp, 1)
                elif k == "panel":
                    nx = next_panel(st)
                    if nx:
                        split(nx)
                    kind, p, c_, b_ = st["kind"], st["p"], st["c"], st["b"]
                    slot = p % 2
                    ts_ = slice(0, TOK) if kind in ("mk", "ak") else cols(l)
                    src = pp[:, slot, :, ts_]
                    if kind in ("mk", "mq"):
                        act.wait_ge(panel_done, p + 1)
                        w = 1 if kind == "mk" else 0
                        act.activation(qk[:, 2 * c_:2 * c_ + 2, w, ts_], src, ACT.Copy,
                                       scale=1.0 if w else float(MQK) ** -0.5).then_inc(mqk_ready, 1)
                        act.wait_ge(mqk_ready, 4 * l + (c_ + 1 if w else 3 + c_))
                        act.sem_inc(slot_free[slot], 1)
                    elif kind == "mo":
                        act.wait_ge(panel_done, p + 1)
                        act.activation(sig_o[:, c_ % 2, :, ts_], src, ACT.Tanh, scale=0.5).then_inc(so_exp, 1)
                        act.wait_ge(so_exp, l * MH + c_ + 1)
                        act.sem_inc(slot_free[slot], 1)
                    elif kind in ("ak", "aq"):
                        j = 0 if kind == "ak" else c_ + 1
                        n = l * 5 + j + 1
                        dst = k_a[:, :, ts_] if kind == "ak" else q_a[:, 2 * c_:2 * c_ + 2, ts_]
                        act.wait_ge(panel_done, p + 1)
                        act.activation(dst, src, ACT.Copy).then_inc(aqk_in, 1)
                        act.wait_ge(aqk_in, n)
                        act.sem_inc(slot_free[slot], 1)
                        if j:
                            bk, un = next(q for q in PLAN if q["k"] == "qss" and q["l"] == l and q["j"] == j - 1)["u"][0]
                            act.wait_ge(full[bk], un + 1)
                        act.activation(q_sq[:, :, ts_], dst, ACT.Square).then_inc(qsq_ready, 1)
                    elif kind == "gate":
                        n = (l * 3 + b_) * NC + c_
                        act.wait_ge(panel_done, p + 1)
                        if n:
                            act.wait_ge(m_ready, n)
                        act.activation(gs[:, :, ts_], src, ACT.Tanh, scale=0.5).then_inc(gate_exp, 1)
                        act.wait_ge(gate_exp, n + 1)
                        act.sem_inc(slot_free[slot], 1)
                    elif kind == "cc":
                        act.wait_ge(panel_done, p + 1)
                        if c_:
                            act.wait_ge(cu_ready, l * NC + c_)
                        act.activation(c_sb[:, :, ts_], src, ACT.Copy).then_inc(cc_ready, 1)
                        act.wait_ge(cc_ready, l * NC + c_ + 1)
                        act.sem_inc(slot_free[slot], 1)
                    elif kind == "cu":
                        act.wait_ge(cu_ready, l * NC + c_ + 1)
                        if c_:
                            act.wait_ge(yf_ready, yf_of[y_no[l, "c", c_ - 1]] + 1)
                        sg = slice(0, 2) if l < DEPTH - 1 else slice(1, 2)
                        for b in range(NB):
                            wt = pars[l][:, ROW_CONV + 2 * c_ + b:ROW_CONV + 2 * c_ + b + 1]
                            act.activation(c_acc[:, b, sg, :], c_u[:, b, sg, 0:LAT], ACT.Copy, scale=wt).then_inc(c1_ready, 1)
                    elif kind == "cb":
                        y_high(y_no[l, "c", c_], y_tmp[:, :, ts_], slice(2 * c_, 2 * c_ + 2), ts_)
                    elif kind == "up":
                        act.wait_ge(panel_done, p + 1)
                        no = y_no[l, "up", b_, c_]
                        act.wait_ge(y_ready, no)
                        act.activation(y_tmp[:, :, ts_], src, ACT.Relu).then_inc(up_ready, 1)
                        act.wait_ge(up_ready, (l * 4 + b_) * NC + c_ + 1)
                        act.sem_inc(slot_free[slot], 1)
                        y_high(no, y_tmp[:, :, ts_], slice(2 * c_, 2 * c_ + 2), ts_)
                elif k == "ss":
                    need = x_needed(st)
                    if need == 0:
                        act.wait_ge(s_xt, KT)
                    else:
                        act.wait_ge(x_ready, need)
                    ts_ = slice(0, TOK) if l < DEPTH and not (l == DEPTH - 1 and st["n"] == 2) else cols(DEPTH)
                    for kt in range(KT):
                        if kt >= 2:
                            act.wait_ge(sq_used, n_norm * (KT - 1) + kt - 1)
                        elif n_norm:
                            act.wait_ge(sq_used, n_norm * (KT - 1))
                        act.activation(n_sq[:, kt % 2, ts_], xT[:, kt, ts_], ACT.Square).then_inc(sq_ready, 1)
                    n_norm += 1
                    b = bank(act, u["ss"])
                    t0 = norm_tiles(st)[0]
                    if n_norm == 1:
                        act.wait_ge(s_const, 3)
                    act.activation(n_sd[:, t0:TT], b[:, t0:TT], ACT.Sqrt, bias=eps).then_inc(sd_ready, 1)
                elif k == "qss":
                    j = st["j"]
                    b = bank(act, u[0])
                    t0 = 0 if j == 0 else cols(l).start // P
                    act.activation(q_sd.rearrange("p (b t) -> p b t", b=NB)[:, :, t0:TT],
                                   b[:, 0:NB * TT].rearrange("p (b t) -> p b t", b=NB)[:, :, t0:TT],
                                   ACT.Sqrt, bias=eps).then_inc(qsd_ready, 1)
                elif k == "apply":
                    ts_ = slice(0, TOK) if not (l == DEPTH - 1 and st["n"] == 2) else cols(l)
                    if st["n"] == 2:
                        act.wait_ge(panel_done, panel_no("wo", l, NC - 1) + 1)
                    elif l:
                        act.wait_ge(panel_done, panel_no("up", l - 1, NC - 1, 3) + 1)
                    for kt in range(KT):
                        act.wait_ge(hf_ready, n_hf + 1)
                        act.activation(hH[:, kt, ts_], n_h[:, kt % 4, ts_], ACT.Copy).then_inc(hH_ready, 1)
                        n_hf += 1
                    n_m += KT
                    if st["n"] == 1:
                        act.wait_ge(s_wg, 80 * (l + 1))
                        act.activation(wgH[:, :, :], w_gate[:, :, :], ACT.Copy).then_inc(wgH_ready, 1)
                elif k == "gate_sel":
                    act.wait_ge(fneg_ready, l + 1)
                    act.activation(rows["f_exp"][0:8, :], rows["f_neg"][0:8, :], ACT.Exp).then_inc(fln_ready, 1)
                    act.wait_ge(fln_ready, 2 * l + 1)
                    act.activation(rows["f_exp"][0:8, :], rows["f_exp"][0:8, :], ACT.Ln, bias=1.0).then_inc(fln_ready, 1)
                    act.wait_ge(erow_ready, l + 1)
                    act.activation(rows["e_run"][0:8, :], rows["e_run"][0:8, :], ACT.Exp).then_inc(eexp_ready, 1)
                elif k == "weigh":
                    h = st["h"]
                    act.wait_ge(gc_ready, l + 1)
                    if h:
                        bk, un = list(next(q for q in PLAN if q["k"] == "value" and q["l"] == l and q["h"] == h - 1)["u"].values())[-1]
                        act.wait_ge(full[bk], un + 1)
                    for d in range(2):
                        b = bank(act, u[f"m{d}"])
                        for s, row in enumerate(packed(l, d)):
                            for a, e, off in row:
                                last = act.activation(EP[:, d, off:off + e - a], b[:, a:e], ACT.Exp, scale=-1.0,
                                                      bias=g_col[:, d, s, d * MH + h:d * MH + h + 1])
                                if (s, a) != (TT - 1, row[-1][0]):
                                    last.then_inc(E_ready, 1)
                        last.then_inc(free[u[f"m{d}"][0]], 1)
                elif k == "value":
                    h = st["h"]
                    tts = range(TT) if l < DEPTH - 1 else range(CTX // P, TT)
                    for i, tt in enumerate(tts):
                        act.wait_ge(hraw_ready, (sum(len(spans_tt(q)) for q in range(l)) * MH) + h * len(tts) + i + 1)
                        if i:
                            act.wait_ge(hss_ready, h_count(l, h, tt - 1))
                        act.activation(junk[:, :], hM[:, h, tt, :], ACT.Square, accum_out=mss[:, tt:tt + 1]).then_inc(hss_ready, 1)
                    act.wait_ge(hss_ready, h_count(l, h, TT - 1))
                    act.activation(mrs[:, tts[0]:TT], mss[:, tts[0]:TT], ACT.Sqrt, scale=1.0 / MV, bias=eps).then_inc(mrs_ready, 1)
                elif k == "turn":
                    h = st["h"]
                    act.wait_ge(y_ready, y_no[l, "m", h])
                    for j in range(2):
                        b = bank(act, u[j])
                        r = ROW_MN + 2 * h + j
                        act.activation(y_tmp[:, j, cols(l)], b[:, cols(l)], ACT.Copy,
                                       scale=pars[l][:, r:r + 1]).then_inc(free[u[j][0]], 1)
                    for j in range(2):
                        act.wait_ge(free[u[j][0]], u[j][1] + 1)
                    act.sem_inc(ot_ready, 1)
                    y_high(y_no[l, "m", h], y_tmp[:, :, cols(l)], slice(2 * h, 2 * h + 2), cols(l))
                elif k == "scores":
                    h = st["h"]
                    act.wait_ge(nb_ready, l * AH + h + 1)
                    for qt in range(2):
                        b = bank(act, u[qt])
                        act.activation(pr[:, qt * TOK:(qt + 1) * TOK], b[:, :], ACT.Exp, bias=anb[:, qt:qt + 1],
                                       scale=float(AHD) ** -0.5, accum_out=asum[:, qt:qt + 1]).then_inc(p_exp, 1)
                    if 2 in u:
                        b = bank(act, u[2])
                        for qt in range(2):
                            act.activation(pr[:, 2 * TOK + qt * CTX:2 * TOK + (qt + 1) * CTX], b[:, qt * CTX:(qt + 1) * CTX],
                                           ACT.Exp, bias=anb[:, 2 + qt:3 + qt], scale=float(AHD) ** -0.5,
                                           accum_out=asum[:, 2 + qt:3 + qt]).then_inc(p_exp, 1)
                elif k == "attend":
                    h = st["h"]
                    b = bank(act, u[0])
                    act.activation(q_a[:, h, cols(l)], b[:, cols(l)], ACT.Copy).then_inc(free[u[0][0]], 1)
                elif k == "ysplit":
                    j = st["j"]
                    no = y_no[l, "a", j]
                    bk, un = next(q for q in PLAN if q["k"] == "attend" and q["l"] == l and q["h"] == 2 * j + 1)["u"][0]
                    act.wait_ge(free[bk], un + 1)
                    act.wait_ge(panel_done, panel_no("proj", l, NC - 1, 0) + 1)
                    act.activation(yH[:, 2 * j:2 * j + 2, cols(l)], q_a[:, 2 * j:2 * j + 2, cols(l)],
                                   ACT.Copy).then_inc(yH_ready, 1)
                elif k == "msplit":
                    j = st["j"]
                    act.wait_ge(m_ready, (l * 3 + 2) * NC + j + 1)
                    act.wait_ge(panel_done, panel_no("gate", l, NC - 1, 2) + 1)
                    act.activation(hH[:, 2 * j:2 * j + 2, cols(l)], merged[:, 2 * j:2 * j + 2, cols(l)],
                                   ACT.Copy).then_inc(hH_ready, 1)

        @block.gpsimd
        def _(pool):
            pool.memset(mean_d, 1.0 / D).then_inc(s_const, 1)
            pool.memset(mean_h, 1.0 / AHD).then_inc(s_const, 1)
            pool.memset(eps, EPS).then_inc(s_const, 1)

            def split(st):
                p, s = st["p"], st["s"]
                pool.wait_ge(wH_ready, s + 1)
                pool.tensor_tensor(wL[:, s % 2, 0:KP, :], raw[:, p % RAW, 0:KP, :], wH[:, s % 2, 0:KP, :].bitcast(F32),
                                   ALU.subtract).then_inc(wL_ready, 1)

            def y_rest(no, src, kts, ts_):
                pool.wait_ge(yH_ready, no + 1)
                pool.tensor_tensor(yL[:, kts, ts_], src, yH[:, kts, ts_].bitcast(F32), ALU.subtract).then_inc(y_ready, 1)

            n_hH = 0
            n_chain = 0
            for st in PLAN:
                k, l, u = st["k"], st["l"], st["u"]
                if k == "panel":
                    nx = next_panel(st)
                    if nx:
                        split(nx)
                    kind, c_, b_ = st["kind"], st["c"], st["b"]
                    ts_ = cols(l)
                    if kind == "proj":
                        n = (l * 3 + b_) * NC + c_
                        pool.wait_ge(mt_ready, n + 1)
                        if b_ == 0:
                            pool.sem_inc(m_ready, 1)
                        else:
                            m = merged[:, 2 * c_:2 * c_ + 2, ts_]
                            pool.tensor_tensor(m, m, gs[:, :, ts_], ALU.add).then_inc(m_ready, 1)
                    elif kind == "cc" and c_ == 0:
                        pool.wait_ge(y_ready, y_no[l, "a", 3] + 1)
                        pool.wait_ge(panel_done, panel_no("gate", l, 1, 1) + 1)
                        pool.memset(c_u[:, :, :, 0:1], 0.0).then_inc(cpad, 1)
                        pool.memset(c_u[:, :, :, LAT + 1:LAT + 2], 0.0).then_inc(cpad, 1)
                    elif kind == "cb":
                        y_rest(y_no[l, "c", c_], y_tmp[:, :, ts_], slice(2 * c_, 2 * c_ + 2), ts_)
                    elif kind == "up":
                        y_rest(y_no[l, "up", b_, c_], y_tmp[:, :, ts_], slice(2 * c_, 2 * c_ + 2), ts_)
                elif k == "apply":
                    ts_ = slice(0, TOK) if not (l == DEPTH - 1 and st["n"] == 2) else cols(l)
                    for kt in range(KT):
                        pool.wait_ge(hH_ready, h_no[l, st["n"]] + kt + 1)
                        pool.tensor_tensor(hL[:, kt, ts_], n_h[:, kt % 4, ts_], hH[:, kt, ts_].bitcast(F32),
                                           ALU.subtract).then_inc(h_ready, 1)
                    if st["n"] == 1:
                        pool.wait_ge(wgH_ready, l + 1)
                        pool.tensor_tensor(wgL[:, :, :], w_gate[:, :, :], wgH[:, :, :].bitcast(F32),
                                           ALU.subtract).then_inc(wg_ready, 1)
                        pool.wait_ge(h_ready, h_no[l, 1] + KT)
                        pool.memset(vaug[:, :, :, MV:MV + 1], 1.0).then_inc(vones, 1)
                        pool.memset(rows["ones"][0:8, :], 1.0).then_inc(orow, 1)
                elif k == "weigh":
                    h = st["h"]
                    pool.wait_ge(P_ready, l * MH + h + 1)
                    last = None
                    for d in range(2):
                        for s, row in enumerate(packed(l, d)):
                            for a, e, off in row:
                                if a <= s * P < e:
                                    v = EP[:, d, off + s * P - a:off + s * P - a + P]
                                    sign = 1 if d == 0 else -1
                                    last = pool.affine_select(out=v, in_=v, compare_op=ALU.is_ge, fill=0.0, base=0,
                                                              pattern=[[sign, P]], channel_multiplier=-sign)
                    last.then_inc(mask_ready, 1)
                elif k == "turn":
                    h = st["h"]
                    y_rest(y_no[l, "m", h], y_tmp[:, :, cols(l)], slice(2 * h, 2 * h + 2), cols(l))
                elif k == "ysplit":
                    j = st["j"]
                    y_rest(y_no[l, "a", j], q_a[:, 2 * j:2 * j + 2, cols(l)], slice(2 * j, 2 * j + 2), cols(l))
                elif k == "msplit":
                    j = st["j"]
                    pool.wait_ge(hH_ready, h_no[l, "m", j] + 1)
                    pool.tensor_tensor(hL[:, 2 * j:2 * j + 2, cols(l)], merged[:, 2 * j:2 * j + 2, cols(l)],
                                       hH[:, 2 * j:2 * j + 2, cols(l)].bitcast(F32), ALU.subtract).then_inc(h_ready, 1)


        @block.vector
        def _(dve):
            count = [0]

            def link(ins):
                count[0] += 1
                ins.then_inc(dchain, 1)
                dve.wait_ge(dchain, count[0])

            def start_link(ins):
                count[0] += 1
                ins.then_inc(dchain, 1)

            def freed(ins, u):
                ins.then_inc(free[u[0]], 1)

            def split(st):
                p, s = st["p"], st["s"]
                dve.wait_ge(wH_ready, s + 1)
                dve.tensor_tensor(wL[:, s % 2, KP:KT, :], raw[:, p % RAW, KP:KT, :], wH[:, s % 2, KP:KT, :].bitcast(F32),
                                  ALU.subtract).then_inc(wLv_ready, 1)

            n_norm = 0
            for st in PLAN:
                k, l, u = st["k"], st["l"], st["u"]
                if k == "start":
                    for i in range(3):
                        n = ROWS if i < 2 else 24
                        b = bank(dve, u[f"par{i}"])
                        freed(dve.tensor_copy(pars[i][:, 0:n], b[:, 0:n]), u[f"par{i}"])
                    for i in range(3):
                        dve.wait_ge(free[u[f"par{i}"][0]], 1)
                    for i in range(DEPTH):
                        v = pars[i][:, ROW_MN:ROW_MN + 8]
                        start_link(dve.tensor_scalar(v, v, 0.5, None, ALU.mult))
                    dve.wait_ge(dchain, count[0])
                    dve.tensor_copy(c2[:, :, 0], pars[2][:, 0:8]).then_inc(s_par, 1)
                    dve.tensor_copy(c2[:, :, 1], pars[2][:, 8:16]).then_inc(s_par, 1)
                    dve.wait_ge(s_par, 2)
                    dve.sem_inc(s_par, 1)
                    dve.wait_ge(s_cexp, 1)
                    link(dve.tensor_scalar(c2e[:, :, :], c2e[:, :, :], 1.0, None, ALU.add))
                    link(dve.reciprocal(c2e[:, :, :], c2e[:, :, :]))
                    dve.tensor_tensor(c2[:, :, :], c2[:, :, :], c2e[:, :, :], ALU.mult).then_inc(s_silu, 1)
                    for kt in range(KT):
                        b = bank(dve, u[f"x{kt}"])
                        freed(dve.tensor_copy(xT[:, kt, :], b[:, :]), u[f"x{kt}"])
                    for kt in range(KT - 4, KT):
                        dve.wait_ge(free[u[f"x{kt}"][0]], u[f"x{kt}"][1] + 1)
                    dve.sem_inc(s_xt, KT)
                elif k == "panel":
                    nx = next_panel(st)
                    if nx:
                        split(nx)
                    kind, p, c_, b_ = st["kind"], st["p"], st["c"], st["b"]
                    slot = p % 2
                    ts_ = cols(l)
                    src = pp[:, slot, :, ts_]
                    if kind == "ada":
                        dve.wait_ge(panel_done, p + 1)
                        half = dict(scalar2=0.5, op1=ALU.mult) if 8 <= c_ < 12 else dict(scalar2=None)
                        start_link(dve.tensor_scalar(out=modT[:, l, 2 * c_, :], in0=pp[:, slot, 0, 0:2],
                                                     scalar1=pars[l][:, ROW_ADA + 2 * c_:ROW_ADA + 2 * c_ + 1],
                                                     op0=ALU.add, **half))
                        dve.tensor_scalar(out=modT[:, l, 2 * c_ + 1, :], in0=pp[:, slot, 1, 0:2],
                                          scalar1=pars[l][:, ROW_ADA + 2 * c_ + 1:ROW_ADA + 2 * c_ + 2],
                                          op0=ALU.add, **half).then_inc(slot_free[slot], 1)
                        dve.wait_ge(dchain, count[0])
                        dve.wait_ge(slot_free[slot], p // 2 + 1)
                    elif kind in ("mv", "av"):
                        dve.wait_ge(panel_done, p + 1)
                        dst = vaug[:, :, c_, 0:MV] if kind == "mv" else v_a[:, :, :]
                        done = mv_ready if kind == "mv" else av_ready
                        dve.tensor_copy(dst, pp[:, slot, :, :].rearrange("p b (t n) -> p (b t) n", t=2)).then_inc(done, 1)
                        dve.wait_ge(done, MH * l + c_ + 1 if kind == "mv" else l + 1)
                        dve.sem_inc(slot_free[slot], 1)
                    elif kind == "proj":
                        dve.wait_ge(panel_done, p + 1)
                        dst = merged[:, 2 * c_:2 * c_ + 2, ts_] if b_ == 0 else gs[:, :, ts_]
                        dve.wait_ge(gate_exp, (l * 3 + b_) * NC + c_ + 1)
                        dve.scalar_tensor_tensor(out=dst, in0=gs[:, :, ts_], scalar=1.0, in1=src,
                                                 op0=ALU.add, op1=ALU.mult).then_inc(mt_ready, 1)
                        dve.wait_ge(mt_ready, (l * 3 + b_) * NC + c_ + 1)
                        dve.sem_inc(slot_free[slot], 1)
                    elif kind == "cu":
                        dve.wait_ge(panel_done, p + 1)
                        dve.wait_ge(cc_ready, l * NC + c_ + 1)
                        if c_ == 0:
                            dve.wait_ge(cpad, 2 * l + 2)
                        sg = slice(0, 2) if l < DEPTH - 1 else slice(1, 2)
                        n = sg.stop - sg.start
                        for b in range(NB):
                            i = dve.tensor_tensor(c_u[:, b, sg, 1:LAT + 1],
                                                  pp[:, slot, b, ts_].rearrange("p (s t) -> p s t", s=n),
                                                  c_sb[:, b, ts_].rearrange("p (s t) -> p s t", s=n), ALU.mult)
                            if b < NB - 1:
                                start_link(i)
                        i.then_inc(cu_ready, 1)
                        dve.wait_ge(dchain, count[0])
                        dve.wait_ge(cu_ready, l * NC + c_ + 1)
                        dve.sem_inc(slot_free[slot], 1)
                        dve.wait_ge(c1_ready, (l * NC + c_ + 1) * NB)
                        for tap in (1, 2):
                            for b in range(NB):
                                r = ROW_CONV + tap * 8 + 2 * c_ + b
                                start_link(dve.scalar_tensor_tensor(
                                    out=c_acc[:, b, sg, :], in0=c_u[:, b, sg, tap:tap + LAT], scalar=pars[l][:, r:r + 1],
                                    in1=c_acc[:, b, sg, :], op0=ALU.mult, op1=ALU.add))
                            dve.wait_ge(dchain, count[0])
                    elif kind == "cb":
                        dve.wait_ge(panel_done, p + 1)
                        no = y_no[l, "c", c_]
                        dve.wait_ge(y_ready, no)
                        sg = slice(0, 2) if l < DEPTH - 1 else slice(1, 2)
                        for b in range(NB):
                            i = dve.tensor_tensor(y_tmp[:, b, ts_], pp[:, slot, b, ts_],
                                                  c_acc[:, b, sg, :].rearrange("p s t -> p (s t)"), ALU.mult)
                            if b < NB - 1:
                                start_link(i)
                        dve.wait_ge(dchain, count[0])
                        i.then_inc(yf_ready, 1)
                        dve.wait_ge(yf_ready, yf_of[no] + 1)
                        dve.sem_inc(slot_free[slot], 1)
                    elif kind == "up":
                        dve.wait_ge(up_ready, (l * 4 + b_) * NC + c_ + 1)
                        dve.tensor_tensor(y_tmp[:, :, ts_], y_tmp[:, :, ts_], y_tmp[:, :, ts_], ALU.mult).then_inc(yf_ready, 1)
                    elif kind in ("wo", "down"):
                        dve.wait_ge(panel_done, p + 1)
                        g = 16 if kind == "wo" else 40
                        n = x_no[l, kind, b_, c_]
                        for b in range(NB):
                            kt = 2 * c_ + b
                            for hs, v in halves(l):
                                i = dve.scalar_tensor_tensor(out=xT[:, kt, hs], in0=pp[:, slot, b, hs],
                                                             scalar=modT[:, l, g + kt, v:v + 1], in1=xT[:, kt, hs],
                                                             op0=ALU.mult, op1=ALU.add)
                                if (b, v) != (NB - 1, halves(l)[-1][1]):
                                    start_link(i)
                        i.then_inc(x_ready, 1)
                        dve.wait_ge(dchain, count[0])
                        dve.wait_ge(x_ready, n + 1)
                        dve.sem_inc(slot_free[slot], 1)
                elif k == "ss":
                    t0 = norm_tiles(st)[0]
                    n_norm += 1
                    dve.wait_ge(sd_ready, n_norm)
                    dve.sem_inc(free[u["ss"][0]], 1)
                    dve.reciprocal(n_rs[:, t0:TT], n_sd[:, t0:TT]).then_inc(rs_ready, 1)
                elif k == "spread":
                    n_r, u_r = bank(dve, u["r"]), u["r"]
                elif k == "apply":
                    n = st["n"]
                    full_ = not (l == DEPTH - 1 and n == 2)
                    ts_ = slice(0, TOK) if full_ else cols(l)
                    hv = [(slice(CTX, TOK), 0)] + ([(slice(0, CTX), 1)] if full_ else [])
                    sh, sc, r = (0, 8, ROW_N1) if n == 1 else (24, 32, ROW_N2)
                    for v in range(2):
                        start_link(dve.scalar_tensor_tensor(out=gain[:, :, v], in0=modT[:, l, sc:sc + 8, v], scalar=1.0,
                                                            in1=pars[l][:, r:r + 8], op0=ALU.add, op1=ALU.mult))
                    dve.wait_ge(dchain, count[0])
                    for kt in range(KT):
                        link(dve.tensor_tensor(n_t[:, kt % 2, ts_], xT[:, kt, ts_], n_r[:, ts_], ALU.mult))
                        if kt >= 4:
                            dve.wait_ge(h_ready, h_no[l, n] + kt - 3)
                        for hs, v in hv:
                            i = dve.tensor_scalar(n_h[:, kt % 4, hs], n_t[:, kt % 2, hs], gain[:, kt, v:v + 1],
                                                  modT[:, l, sh + kt, v:v + 1], ALU.mult, ALU.add)
                            if (hs, v) != hv[-1]:
                                start_link(i)
                        i.then_inc(hf_ready, 1)
                    dve.sem_inc(free[u_r[0]], 1)
                elif k == "gate_tok":
                    b = bank(dve, u["g"])
                    dve.tensor_copy(g_tok[:, :, :], b[:, 0:TT * 16].rearrange("p (t n) -> p t n", t=TT)).then_inc(g_ready, 1)
                    dve.wait_ge(g_ready, l + 1)
                    dve.sem_inc(free[u["g"][0]], 1)
                elif k == "gate_rows":
                    b = bank(dve, u["g"])
                    dve.tensor_copy(rows["g_rows"][:, :], b[0:16, :]).then_inc(gr_ready, 1)
                    dve.wait_ge(gr_ready, 3 * l + 1)
                    dve.sem_inc(free[u["g"][0]], 1)
                    dve.tensor_copy(rows["g_back"][:, 0:CTX], rows["g_rows"][:, CTX - 1::-1]).then_inc(gr_ready, 1)
                    dve.tensor_copy(rows["g_back"][:, CTX:TOK], rows["g_rows"][:, TOK - 1:CTX - 1:-1]).then_inc(gr_ready, 1)
                elif k == "gate_sel":
                    R = {n: t[0:8, :] for n, t in rows.items()}
                    dve.wait_ge(s_wg, 80 * (l + 1))
                    b = bank(dve, u["f"])
                    freed(dve.tensor_scalar(R["f_pre"], b[0:8, :], gb[0:8, 1:2], None, ALU.add), u["f"])
                    dve.wait_ge(free[u["f"][0]], u["f"][1] + 1)
                    dve.scalar_tensor_tensor(out=R["f_neg"], in0=R["f_pre"], scalar=-1.0, in1=R["f_pre"],
                                             op0=ALU.mult, op1=ALU.min).then_inc(fneg_ready, 1)
                    dve.wait_ge(fln_ready, 2 * l + 2)
                    link(dve.scalar_tensor_tensor(out=R["log_f"], in0=R["f_pre"], scalar=0.0, in1=R["f_exp"],
                                                  op0=ALU.min, op1=ALU.subtract))
                    dve.wait_ge(orow, l + 1)
                    link(dve.tensor_tensor_scan(R["F_run"], R["ones"], R["log_f"], 0.0, ALU.mult, ALU.add))
                    b = bank(dve, u["i"])
                    dve.scalar_tensor_tensor(out=R["a_run"], in0=b[0:8, :], scalar=gb[0:8, 0:1], in1=R["F_run"],
                                             op0=ALU.add, op1=ALU.subtract).then_inc(cols_in, 1)
                    dve.wait_ge(cols_in, 4 * l + 1)
                    dve.sem_inc(free[u["i"][0]], 1)
                    link(dve.tensor_tensor_scan(R["M_run"], R["a_run"], R["a_run"], 0.0, ALU.max, ALU.max))
                    dve.scalar_tensor_tensor(out=R["e_run"], in0=R["F_run"], scalar=-1.0, in1=R["M_run"],
                                             op0=ALU.mult, op1=ALU.subtract).then_inc(erow_ready, 1)
                    for nm, fr in (("M_back", "M_run"), ("a_back", "a_run")):
                        start_link(dve.tensor_copy(R[nm][:, 0:CTX], R[fr][:, CTX - 1::-1]))
                        i = dve.tensor_copy(R[nm][:, CTX:TOK], R[fr][:, TOK - 1:CTX - 1:-1])
                        if nm == "M_back":
                            start_link(i)
                        else:
                            i.then_inc(cols_in, 1)
                    dve.wait_ge(dchain, count[0])
                    dve.wait_ge(eexp_ready, l + 1)
                    dve.tensor_copy(R["e_back"][:, 0:CTX], R["e_run"][:, CTX - 1::-1]).then_inc(cols_in, 1)
                    dve.tensor_copy(R["e_back"][:, CTX:TOK], R["e_run"][:, TOK - 1:CTX - 1:-1]).then_inc(cols_in, 1)
                elif k == "gate_cols":
                    b = bank(dve, u["g"])
                    dve.tensor_copy(g_col[:, :, :, :], b[:, 0:4 * TT * 8].rearrange("p (i t n) -> p i t n", i=4, t=TT)
                                    ).then_inc(gc_ready, 1)
                    dve.wait_ge(gc_ready, l + 1)
                    dve.sem_inc(free[u["g"][0]], 1)
                elif k == "weigh":
                    h = st["h"]
                    for d in range(2):
                        dve.wait_ge(free[u[f"m{d}"][0]], u[f"m{d}"][1] + 1)
                    dve.wait_ge(E_ready, e_count(l, h))
                    for s in range(TT):
                        us = u[f"s{min(s, 2)}"]
                        b = bank(dve, us)
                        for d in range(2):
                            for a, e, off in packed(l, d)[s]:
                                src = b[:, a:e] if s < 2 else b[:, (s - 2) * LAT + a - CTX:(s - 2) * LAT + e - CTX]
                                v = EP[:, d, off:off + e - a]
                                i = dve.tensor_tensor(v, v, src, ALU.mult)
                                if not (s != 2 and (d, a) == (1, packed(l, 1)[s][-1][0])):
                                    start_link(i)
                        if s != 2:
                            freed(i, us)
                    for s in (0, 1, 3):
                        us = u[f"s{min(s, 2)}"]
                        dve.wait_ge(free[us[0]], us[1] + 1)
                    dve.wait_ge(dchain, count[0])
                    dve.sem_inc(P_ready, 1)
                elif k == "value":
                    h = st["h"]
                    tts = spans_tt(l)
                    for tt in tts:
                        bs = [bank(dve, u[tt, d]) for d in range(2)]
                        for d in range(2):
                            start_link(dve.tensor_scalar(mstat[:, tt, d:d + 1], bs[d][:, MV:MV + 1], -1.0,
                                                         g_col[:, 2 + d, tt, d * MH + h:d * MH + h + 1], ALU.mult, ALU.max))
                        dve.wait_ge(dchain, count[0])
                        for d in range(2):
                            start_link(dve.tensor_scalar(mstat[:, tt, 2 + d:3 + d], bs[d][:, MV:MV + 1],
                                                         mstat[:, tt, d:d + 1], None, ALU.max))
                        dve.wait_ge(dchain, count[0])
                        link(dve.reciprocal(mstat[:, tt, 4:6], mstat[:, tt, 2:4]))
                        dve.tensor_scalar(hM[:, h, tt, :], bs[0][:, 0:MV], mstat[:, tt, 4:5], None,
                                          ALU.mult).then_inc(free[u[tt, 0][0]], 1)
                        dve.wait_ge(free[u[tt, 0][0]], u[tt, 0][1] + 1)
                        dve.scalar_tensor_tensor(out=hM[:, h, tt, :], in0=bs[1][:, 0:MV], scalar=mstat[:, tt, 5:6],
                                                 in1=hM[:, h, tt, :], op0=ALU.mult, op1=ALU.add).then_inc(hraw_ready, 1)
                        dve.wait_ge(hraw_ready, h_count(l, h, tt))
                        dve.sem_inc(free[u[tt, 1][0]], 1)
                    dve.wait_ge(mrs_ready, l * MH + h + 1)
                    rs = mrs[:, tts[0]:TT]
                    link(dve.reciprocal(rs, rs))
                    for tt in tts:
                        i = dve.tensor_scalar(hM[:, h, tt, :], hM[:, h, tt, :], mrs[:, tt:tt + 1], None, ALU.mult)
                        if tt < TT - 1:
                            start_link(i)
                    i.then_inc(hn_ready, 1)
                elif k == "turn":
                    h = st["h"]
                    ts_ = cols(l)
                    dve.wait_ge(ot_ready, l * MH + h + 1)
                    v = y_tmp[:, :, ts_]
                    dve.scalar_tensor_tensor(out=v, in0=sig_o[:, h % 2, :, ts_], scalar=1.0, in1=v,
                                             op0=ALU.add, op1=ALU.mult).then_inc(yf_ready, 1)
                elif k == "qss":
                    j = st["j"]
                    t0 = 0 if j == 0 else cols(l).start // P
                    dve.wait_ge(qsd_ready, l * 5 + j + 1)
                    dve.sem_inc(free[u[0][0]], 1)
                    dve.reciprocal(q_rs.rearrange("p (b t) -> p b t", b=NB)[:, :, t0:TT],
                                   q_sd.rearrange("p (b t) -> p b t", b=NB)[:, :, t0:TT]).then_inc(qrs_ready, 1)
                elif k == "qbc":
                    j = st["j"]
                    ts_ = slice(0, TOK) if j == 0 else cols(l)
                    g = ROW_KN if j == 0 else ROW_QN
                    for b_ in range(NB):
                        b = bank(dve, u[b_])
                        dst = k_a[:, b_, ts_] if j == 0 else q_a[:, 2 * j - 2 + b_, ts_]
                        freed(dve.scalar_tensor_tensor(out=dst, in0=dst, scalar=pars[l][:, g:g + 1], in1=b[:, ts_],
                                                       op0=ALU.mult, op1=ALU.mult), u[b_])
                    for b_ in range(NB):
                        dve.wait_ge(free[u[b_][0]], u[b_][1] + 1)
                    dve.sem_inc(qn_ready, 1)
                elif k == "qrot":
                    j = st["j"]
                    b = bank(dve, u[0])
                    dst = [k_a[:, b_, CTX:TOK] if j == 0 else q_a[:, 2 * j - 2 + b_, CTX:TOK] for b_ in range(NB)]
                    for b_ in range(NB):
                        i = dve.tensor_tensor(q_t[:, b_, :], b[:, b_ * LAT:(b_ + 1) * LAT], ropeS, ALU.mult)
                        if b_ < NB - 1:
                            start_link(i)
                        else:
                            freed(i, u[0])
                        start_link(dve.tensor_tensor(dst[b_], dst[b_], ropeC, ALU.mult))
                    dve.wait_ge(dchain, count[0])
                    dve.wait_ge(free[u[0][0]], u[0][1] + 1)
                    start_link(dve.tensor_tensor(dst[0], dst[0], q_t[:, 0, :], ALU.add))
                    dve.tensor_tensor(dst[1], dst[1], q_t[:, 1, :], ALU.add).then_inc(qk_ready, 1)
                elif k == "scores":
                    h = st["h"]
                    nq = 4 if 2 in u else 2
                    for qt in range(2):
                        b = bank(dve, u[qt])
                        start_link(dve.reduce_max(amax[:, qt:qt + 1], b[:, :], AX))
                    if 2 in u:
                        b = bank(dve, u[2])
                        start_link(dve.reduce_max(amax[:, 2:4], b[:, :].rearrange("p (q k) -> p q k", q=2), AX))
                    dve.wait_ge(dchain, count[0])
                    dve.tensor_scalar(anb[:, 0:nq], amax[:, 0:nq], -float(AHD) ** -0.5, None, ALU.mult).then_inc(nb_ready, 1)
                    dve.wait_ge(p_exp, p_count(l, h))
                    for i in range(3 if 2 in u else 2):
                        dve.sem_inc(free[u[i][0]], 1)
                    link(dve.reciprocal(ars[:, 0:nq], asum[:, 0:nq]))
                    for qt in range(nq):
                        a = qt * TOK if qt < 2 else 2 * TOK + (qt - 2) * CTX
                        v = pr[:, a:a + (TOK if qt < 2 else CTX)]
                        i = dve.tensor_scalar(v, v, ars[:, qt:qt + 1], None, ALU.mult)
                        if qt < nq - 1:
                            start_link(i)
                    dve.wait_ge(dchain, count[0])
                    i.then_inc(p_ready, 1)
                elif k == "probs":
                    h = st["h"]
                    nb = 3 if 2 in u else 2
                    for i in range(nb):
                        b = bank(dve, u[i])
                        freed(dve.tensor_copy(prT[:, i * TOK:(i + 1) * TOK], b[:, :]), u[i])
                    for i in range(nb):
                        dve.wait_ge(free[u[i][0]], u[i][1] + 1)
                    dve.sem_inc(pT_ready, 1)
                elif k == "final":
                    ts_ = cols(DEPTH)
                    for kt in range(KT):
                        dve.scalar_tensor_tensor(out=xT[:, kt, ts_], in0=xT[:, kt, ts_],
                                                 scalar=pars[2][:, 16 + kt:17 + kt], in1=n_r[:, ts_],
                                                 op0=ALU.mult, op1=ALU.mult).then_inc(hf_ready, 1)
                    dve.wait_ge(hf_ready, n_fin + KT)
                    dve.sem_inc(free[u_r[0]], 1)
                    for i in range(4):
                        b = bank(dve, u[i])
                        j = dve.tensor_copy(f_out[:, i // 2, (i % 2) * 512:(i % 2 + 1) * 512], b[:, :])
                        if i % 2 == 0:
                            start_link(j)
                            dve.wait_ge(dchain, count[0])
                        else:
                            j.then_inc(f_ready, 1)


def e_count(l, h):
    per = [sum(len(r) for d in range(2) for r in packed(q, d)) - 2 for q in range(DEPTH)]
    return sum(per[q] * MH for q in range(l)) + per[l] * (h + 1)


def h_count(l, h, tt):
    n = [TT if q < DEPTH - 1 else TT - CTX // P for q in range(DEPTH)]
    first = TT - n[l]
    return sum(n[q] * MH for q in range(l)) + n[l] * h + tt - first + 1


def p_count(l, h):
    n = [4 if q < DEPTH - 1 else 2 for q in range(DEPTH)]
    return sum(n[q] * AH for q in range(l)) + n[l] * (h + 1)


_INS = ["x", "c", "ctx", "c_ctx", "w_ada", "b_ada", "norm1", "norm2", "w_in", "mlstm_gate_b", "mlstm_norm", "q_norm",
        "k_norm", "conv_w", "w_proj_m", "w_proj_a", "w_proj_c", "w_out", "w_up", "w_down", "final_norm"]


def kernel(**inputs):
    import numpy as _np
    import concourse.bacc as _bacc
    from concourse import mybir as _mybir
    from concourse.bass_utils import run_bass_kernel_spmd as _run

    nc = _bacc.Bacc("TRN2", target_bir_lowering=False, num_devices=1)
    arrays, args = {}, []
    for name in _INS:
        a = _np.ascontiguousarray(inputs[name])
        arrays[f"in_{name}"] = a
        args.append(nc.dram_tensor(f"in_{name}", a.shape, _mybir.dt.from_np(a.dtype), kind="ExternalInput").ap())
    arrays["constants"] = make_constants()
    args.append(nc.dram_tensor("constants", (P, CONST_COLS), F32, kind="ExternalInput").ap())
    args.append(nc.dram_tensor("out", (1, LAT, D), F32, kind="ExternalOutput").ap())
    trunk(nc, *args)
    return _run(nc, [arrays], core_ids=[0]).results[0]["out"]
```

```python
from contextlib import ExitStack

import numpy as np

import concourse.bass as bass
from concourse import mybir

F32 = mybir.dt.float32
F32R = mybir.dt.float32r
ALU = mybir.AluOpType
ACT = mybir.ActivationFunctionType
AX = mybir.AxisListType.X

P = 128
D = 1024
KT = D // P
DEPTH = 2
CTX = 256
LAT = 256
TOK = CTX + LAT
TT = TOK // P
GRID_W = 64
MH, MQK, MV = 4, 128, 256
AH, AKV, AHD = 8, 2, 128
CONV_K = 3
FF = 4 * D
PC = 256
NB = PC // P
NC = D // PC
EPS = 1e-6
ROPE_THETA = 10000.0
RAW = 3
KH = KT // 2
KP = 2

SIZES = dict(mq=512, mk=512, mv=1024, mo=1024, mg=16, aq=1024, ak=256, av=256, cu=D, cb=D, cc=D, g0=D, g1=D, g2=D)
COL, _at = {}, 0
for _n, _s in SIZES.items():
    COL[_n] = _at
    _at += _s

ROW_ADA, ROW_N1, ROW_N2, ROW_MN, ROW_CONV, ROW_QN, ROW_KN = 0, 48, 56, 64, 72, 96, 97
ROWS = 98
BACK = [1, 0, 3, 2]


def make_constants():
    ident = np.eye(P, dtype=np.float32)
    rot = np.zeros((P, P), np.float32)
    for m in range(P):
        if m % 64 < 32:
            rot[m + 32, m] = -1.0
        else:
            rot[m - 32, m] = 1.0
    nf = AHD // 4
    inv = (np.float32(ROPE_THETA) ** (-np.arange(nf, dtype=np.float32) / np.float32(nf))).astype(np.float32)
    t = np.arange(LAT)
    pos = np.stack([t // GRID_W, t % GRID_W]).astype(np.float32)
    d = np.arange(P)
    ang = (pos[d // 64][:, :] * inv[d % 32][:, None]).astype(np.float32)
    sel = np.zeros((P, 4, 8), np.float32)
    for g in range(2):
        for dr in range(2):
            for h in range(MH):
                sel[dr * 8 + g * 4 + h, g * 2 + dr, dr * 4 + h] = 1.0
    add = np.zeros((P, 2), np.float32)
    add[[0, 2], 0] = add[[1, 3], 1] = 1.0
    return np.concatenate([ident, rot, np.cos(ang), np.sin(ang), sel.reshape(P, 32), add], axis=1).astype(np.float32)


CONST_COLS = P + P + LAT + LAT + 32 + 2


def spans(l, d, s):
    if d == 0:
        out = [(P * s, TOK)]
    elif s < CTX // P:
        out = [(0, P * (s + 1)), (CTX, TOK)]
    else:
        out = [(CTX, P * (s + 1))]
    if l == DEPTH - 1:
        out = [(max(a, CTX), b) for a, b in out if b > CTX]
    if len(out) == 2 and out[0][1] == out[1][0]:
        out = [(out[0][0], out[1][1])]
    return out


def packed(l, d):
    at, res = 0, []
    for s in range(TT):
        row = []
        for a, b in spans(l, d, s):
            row.append((a, b, at))
            at += b - a
        res.append(row)
    return res


EPW = 1280


def make_plan():
    plan = []

    owed = []
    modulation = [(l, c) for l in range(DEPTH) for c in range(6 * NC)]

    def settle():
        while owed:
            l, m = owed.pop(0)
            step("adaturn", l, m=m)

    def panel(kind, l, c, b=0):
        plan.append(dict(k="panel", kind=kind, l=l, c=c, b=b))
        if kind != "ada":
            settle()

    def step(k, l, **kw):
        plan.append(dict(k=k, l=l, **kw))

    def ada(n):
        for _ in range(n):
            l, c = modulation.pop(0)
            if c % NC == 0:
                settle()
            panel("ada", l, c)
            if c % NC == NC - 1:
                owed.append((l, c // NC))

    def apply(l, n, fill):
        for j in range(NC):
            if j < fill:
                ada(1)
            step("apply", l, n=n, j=j)

    for l in range(DEPTH):
        more = l < DEPTH - 1
        if l == 0:
            for j in range(NC):
                step("squares", l, n=1, j=j)
            ada(2 * NC)
            settle()
        apply(l, 1, 4 if l else 0)
        step("gate_tok", l)
        panel("mk", l, 0)
        step("gate_sel", l)
        panel("mk", l, 1)
        step("gate_exp", l)
        panel("mq", l, 0)
        step("gate_scan", l)
        panel("mq", l, 1)
        step("gate_e", l)
        panel("mv", l, 0)
        step("gate_e2", l)
        panel("mv", l, 1)
        step("gate_cols", l)
        panel("mv", l, 2)
        panel("mv", l, 3)
        for h in range(MH):
            step("weigh", l, h=h)
            panel("mo", l, h)
            if l == 0 or h % 2:
                ada(1)
            if h:
                step("turn", l, h=h - 1)
            step("value", l, h=h)
        panel("av", l, 0)
        step("turn", l, h=MH - 1)
        stream = [("ak", 0), ("aq", 0), ("aq", 1), ("aq", 2), ("aq", 3), ("gate", 0), ("proj", 0)]
        for j, (kind, c) in enumerate(stream):
            panel(kind, l, c)
            if j >= 3:
                step("qrot", l, j=j - 3)
            if 2 <= j <= 6:
                step("qbc", l, j=j - 2)
            if 1 <= j <= 5:
                step("qss", l, j=j - 1)
        beside = {i: p for i, p in zip((0, 1, 2, 3, 5, 6), [(k, c, 0) for c in range(1, NC) for k in ("gate", "proj")])}
        beside[8] = ("gate", 0, 1)
        for i in range(AH + 2):
            if i in beside:
                kind, c, b = beside[i]
                panel(kind, l, c, b)
            elif l == 0 or i != 9:
                ada(1)
            if i == 0:
                step("qrot", l, j=4)
            if i >= 2:
                step("attend", l, h=i - 2)
            if 1 <= i <= AH:
                step("probs", l, h=i - 1)
            if i < AH:
                step("scores", l, h=i)
        for j in range(4):
            step("ysplit", l, j=j)
        for c in range(NC):
            if c:
                panel("gate", l, c, 1)
            panel("proj", l, c, 1)
        for c in range(NC):
            panel("cc", l, c)
            panel("cu", l, c)
            panel("cb", l, c)
            if l == 0 or c % 2:
                ada(1)
        for c in range(NC):
            panel("gate", l, c, 2)
            if c == NC - 1:
                for j in range(NC - 1):
                    step("msplit", l, j=j)
            panel("proj", l, c, 2)
            if c == 0 or (l and c == 2):
                ada(1)
        step("msplit", l, j=NC - 1)
        for c in range(NC):
            panel("wo", l, c)
            if c:
                step("squares", l, n=2, j=c - 1)
        step("squares", l, n=2, j=NC - 1)
        apply(l, 2, 4)
        for g in range(FF // D):
            for c in range(NC):
                panel("up", l, c, g)
            for c in range(NC):
                panel("down", l, c, g)
                if more and c in (0, 2):
                    ada(1)
                if g == FF // D - 1 and c:
                    step("squares", l + 1, n=1, j=c - 1)
        step("squares", l + 1, n=1, j=NC - 1)
    step("final", DEPTH)
    assert not modulation and not owed

    p = s = 0
    uses = [0, 0, 0, 0]
    for st in plan:
        if st["k"] == "panel":
            st["p"] = p
            p += 1
            st["s"] = s
            s += 1
        st["u"] = {}

    def use(st, name, bank):
        st["u"][name] = (bank, uses[bank])
        uses[bank] += 1

    start = dict(k="start", l=0, u={})
    use(start, "par2", 3)
    for kt in range(KT):
        use(start, f"x{kt}", kt % 4)
    for i in range(DEPTH):
        use(start, f"par{i}", i)
    for st in plan:
        k = st["k"]
        if k == "squares" and st["j"] == 0:
            use(st, "ss", 3)
            norm_use = st["u"]
        elif k == "squares":
            st["u"] = norm_use
        elif k == "adaturn":
            use(st, 0, 2)
        elif k == "gate_tok":
            use(st, "g", 1)
        elif k == "gate_sel":
            use(st, "i", 2)
            use(st, "f", 3)
        elif k == "gate_cols":
            use(st, "g", 0)
        elif k == "weigh":
            use(st, "m0", 3)
            use(st, "m1", 2)
            use(st, "s0", 0)
            use(st, "s1", 1)
            use(st, "s2", 3)
        elif k == "value":
            for tt in range(TT) if st["l"] < DEPTH - 1 else range(CTX // P, TT):
                for d in range(2):
                    use(st, (tt, d), (2 * tt + d) % 4)
        elif k == "turn":
            use(st, 0, 0)
            use(st, 1, 1)
        elif k == "gate_scan":
            st["u"] = next(q for q in plan if q["k"] == "gate_sel" and q["l"] == st["l"])["u"]
        elif k == "qss":
            use(st, 0, 3)
        elif k == "qbc":
            use(st, 0, 0)
            use(st, 1, 1)
        elif k == "qrot":
            use(st, 0, 2)
        elif k in ("scores", "probs"):
            for b in range(3 if st["l"] < DEPTH - 1 else 2):
                use(st, b, b)
        elif k == "attend":
            use(st, 0, 3)
        elif k == "final":
            for i in range(4):
                use(st, i, i)
    return [start] + plan, p, s


PLAN, NPANELS, NSPLIT = make_plan()
PANELS = [st for st in PLAN if st["k"] == "panel"]


def panel_no(kind, l, c, b=0):
    return next(st["p"] for st in PANELS if (st["kind"], st["l"], st["c"], st["b"]) == (kind, l, c, b))


def trunk(nc, x, c, ctx_in, c_ctx, w_ada, b_ada, norm1, norm2, w_in, gate_b, mnorm, qnorm, knorm, conv_w,
          w_pm, w_pa, w_pc, w_out, w_up, w_down, fnorm, consts, out):
    ctx = ExitStack()
    with ctx:
        place = {}
        base = (nc.sbuf_base + 63) // 64 * 64

        def at(name, shape, dt, offset):
            return nc.alloc_sbuf_tensor_at(name, shape, dt, offset=base + offset)

        K16 = KT * TOK * 4
        o = 0
        xT = at("xT", [P, KT, TOK], F32, o); o += K16
        hH = at("hH", [P, KT, TOK], F32R, o); o += K16
        hL = at("hL", [P, KT, TOK], F32R, o); o += K16
        raw = at("raw", [P, RAW, KT, PC], F32, o); o += RAW * KT * PC * 4
        wH = at("wH", [P, 2, KT, PC], F32R, o); o += 2 * KT * PC * 4
        wL = at("wL", [P, 2, KT, PC], F32R, o); o += 2 * KT * PC * 4
        Y = o
        yH = at("yH", [P, KT, TOK], F32R, o); o += K16
        yL = at("yL", [P, KT, TOK], F32R, o); o += K16
        names = ["g_rows", "g_back", "f_pre", "f_neg", "f_exp", "log_f", "F_run", "a_run", "e_run"]
        rows = {n: at(n, [16, TOK], F32, Y + i * TOK * 4) for i, n in enumerate(names)}
        rows["a_back"] = at("a_back", [16, TOK], F32, Y + 9 * TOK * 4)
        rows["e_back"] = at("e_back", [16, TOK], F32, Y + 10 * TOK * 4)
        rows["ones"] = at("ones_row", [16, TOK], F32, Y + 11 * TOK * 4)
        rows["M_run"] = at("M_run", [16, TOK], F32, Y + 14 * TOK * 4)
        rows["M_back"] = at("M_back", [16, TOK], F32, Y + 15 * TOK * 4)
        G = o
        merged = at("merged", [P, KT, TOK], F32, o); o += K16
        x_in = at("x_in", [P, TT, D], F32, G)
        qk = at("qk", [P, MH, 2, TOK], F32, G)
        hM = at("hM", [P, MH, TT, MV], F32, G)
        T = o
        vaug = at("vaug", [P, TT, MH, MV + 1], F32, T)
        EP = at("EP", [P, 2, EPW], F32, T + 16448)
        sig_o = at("sig_o", [P, 2, NB, TOK], F32, T + 26688)
        y_tmp = at("y_tmp", [P, NB, TOK], F32, T + 34944)
        junk = at("junk", [P, MV], F32, T + 39040)
        g_col = at("g_col", [P, 4, TT, 8], F32, T + 40320)
        mstat = at("mstat", [P, TT, 6], F32, T + 40832)
        mss = at("mss", [P, TT], F32, T + 40960)
        mrs = at("mrs", [P, TT], F32, T + 41024)
        w_gate = at("w_gate", [P, KT, 16], F32, T + 41088)
        wgH = at("wgH", [P, KT, P], F32R, T + 26688)
        wgL = at("wgL", [P, KT, P], F32R, T + 30784)
        gb = at("gb", [8, 2], F32, T + 41600)
        v_a = at("v_a", [P, TT, PC], F32, T)
        k_a = at("k_a", [P, NB, TOK], F32, T + 4096)
        q_a = at("q_a", [P, AH, TOK], F32, T + 8192)
        pr = at("pr", [P, 6 * 256], F32, T + 24576)
        prT = at("prT", [P, 6 * 256], F32, T + 30720)
        q_sq = at("q_sq", [P, NB, TOK], F32, T + 30720)
        q_t = at("q_t", [P, NB, LAT], F32, T + 36864)
        c_sb = at("c_sb", [P, NB, TOK], F32, T)
        c_u = at("c_u", [P, NB, 2, LAT + 2], F32, T + 4096)
        c_acc = at("c_acc", [P, NB, 2, LAT], F32, T + 8256)
        n_sq = at("n_sq", [P, 2, 2, TOK], F32, T)
        n_r = at("n_r", [P, TOK], F32, T + 8192)
        n_t = at("n_t", [P, 2, TOK], F32, T + 10240)
        n_h = at("n_h", [P, 4, TOK], F32, T + 14336)
        f_out = at("f_out", [P, 2, D], F32, T + 22528)
        par_rows = [at(f"par_rows{i}", [P, P], F32, T + 30720 + 512 * i) for i in range(3)]
        o = T + 41664
        gs = at("gs", [P, NB, TOK], F32, o); o += NB * TOK * 4
        con = at("con", [P, CONST_COLS], F32, o); o += (CONST_COLS * 4 + 31) // 32 * 32
        small = at("small", [P, 32], F32, o); o += 128
        mean_d, mean_h, eps = small[:, 0:1], small[:, 1:2], small[:, 2:3]
        q_sd, q_rs = small[:, 16:24], small[:, 24:32]
        pars = [at(f"pars{i}", [P, P if i < 2 else 24], F32, o + 512 * i) for i in range(3)]; o += 1120
        ada_rows = at("ada_rows", [4, D], F32, o); o += 4 * D
        c_win = at("c_win", [P, KT * 4 + P], F32R, o); o += 640
        cHL = c_win[:, 0:KT * 4].rearrange("p (k n) -> p k n", n=4)
        modT = at("modT", [P, 2, 48, 2], F32, o); o += 768
        c2 = at("c2", [P, KT, 2], F32, o); o += 64
        c2e = at("c2e", [P, KT, 2], F32, o); o += 64
        gain = at("gain", [P, KT, 2], F32, o); o += 64
        amax = at("amax", [P, 4], F32, o); o += 32
        anb = at("anb", [P, 4], F32, o); o += 32
        asum = at("asum", [P, 4], F32, o); o += 32
        ars = at("ars", [P, 4], F32, o); o += 32

        pairs = con[:, CONST_COLS - 2:CONST_COLS]
        ident, rot = con[:, 0:P], con[:, P:2 * P]
        ropeC, ropeS = con[:, 2 * P:2 * P + LAT], con[:, 2 * P + LAT:2 * P + 2 * LAT]
        sel = con[:, 2 * P + 2 * LAT:CONST_COLS - 2].rearrange("p (g m) -> p g m", g=4)

        pp = ctx.enter_context(nc.psum_tensor("pp", [P, 2, NB, TOK], F32))
        pc = ctx.enter_context(nc.psum_tensor("pc", [P, 4, TOK], F32))

        def sem(name):
            return ctx.enter_context(nc.semaphore(name))

        s_small = sem("small_loaded")
        s_par_rows = sem("param_rows_loaded")
        s_x = sem("x_loaded")
        s_wg = sem("gate_weights_loaded")
        s_raw = [sem(f"raw_loaded{i}") for i in range(RAW)]
        s_out = sem("out_stored")
        wH_ready = sem("weights_high_ready")
        wL_ready = sem("weights_rest_ready")
        panel_done = sem("panel_done")
        slot_free = [sem(f"slot_free{i}") for i in range(2)]
        full = [sem(f"bank_full{i}") for i in range(4)]
        free = [sem(f"bank_free{i}") for i in range(4)]
        s_const = sem("constants_ready")
        s_silu = sem("silu_ready")
        s_cexp = sem("c_exp_ready")
        s_xt = sem("x_turned")
        s_par = sem("params_ready")
        x_ready = sem("x_pair_ready")
        sd_ready = sem("deviation_ready")
        rs_ready = sem("reciprocal_ready")
        ada_copied = sem("ada_rows_copied")
        mod_ready = sem("modulation_ready")
        s_cz = sem("c_window_zeroed")
        cH_ready = sem("c_high_ready")
        wgz_ready = sem("gate_w_zeroed")
        qsd_ready = sem("q_deviation_ready")
        qrs_ready = sem("q_reciprocal_ready")
        mrs_ready = sem("h_deviation_ready")
        ot_ready = sem("h_turned_scaled")
        wLv_ready = sem("weights_rest_vector_ready")
        sq_ready = sem("squares_ready")
        sq_used = sem("squares_used")
        hf_ready = sem("h_float_ready")
        hH_ready = sem("h_high_ready")
        h_ready = sem("h_ready")
        y_ready = sem("y_ready")
        yf_ready = sem("y_float_ready")
        yH_ready = sem("y_high_ready")
        wgH_ready = sem("gate_w_high_ready")
        wg_ready = sem("gate_w_ready")
        g_ready = sem("gates_tok_ready")
        gr_ready = sem("gates_rows_ready")
        fneg_ready = sem("f_neg_ready")
        fln_ready = sem("f_ln_ready")
        erow_ready = sem("e_row_ready")
        eexp_ready = sem("e_exp_ready")
        cols_in = sem("gate_cols_inputs")
        gc_ready = sem("gate_cols_ready")
        mqk_ready = sem("mqk_ready")
        mv_ready = sem("mv_ready")
        E_ready = sem("E_ready")
        P_ready = sem("P_ready")
        mask_ready = sem("mask_ready")
        hraw_ready = sem("h_out_ready")
        hss_ready = sem("h_ss_ready")
        hn_ready = sem("h_norm_ready")
        so_exp = sem("sig_o_exp_ready")
        aqk_in = sem("aqk_copied")
        qsq_ready = sem("q_squares_ready")
        qn_ready = sem("q_normed")
        qk_ready = sem("qk_roped")
        av_ready = sem("av_ready")
        nb_ready = sem("neg_max_ready")
        p_exp = sem("p_exp_ready")
        p_ready = sem("p_scaled")
        pT_ready = sem("pT_ready")
        ya_ready = sem("ya_ready")
        gate_exp = sem("gate_exp_ready")
        mt_ready = sem("merge_term_ready")
        m_ready = sem("merged_ready")
        cc_ready = sem("cc_copied")
        cu_ready = sem("cu_ready")
        cpad = sem("conv_pad_zeroed")
        c1_ready = sem("conv_first_tap")
        up_ready = sem("up_relu_ready")
        f_ready = sem("final_rows_ready")
        vones = sem("value_ones")
        orow = sem("ones_row_ready")

        def cols(l):
            return slice(0, TOK) if l < DEPTH - 1 else slice(CTX, TOK)

        def halves(l):
            return [(slice(CTX, TOK), 0)] + ([(slice(0, CTX), 1)] if l < DEPTH - 1 else [])

        def panel_source(st):
            kind, l, c, b = st["kind"], st["l"], st["c"], st["b"]
            if kind == "ada":
                w, at_ = w_ada[l], 0
            elif kind in COL:
                w, at_ = w_in[l], COL[kind]
            elif kind == "gate":
                w, at_ = w_in[l], COL[f"g{b}"]
            elif kind == "proj":
                w, at_ = (w_pm, w_pa, w_pc)[b][l], 0
            elif kind == "wo":
                w, at_ = w_out[l], 0
            elif kind == "up":
                w, at_ = w_up[l], b * D
            else:
                w, at_ = w_down[l][b * D:(b + 1) * D, :], 0
            return w.rearrange("(k p) n -> p k n", p=P)[:, :, at_ + c * PC:at_ + (c + 1) * PC]

        y_no, h_no = {}, {}
        n_y = n_h_ = n_x = 0
        x_no = {}
        for st in PLAN:
            k, l = st["k"], st["l"]
            if k == "turn":
                y_no[l, "m", st["h"]] = n_y; n_y += 1
            elif k == "ysplit":
                y_no[l, "a", st["j"]] = n_y; n_y += 1
            elif k == "panel" and st["kind"] == "cb":
                y_no[l, "c", st["c"]] = n_y; n_y += 1
            elif k == "panel" and st["kind"] == "up":
                y_no[l, "up", st["b"], st["c"]] = n_y; n_y += 1
            elif k == "apply":
                h_no.setdefault((l, st["n"]), n_h_)
                n_h_ += 2
            elif k == "msplit":
                h_no[l, "m", st["j"]] = n_h_; n_h_ += 1
            elif k == "panel" and st["kind"] in ("wo", "down"):
                x_no[l, st["kind"], st["b"], st["c"]] = n_x; n_x += 1

        taken = [no for key, no in sorted(y_no.items(), key=lambda kv: kv[1]) if key[1] != "a"]
        yf_of = {no: i for i, no in enumerate(taken)}

        def x_needed(st):
            l, n, j = st["l"], st["n"], st["j"]
            if n == 2:
                return x_no[l, "wo", 0, j] + 1
            return x_no[l - 1, "down", FF // D - 1, j] + 1

        def operand(st):
            kind, l, c, b = st["kind"], st["l"], st["c"], st["b"]
            if kind == "proj":
                br = "mac"[b]
                return yH, yL, y_ready, lambda kt: y_no[l, br, kt // 2] + 1
            if kind == "wo":
                return hH, hL, h_ready, lambda kt: h_no[l, "m", kt // 2] + 1
            if kind == "down":
                return yH, yL, y_ready, lambda kt: y_no[l, "up", b, kt // 2] + 1
            n = 2 if kind == "up" else 1
            return hH, hL, h_ready, lambda kt: h_no[l, n] + kt + 1

        def next_panel(st):
            p = st["p"] + 1
            return PANELS[p] if p < NPANELS else None

        def raw_arrived(eng, p):
            eng.wait_ge(s_raw[p % RAW], 16 * (p // RAW + 1))

        def bank(eng, u, what=None):
            b, n = u
            eng.wait_ge(full[b], n + 1)
            return pc[:, b, :]

        n_fin = KT * 2 * DEPTH
        dchain = sem("vector_chain")

        def spans_tt(l):
            return list(range(TT)) if l < DEPTH - 1 else list(range(CTX // P, TT))

        def norm_cols(st):
            only_latent = st["l"] == DEPTH or (st["l"] == DEPTH - 1 and st["n"] == 2)
            return slice(CTX, TOK) if only_latent else slice(0, TOK)

        block = ctx.enter_context(nc.Block())

        @block.sync
        def _(sp):
            for st in PLAN:
                if st["k"] == "gate_tok":
                    l = st["l"]
                    if l:
                        sp.wait_ge(panel_done, panel_no("down", l - 1, NC - 1, FF // D - 1) + 1)
                    else:
                        sp.wait_ge(s_par, 3)
                    sp.dma_start(w_gate[:, :, :], w_in[l].rearrange("(k p) n -> p k n", p=P)[
                        :, :, COL["mg"]:COL["mg"] + 16]).then_inc(s_wg, 16)
                    for g in range(2):
                        for dr in range(2):
                            sp.dma_start(gb[dr * 4:dr * 4 + 4, g:g + 1],
                                         gate_b[l, dr, g].rearrange("(h a) -> h a", a=1)).then_inc(s_wg, 16)
                if st["k"] != "panel":
                    continue
                p = st["p"]
                if p >= RAW:
                    sp.wait_ge(wL_ready, 2 * (p - RAW + 1))
                    sp.wait_ge(wLv_ready, 2 * (p - RAW + 1))
                sp.dma_start(raw[:, p % RAW, :, :], panel_source(st)).then_inc(s_raw[p % RAW], 16)
            ov = out[0].rearrange("(t p) d -> p t d", p=P)
            for tt in range(2):
                sp.wait_ge(f_ready, tt + 1)
                sp.dma_start(ov[:, tt, :], f_out[:, tt, :]).then_inc(s_out, 16)
            sp.wait_ge(s_out, 32)

        @block.tensor
        def _(pe):
            def claim(u):
                b, n = u
                if n:
                    pe.wait_ge(free[b], n)
                return pc[:, b, :]

            def filled(ins, u):
                ins.then_inc(full[u[0]], 1)

            def run_panel(st):
                p, kind, l = st["p"], st["kind"], st["l"]
                slot = p % 2
                if p >= 2:
                    pe.wait_ge(slot_free[slot], p // 2)
                ws = st["s"] % 2

                def split_ready(kt):
                    if kt % KH == 0:
                        pe.wait_ge(wL_ready, 2 * p + kt // KH + 1)
                        pe.wait_ge(wLv_ready, 2 * p + kt // KH + 1)

                if kind == "ada":
                    if p == 0:
                        pe.wait_ge(s_silu, 2)
                    for kt in range(KT):
                        split_ready(kt)
                        four = c_win[:, 4 * kt:4 * kt + P]
                        for part in (wH, wL):
                            last = pe.matmul(pp[:, slot, 0, 0:PC], four, part[:, ws, kt, :],
                                             start=kt == 0 and part is wH, stop=kt == KT - 1 and part is wL)
                    last.then_inc(panel_done, 1)
                    return
                hi, lo, ready, need = operand(st)
                if kind in ("mv", "av"):
                    pe.wait_ge(ready, need(KT - 1))
                    split_ready(0)
                    split_ready(KH)
                    for tt in range(TT):
                        dst = pp[:, slot, tt // 2, (tt % 2) * PC:(tt % 2 + 1) * PC]
                        ts_ = slice(tt * P, (tt + 1) * P)
                        for kt in range(KT):
                            pe.matmul(dst, hi[:, kt, ts_], wH[:, ws, kt, :], start=kt == 0, stop=False)
                            pe.matmul(dst, hi[:, kt, ts_], wL[:, ws, kt, :], start=False, stop=False)
                            last = pe.matmul(dst, lo[:, kt, ts_], wH[:, ws, kt, :], start=False, stop=kt == KT - 1)
                    last.then_inc(panel_done, 1)
                    return
                ts_ = slice(0, TOK) if kind in ("mk", "ak") else cols(l)
                seen = 0
                for kt in range(KT):
                    split_ready(kt)
                    if need(kt) > seen:
                        seen = need(kt)
                        pe.wait_ge(ready, seen)
                    for b in range(NB):
                        dst = pp[:, slot, b, ts_]
                        w = slice(b * P, (b + 1) * P)
                        pe.matmul(dst, wH[:, ws, kt, w], hi[:, kt, ts_], start=kt == 0, stop=False)
                        pe.matmul(dst, wH[:, ws, kt, w], lo[:, kt, ts_], start=False, stop=False)
                        last = pe.matmul(dst, wL[:, ws, kt, w], hi[:, kt, ts_], start=False, stop=kt == KT - 1)
                last.then_inc(panel_done, 1)

            n_norm = 0
            for st in PLAN:
                k, l, u = st["k"], st["l"], st["u"]
                if k == "panel":
                    run_panel(st)
                elif k == "start":
                    pe.wait_ge(s_small, 64)
                    filled(pe.transpose(claim(u["par2"])[:, 0:24], par_rows[2][0:24, :], ident[0:24, 0:24]), u["par2"])
                    pe.wait_ge(s_x, 32)
                    for kt in range(KT):
                        b = claim(u[f"x{kt}"])
                        for tt in range(TT):
                            last = pe.transpose(b[:, tt * P:(tt + 1) * P], x_in[:, tt, kt * P:(kt + 1) * P], ident)
                        filled(last, u[f"x{kt}"])
                    pe.wait_ge(s_par_rows, 16 * 7 * DEPTH)
                    for i in range(2):
                        b = claim(u[f"par{i}"])
                        filled(pe.transpose(b[:, 0:ROWS], par_rows[i][0:ROWS, :], ident[0:ROWS, 0:ROWS]), u[f"par{i}"])
                elif k == "squares":
                    j = st["j"]
                    b = claim(u["ss"]) if j == 0 else pc[:, u["ss"][0], :]
                    if n_norm == 0 and j == 0:
                        pe.wait_ge(s_const, 3)
                    pe.wait_ge(sq_ready, n_norm * NC + j + 1)
                    ts_ = norm_cols(st)
                    for i in range(2):
                        last = pe.matmul(b[:, ts_], mean_d.to_broadcast([P, P]), n_sq[:, j % 2, i, ts_],
                                         start=j == 0 and i == 0, stop=j == NC - 1 and i == 1)
                    if j < NC - 1:
                        last.then_inc(sq_used, 1)
                    else:
                        filled(last, u["ss"])
                        n_norm += 1
                elif k == "adaturn":
                    b = claim(u[0])
                    pe.wait_ge(ada_copied, 6 * NC * l + NC * (st["m"] + 1))
                    for i in range(KT):
                        last = pe.matmul(b[:, 2 * i:2 * i + 2], ada_rows[:, i * P:(i + 1) * P], pairs[0:4, :],
                                         start=True, stop=True)
                    filled(last, u[0])
                elif k == "gate_tok":
                    b = claim(u["g"])
                    pe.wait_ge(wg_ready, l + 1)
                    for kt in range(KT):
                        pe.wait_ge(h_ready, h_no[l, 1] + kt + 1)
                        pe.matmul(b[:, :], wgH[:, kt, :], hH[:, kt, :], start=kt == 0, stop=False)
                        pe.matmul(b[:, :], wgH[:, kt, :], hL[:, kt, :], start=False, stop=False)
                        last = pe.matmul(b[:, :], wgL[:, kt, :], hH[:, kt, :], start=False, stop=kt == KT - 1)
                    filled(last, u["g"])
                elif k == "gate_sel":
                    pe.wait_ge(gr_ready, 3 * l + 3)
                    for name, g in (("i", 0), ("f", 1)):
                        b = claim(u[name])
                        pe.matmul(b[0:8, :], sel[0:16, 2 * g, :], rows["g_rows"][:, :], start=True, stop=False)
                        last = pe.matmul(b[0:8, :], sel[0:16, 2 * g + 1, :], rows["g_back"][:, :], start=False, stop=True)
                        filled(last, u[name])
                elif k == "gate_cols":
                    b = claim(u["g"])
                    pe.wait_ge(cols_in, 4 * l + 4)
                    for i, name in enumerate(("a_run", "a_back", "e_run", "e_back")):
                        for tt in range(TT):
                            c0 = (i * TT + tt) * 8
                            last = pe.matmul(b[:, c0:c0 + 8], rows[name][0:8, tt * P:(tt + 1) * P], ident[0:8, 0:8],
                                             start=True, stop=True)
                    filled(last, u["g"])
                elif k == "weigh":
                    h = st["h"]
                    for d in range(2):
                        b = claim(u[f"m{d}"])
                        src = rows["M_run" if d == 0 else "M_back"]
                        r = d * MH + h
                        last = pe.matmul(b[:, :], ident[0:8, r:r + 1].to_broadcast([8, P]), src[0:8, :], start=True, stop=True)
                        filled(last, u[f"m{d}"])
                    pe.wait_ge(mqk_ready, 4 * l + 4)
                    for s in range(2):
                        b = claim(u[f"s{s}"])
                        filled(pe.matmul(b[:, cols(l)], qk[:, h, 1, s * P:(s + 1) * P], qk[:, h, 0, cols(l)],
                                         start=True, stop=True), u[f"s{s}"])
                    b = claim(u["s2"])
                    for s in range(2, 4):
                        last = pe.matmul(b[:, (s - 2) * LAT:(s - 1) * LAT], qk[:, h, 1, s * P:(s + 1) * P],
                                         qk[:, h, 0, CTX:TOK], start=True, stop=True)
                    filled(last, u["s2"])
                elif k == "value":
                    h = st["h"]
                    n = l * MH + h + 1
                    pe.wait_ge(P_ready, n)
                    pe.wait_ge(mask_ready, n)
                    pe.wait_ge(mv_ready, MH * l + h + 1)
                    pe.wait_ge(vones, l + 1)
                    for tt in sorted({key[0] for key in u}):
                        for d in range(2):
                            b = claim(u[tt, d])
                            terms = [(s, off + tt * P - a) for s, row in enumerate(packed(l, d)) for a, e, off in row
                                     if a <= tt * P < e]
                            for i, (s, off) in enumerate(terms):
                                last = pe.matmul(b[:, 0:MV + 1], EP[:, d, off:off + P], vaug[:, s, h, :],
                                                 start=i == 0, stop=i == len(terms) - 1)
                            filled(last, u[tt, d])
                elif k == "turn":
                    h = st["h"]
                    tts = range(TT) if l < DEPTH - 1 else range(CTX // P, TT)
                    pe.wait_ge(hn_ready, l * MH + h + 1)
                    for j in range(2):
                        b = claim(u[j])
                        for tt in tts:
                            last = pe.transpose(b[:, tt * P:(tt + 1) * P], hM[:, h, tt, j * P:(j + 1) * P], ident)
                        filled(last, u[j])
                elif k == "qss":
                    j = st["j"]
                    ts_ = slice(0, TOK) if j == 0 else cols(l)
                    pe.wait_ge(qsq_ready, l * 5 + j + 1)
                    b = claim(u[0])
                    for b_ in range(NB):
                        for tt in range(ts_.start // P, TT):
                            last = pe.matmul(b[:, b_ * TT + tt:b_ * TT + tt + 1], q_sq[:, b_, tt * P:(tt + 1) * P], mean_h,
                                             start=True, stop=True)
                    filled(last, u[0])
                elif k == "qbc":
                    j = st["j"]
                    pe.wait_ge(qrs_ready, l * 5 + j + 1)
                    for b_ in range(NB):
                        b = claim(u[b_])
                        for tt in range(0 if j == 0 else cols(l).start // P, TT):
                            n = b_ * TT + tt
                            last = pe.matmul(b[:, tt * P:(tt + 1) * P], q_rs[:, n:n + 1].to_broadcast([P, P]), ident,
                                             start=True, stop=True)
                        filled(last, u[b_])
                elif k == "qrot":
                    j = st["j"]
                    pe.wait_ge(qn_ready, l * 5 + j + 1)
                    b = claim(u[0])
                    for b_ in range(NB):
                        src = k_a[:, b_, CTX:TOK] if j == 0 else q_a[:, 2 * (j - 1) + b_, CTX:TOK]
                        last = pe.matmul(b[:, b_ * LAT:(b_ + 1) * LAT], rot, src, start=True, stop=True)
                    filled(last, u[0])
                elif k == "scores":
                    h = st["h"]
                    kv = h // (AH // AKV)
                    pe.wait_ge(qk_ready, l * 5 + h // 2 + 2)
                    for i in range(2):
                        b = claim(u[i])
                        filled(pe.matmul(b[:, :], q_a[:, h, CTX + i * P:CTX + (i + 1) * P], k_a[:, kv, :],
                                         start=True, stop=True), u[i])
                    if 2 in u:
                        b = claim(u[2])
                        for i in range(2):
                            last = pe.matmul(b[:, i * CTX:(i + 1) * CTX], q_a[:, h, i * P:(i + 1) * P], k_a[:, kv, 0:CTX],
                                             start=True, stop=True)
                        filled(last, u[2])
                elif k == "probs":
                    h = st["h"]
                    pe.wait_ge(p_ready, l * AH + h + 1)
                    for i in range(2):
                        b = claim(u[i])
                        for kt in range(2 * i, 2 * i + 2):
                            for qt in range(2):
                                last = pe.transpose(b[:, (kt % 2) * 256 + qt * P:(kt % 2) * 256 + (qt + 1) * P],
                                                    pr[:, qt * TOK + kt * P:qt * TOK + (kt + 1) * P], ident)
                        filled(last, u[i])
                    if 2 in u:
                        b = claim(u[2])
                        for kt in range(2):
                            for qt in range(2):
                                last = pe.transpose(b[:, kt * 256 + qt * P:kt * 256 + (qt + 1) * P],
                                                    pr[:, 2 * TOK + qt * CTX + kt * P:2 * TOK + qt * CTX + (kt + 1) * P],
                                                    ident)
                        filled(last, u[2])
                elif k == "attend":
                    h = st["h"]
                    kv = h // (AH // AKV)
                    pe.wait_ge(pT_ready, l * AH + h + 1)
                    if h == 0:
                        pe.wait_ge(av_ready, l + 1)
                    b = claim(u[0])
                    if l < DEPTH - 1:
                        for kt in range(2):
                            pe.matmul(b[:, 0:CTX], v_a[:, kt, kv * P:(kv + 1) * P],
                                      prT[:, 2 * TOK + kt * 256:2 * TOK + (kt + 1) * 256], start=kt == 0, stop=kt == 1)
                    for kt in range(4):
                        last = pe.matmul(b[:, CTX:TOK], v_a[:, kt, kv * P:(kv + 1) * P], prT[:, kt * 256:(kt + 1) * 256],
                                         start=kt == 0, stop=kt == 3)
                    filled(last, u[0])
                elif k == "final":
                    for i in range(4):
                        b = claim(u[i])
                        pe.wait_ge(hf_ready, n_fin + 4 * (i % 2) + 4)
                        tt, half = i // 2, i % 2
                        for kt in range(4 * half, 4 * half + 4):
                            last = pe.transpose(b[:, (kt % 4) * P:(kt % 4 + 1) * P],
                                                xT[:, kt, CTX + tt * P:CTX + (tt + 1) * P], ident)
                        filled(last, u[i])

        @block.scalar
        def _(act):
            def split(st):
                p, s = st["p"], st["s"]
                raw_arrived(act, p)
                if s >= 2:
                    act.wait_ge(panel_done, p - 1)
                for a in (0, KH):
                    act.activation(wH[:, s % 2, a:a + KH, :], raw[:, p % RAW, a:a + KH, :], ACT.Copy).then_inc(wH_ready, 1)

            def y_high(no, src, kts, ts_):
                act.wait_ge(yf_ready, yf_of[no] + 1)
                act.activation(yH[:, kts, ts_], src, ACT.Copy).then_inc(yH_ready, 1)

            n_norm = n_hf = 0
            act.dma_start(con[:, :], consts).then_inc(s_small, 16)
            act.dma_start(par_rows[2][0:8, :], c.rearrange("a (r q) -> (a r) q", q=P)).then_inc(s_small, 16)
            act.dma_start(par_rows[2][8:16, :], c_ctx.rearrange("(r q) -> r q", q=P)).then_inc(s_small, 16)
            act.dma_start(par_rows[2][16:24, :], fnorm.rearrange("(r q) -> r q", q=P)).then_inc(s_small, 16)
            act.dma_start(x_in[:, 0:2, :], ctx_in[0].rearrange("(t p) d -> p t d", p=P)).then_inc(s_x, 16)
            act.dma_start(x_in[:, 2:4, :], x[0].rearrange("(t p) d -> p t d", p=P)).then_inc(s_x, 16)
            for l in range(DEPTH):
                pr_ = par_rows[l]
                for row, src, n in ((ROW_ADA, b_ada[l], 48), (ROW_N1, norm1[l], 8), (ROW_N2, norm2[l], 8),
                                    (ROW_MN, mnorm[l], 8), (ROW_QN, qnorm[l], 1), (ROW_KN, knorm[l], 1)):
                    act.dma_start(pr_[row:row + n, :], src.rearrange("(r q) -> r q", q=P)).then_inc(s_par_rows, 16)
                act.dma_start(pr_[ROW_CONV:ROW_CONV + 24, :],
                              conv_w[l].rearrange("k (r q) -> (k r) q", q=P)).then_inc(s_par_rows, 16)
            for st in PLAN:
                k, l, u = st["k"], st["l"], st["u"]
                if k == "start":
                    act.wait_ge(s_par, 2)
                    act.activation(c2e[:, :, :], c2[:, :, :], ACT.Exp, scale=-1.0).then_inc(s_cexp, 1)
                    act.wait_ge(s_silu, 1)
                    act.wait_ge(s_cz, 1)
                    act.activation(cHL[:, :, 0:2], c2[:, :, :], ACT.Copy).then_inc(cH_ready, 1)
                    split(PANELS[0])
                elif k == "panel":
                    nx = next_panel(st)
                    if nx:
                        split(nx)
                    kind, p, c_, b_ = st["kind"], st["p"], st["c"], st["b"]
                    slot = p % 2
                    ts_ = slice(0, TOK) if kind in ("mk", "ak") else cols(l)
                    src = pp[:, slot, :, ts_]
                    if kind in ("mk", "mq"):
                        act.wait_ge(panel_done, p + 1)
                        w = 1 if kind == "mk" else 0
                        act.activation(qk[:, 2 * c_:2 * c_ + 2, w, ts_], src, ACT.Copy,
                                       scale=1.0 if w else float(MQK) ** -0.5).then_inc(mqk_ready, 1)
                        act.wait_ge(mqk_ready, 4 * l + (c_ + 1 if w else 3 + c_))
                        act.sem_inc(slot_free[slot], 1)
                    elif kind == "mo":
                        act.wait_ge(panel_done, p + 1)
                        act.activation(sig_o[:, c_ % 2, :, ts_], src, ACT.Tanh, scale=0.5).then_inc(so_exp, 1)
                        act.wait_ge(so_exp, l * MH + c_ + 1)
                        act.sem_inc(slot_free[slot], 1)
                    elif kind in ("ak", "aq"):
                        j = 0 if kind == "ak" else c_ + 1
                        n = l * 5 + j + 1
                        dst = k_a[:, :, ts_] if kind == "ak" else q_a[:, 2 * c_:2 * c_ + 2, ts_]
                        act.wait_ge(panel_done, p + 1)
                        act.activation(dst, src, ACT.Copy).then_inc(aqk_in, 1)
                        act.wait_ge(aqk_in, n)
                        act.sem_inc(slot_free[slot], 1)
                        if j:
                            bk, un = next(q for q in PLAN if q["k"] == "qss" and q["l"] == l and q["j"] == j - 1)["u"][0]
                            act.wait_ge(full[bk], un + 1)
                        act.activation(q_sq[:, :, ts_], dst, ACT.Square).then_inc(qsq_ready, 1)
                    elif kind == "gate":
                        n = (l * 3 + b_) * NC + c_
                        act.wait_ge(panel_done, p + 1)
                        if n:
                            act.wait_ge(m_ready, n)
                        act.activation(gs[:, :, ts_], src, ACT.Tanh, scale=0.5).then_inc(gate_exp, 1)
                        act.wait_ge(gate_exp, n + 1)
                        act.sem_inc(slot_free[slot], 1)
                    elif kind == "cc":
                        act.wait_ge(panel_done, p + 1)
                        if c_:
                            act.wait_ge(cu_ready, l * NC + c_)
                        act.activation(c_sb[:, :, ts_], src, ACT.Copy).then_inc(cc_ready, 1)
                        act.wait_ge(cc_ready, l * NC + c_ + 1)
                        act.sem_inc(slot_free[slot], 1)
                    elif kind == "cu":
                        act.wait_ge(cu_ready, l * NC + c_ + 1)
                        if c_:
                            act.wait_ge(yf_ready, yf_of[y_no[l, "c", c_ - 1]] + 1)
                        sg = slice(0, 2) if l < DEPTH - 1 else slice(1, 2)
                        for b in range(NB):
                            wt = pars[l][:, ROW_CONV + 2 * c_ + b:ROW_CONV + 2 * c_ + b + 1]
                            act.activation(c_acc[:, b, sg, :], c_u[:, b, sg, 0:LAT], ACT.Copy, scale=wt).then_inc(c1_ready, 1)
                    elif kind == "cb":
                        y_high(y_no[l, "c", c_], y_tmp[:, :, ts_], slice(2 * c_, 2 * c_ + 2), ts_)
                    elif kind == "up":
                        act.wait_ge(panel_done, p + 1)
                        no = y_no[l, "up", b_, c_]
                        act.wait_ge(y_ready, no)
                        act.activation(y_tmp[:, :, ts_], src, ACT.Relu).then_inc(up_ready, 1)
                        act.wait_ge(up_ready, (l * 4 + b_) * NC + c_ + 1)
                        act.sem_inc(slot_free[slot], 1)
                        y_high(no, y_tmp[:, :, ts_], slice(2 * c_, 2 * c_ + 2), ts_)
                elif k == "squares":
                    j, ts_ = st["j"], norm_cols(st)
                    if l == 0 and st["n"] == 1:
                        act.wait_ge(s_xt, KT)
                    else:
                        act.wait_ge(x_ready, x_needed(st))
                    if n_norm or j >= 2:
                        act.wait_ge(sq_used, n_norm * (NC - 1) + max(j - 1, 0))
                    act.activation(n_sq[:, j % 2, :, ts_], xT[:, 2 * j:2 * j + 2, ts_], ACT.Square).then_inc(sq_ready, 1)
                    if j == NC - 1:
                        n_norm += 1
                        b = bank(act, u["ss"])
                        if n_norm == 1:
                            act.wait_ge(s_const, 3)
                        act.activation(n_r[:, ts_], b[:, ts_], ACT.Sqrt, bias=eps).then_inc(sd_ready, 1)
                elif k == "qss":
                    j = st["j"]
                    b = bank(act, u[0])
                    t0 = 0 if j == 0 else cols(l).start // P
                    act.activation(q_sd.rearrange("p (b t) -> p b t", b=NB)[:, :, t0:TT],
                                   b[:, 0:NB * TT].rearrange("p (b t) -> p b t", b=NB)[:, :, t0:TT],
                                   ACT.Sqrt, bias=eps).then_inc(qsd_ready, 1)
                elif k == "apply":
                    ts_ = slice(0, TOK) if not (l == DEPTH - 1 and st["n"] == 2) else cols(l)
                    j = st["j"]
                    if j == 0 and st["n"] == 2:
                        act.wait_ge(panel_done, panel_no("wo", l, NC - 1) + 1)
                    elif j == 0 and l:
                        act.wait_ge(panel_done, panel_no("up", l - 1, NC - 1, 3) + 1)
                    for kt in (2 * j, 2 * j + 1):
                        act.wait_ge(hf_ready, n_hf + 1)
                        act.activation(hH[:, kt, ts_], n_h[:, kt % 4, ts_], ACT.Copy).then_inc(hH_ready, 1)
                        n_hf += 1
                    if st["n"] == 1 and j == 0:
                        act.wait_ge(s_wg, 80 * (l + 1))
                        act.wait_ge(wgz_ready, 2 * l + 2)
                        act.activation(wgH[:, :, 0:16], w_gate[:, :, :], ACT.Copy).then_inc(wgH_ready, 1)
                elif k == "gate_exp":
                    act.wait_ge(fneg_ready, l + 1)
                    act.activation(rows["f_exp"][0:8, :], rows["f_neg"][0:8, :], ACT.Exp).then_inc(fln_ready, 1)
                    act.wait_ge(fln_ready, 2 * l + 1)
                    act.activation(rows["f_exp"][0:8, :], rows["f_exp"][0:8, :], ACT.Ln, bias=1.0).then_inc(fln_ready, 1)
                elif k == "gate_e":
                    act.wait_ge(erow_ready, l + 1)
                    act.activation(rows["e_run"][0:8, :], rows["e_run"][0:8, :], ACT.Exp).then_inc(eexp_ready, 1)
                elif k == "weigh":
                    h = st["h"]
                    act.wait_ge(gc_ready, l + 1)
                    if h:
                        bk, un = list(next(q for q in PLAN if q["k"] == "value" and q["l"] == l and q["h"] == h - 1)["u"].values())[-1]
                        act.wait_ge(full[bk], un + 1)
                    for d in range(2):
                        b = bank(act, u[f"m{d}"])
                        for s, row in enumerate(packed(l, d)):
                            for a, e, off in row:
                                last = act.activation(EP[:, d, off:off + e - a], b[:, a:e], ACT.Exp, scale=-1.0,
                                                      bias=g_col[:, d, s, d * MH + h:d * MH + h + 1])
                                if (s, a) != (TT - 1, row[-1][0]):
                                    last.then_inc(E_ready, 1)
                        last.then_inc(free[u[f"m{d}"][0]], 1)
                elif k == "value":
                    h = st["h"]
                    tts = range(TT) if l < DEPTH - 1 else range(CTX // P, TT)
                    for i, tt in enumerate(tts):
                        act.wait_ge(hraw_ready, (sum(len(spans_tt(q)) for q in range(l)) * MH) + h * len(tts) + i + 1)
                        if i:
                            act.wait_ge(hss_ready, h_count(l, h, tt - 1))
                        act.activation(junk[:, :], hM[:, h, tt, :], ACT.Square, accum_out=mss[:, tt:tt + 1]).then_inc(hss_ready, 1)
                    act.wait_ge(hss_ready, h_count(l, h, TT - 1))
                    act.activation(mrs[:, tts[0]:TT], mss[:, tts[0]:TT], ACT.Sqrt, scale=1.0 / MV, bias=eps).then_inc(mrs_ready, 1)
                elif k == "turn":
                    h = st["h"]
                    act.wait_ge(y_ready, y_no[l, "m", h])
                    for j in range(2):
                        b = bank(act, u[j])
                        r = ROW_MN + 2 * h + j
                        act.activation(y_tmp[:, j, cols(l)], b[:, cols(l)], ACT.Copy,
                                       scale=pars[l][:, r:r + 1]).then_inc(free[u[j][0]], 1)
                    for j in range(2):
                        act.wait_ge(free[u[j][0]], u[j][1] + 1)
                    act.sem_inc(ot_ready, 1)
                    y_high(y_no[l, "m", h], y_tmp[:, :, cols(l)], slice(2 * h, 2 * h + 2), cols(l))
                elif k == "scores":
                    h = st["h"]
                    act.wait_ge(nb_ready, l * AH + h + 1)
                    for qt in range(2):
                        b = bank(act, u[qt])
                        act.activation(pr[:, qt * TOK:(qt + 1) * TOK], b[:, :], ACT.Exp, bias=anb[:, qt:qt + 1],
                                       scale=float(AHD) ** -0.5, accum_out=asum[:, qt:qt + 1]).then_inc(p_exp, 1)
                    if 2 in u:
                        b = bank(act, u[2])
                        for qt in range(2):
                            act.activation(pr[:, 2 * TOK + qt * CTX:2 * TOK + (qt + 1) * CTX], b[:, qt * CTX:(qt + 1) * CTX],
                                           ACT.Exp, bias=anb[:, 2 + qt:3 + qt], scale=float(AHD) ** -0.5,
                                           accum_out=asum[:, 2 + qt:3 + qt]).then_inc(p_exp, 1)
                elif k == "attend":
                    h = st["h"]
                    b = bank(act, u[0])
                    act.activation(q_a[:, h, cols(l)], b[:, cols(l)], ACT.Copy).then_inc(free[u[0][0]], 1)
                elif k == "ysplit":
                    j = st["j"]
                    no = y_no[l, "a", j]
                    bk, un = next(q for q in PLAN if q["k"] == "attend" and q["l"] == l and q["h"] == 2 * j + 1)["u"][0]
                    act.wait_ge(free[bk], un + 1)
                    act.wait_ge(panel_done, panel_no("proj", l, NC - 1, 0) + 1)
                    act.activation(yH[:, 2 * j:2 * j + 2, cols(l)], q_a[:, 2 * j:2 * j + 2, cols(l)],
                                   ACT.Copy).then_inc(yH_ready, 1)
                elif k == "msplit":
                    j = st["j"]
                    act.wait_ge(m_ready, (l * 3 + 2) * NC + j + 1)
                    act.wait_ge(panel_done, panel_no("gate", l, NC - 1, 2) + 1)
                    act.activation(hH[:, 2 * j:2 * j + 2, cols(l)], merged[:, 2 * j:2 * j + 2, cols(l)],
                                   ACT.Copy).then_inc(hH_ready, 1)

        @block.gpsimd
        def _(pool):
            pool.memset(c_win[:, :].bitcast(F32), 0.0).then_inc(s_cz, 1)
            pool.memset(mean_d, 1.0 / D).then_inc(s_const, 1)
            pool.memset(mean_h, 1.0 / AHD).then_inc(s_const, 1)
            pool.memset(eps, EPS).then_inc(s_const, 1)

            def split(st):
                p, s = st["p"], st["s"]
                for i in range(2):
                    ks = slice(i * KH, i * KH + KP)
                    pool.wait_ge(wH_ready, 2 * s + i + 1)
                    pool.tensor_tensor(wL[:, s % 2, ks, :], raw[:, p % RAW, ks, :], wH[:, s % 2, ks, :].bitcast(F32),
                                       ALU.subtract).then_inc(wL_ready, 1)

            def y_rest(no, src, kts, ts_):
                pool.wait_ge(yH_ready, no + 1)
                pool.tensor_tensor(yL[:, kts, ts_], src, yH[:, kts, ts_].bitcast(F32), ALU.subtract).then_inc(y_ready, 1)

            for st in PLAN:
                k, l, u = st["k"], st["l"], st["u"]
                if k == "start":
                    split(PANELS[0])
                elif k == "panel":
                    nx = next_panel(st)
                    if nx:
                        split(nx)
                    kind, c_, b_ = st["kind"], st["c"], st["b"]
                    ts_ = cols(l)
                    if kind == "proj":
                        n = (l * 3 + b_) * NC + c_
                        pool.wait_ge(mt_ready, n + 1)
                        if b_ == 0:
                            pool.sem_inc(m_ready, 1)
                        else:
                            m = merged[:, 2 * c_:2 * c_ + 2, ts_]
                            pool.tensor_tensor(m, m, gs[:, :, ts_], ALU.add).then_inc(m_ready, 1)
                    elif kind == "cc" and c_ == 0:
                        pool.wait_ge(y_ready, y_no[l, "a", 3] + 1)
                        pool.wait_ge(panel_done, panel_no("gate", l, 1, 1) + 1)
                        pool.memset(c_u[:, :, :, 0:1], 0.0).then_inc(cpad, 1)
                        pool.memset(c_u[:, :, :, LAT + 1:LAT + 2], 0.0).then_inc(cpad, 1)
                    elif kind == "cb":
                        y_rest(y_no[l, "c", c_], y_tmp[:, :, ts_], slice(2 * c_, 2 * c_ + 2), ts_)
                elif k == "apply":
                    ts_ = slice(0, TOK) if not (l == DEPTH - 1 and st["n"] == 2) else cols(l)
                    j = st["j"]
                    if st["n"] == 1 and j == 0:
                        if l:
                            pool.wait_ge(panel_done, panel_no("down", l - 1, NC - 1, FF // D - 1) + 1)
                        else:
                            pool.wait_ge(s_par, 3)
                        for t in (wgH, wgL):
                            pool.memset(t[:, :, :].bitcast(F32), 0.0).then_inc(wgz_ready, 1)
                    for kt in (2 * j, 2 * j + 1):
                        pool.wait_ge(hH_ready, h_no[l, st["n"]] + kt + 1)
                        pool.tensor_tensor(hL[:, kt, ts_], n_h[:, kt % 4, ts_], hH[:, kt, ts_].bitcast(F32),
                                           ALU.subtract).then_inc(h_ready, 1)
                    if st["n"] == 1 and j == 0:
                        pool.wait_ge(wgH_ready, l + 1)
                        pool.tensor_tensor(wgL[:, :, 0:16], w_gate[:, :, :], wgH[:, :, 0:16].bitcast(F32),
                                           ALU.subtract).then_inc(wg_ready, 1)
                    if st["n"] == 1 and j == NC - 1:
                        pool.wait_ge(h_ready, h_no[l, 1] + KT)
                        pool.memset(vaug[:, :, :, MV:MV + 1], 1.0).then_inc(vones, 1)
                        pool.memset(rows["ones"][0:8, :], 1.0).then_inc(orow, 1)
                elif k == "weigh":
                    h = st["h"]
                    pool.wait_ge(P_ready, l * MH + h + 1)
                    last = None
                    for d in range(2):
                        for s, row in enumerate(packed(l, d)):
                            for a, e, off in row:
                                if a <= s * P < e:
                                    v = EP[:, d, off + s * P - a:off + s * P - a + P]
                                    sign = 1 if d == 0 else -1
                                    last = pool.affine_select(out=v, in_=v, compare_op=ALU.is_ge, fill=0.0, base=0,
                                                              pattern=[[sign, P]], channel_multiplier=-sign)
                    last.then_inc(mask_ready, 1)
                elif k == "turn":
                    h = st["h"]
                    y_rest(y_no[l, "m", h], y_tmp[:, :, cols(l)], slice(2 * h, 2 * h + 2), cols(l))
                elif k == "ysplit":
                    j = st["j"]
                    y_rest(y_no[l, "a", j], q_a[:, 2 * j:2 * j + 2, cols(l)], slice(2 * j, 2 * j + 2), cols(l))
                elif k == "msplit":
                    j = st["j"]
                    pool.wait_ge(hH_ready, h_no[l, "m", j] + 1)
                    pool.tensor_tensor(hL[:, 2 * j:2 * j + 2, cols(l)], merged[:, 2 * j:2 * j + 2, cols(l)],
                                       hH[:, 2 * j:2 * j + 2, cols(l)].bitcast(F32), ALU.subtract).then_inc(h_ready, 1)


        @block.vector
        def _(dve):
            count = [0]

            def link(ins):
                count[0] += 1
                ins.then_inc(dchain, 1)
                dve.wait_ge(dchain, count[0])

            def start_link(ins):
                count[0] += 1
                ins.then_inc(dchain, 1)

            def freed(ins, u):
                ins.then_inc(free[u[0]], 1)

            def split(st):
                p, s = st["p"], st["s"]
                for i in range(2):
                    ks = slice(i * KH + KP, (i + 1) * KH)
                    dve.wait_ge(wH_ready, 2 * s + i + 1)
                    dve.tensor_tensor(wL[:, s % 2, ks, :], raw[:, p % RAW, ks, :], wH[:, s % 2, ks, :].bitcast(F32),
                                      ALU.subtract).then_inc(wLv_ready, 1)

            n_norm = 0
            for st in PLAN:
                k, l, u = st["k"], st["l"], st["u"]
                if k == "start":
                    up = u["par2"]
                    freed(dve.tensor_copy(pars[2][:, :], bank(dve, up)[:, 0:24]), up)
                    dve.wait_ge(free[up[0]], up[1] + 1)
                    dve.tensor_copy(c2[:, :, 0], pars[2][:, 0:8]).then_inc(s_par, 1)
                    dve.tensor_copy(c2[:, :, 1], pars[2][:, 8:16]).then_inc(s_par, 1)
                    dve.wait_ge(s_par, 2)
                    dve.wait_ge(s_cexp, 1)
                    link(dve.tensor_scalar(c2e[:, :, :], c2e[:, :, :], 1.0, None, ALU.add))
                    link(dve.reciprocal(c2e[:, :, :], c2e[:, :, :]))
                    dve.tensor_tensor(c2[:, :, :], c2[:, :, :], c2e[:, :, :], ALU.mult).then_inc(s_silu, 1)
                    dve.wait_ge(cH_ready, 1)
                    dve.tensor_tensor(cHL[:, :, 2:4], c2[:, :, :], cHL[:, :, 0:2].bitcast(F32),
                                      ALU.subtract).then_inc(s_silu, 1)
                    split(PANELS[0])
                    for kt in range(KT):
                        b = bank(dve, u[f"x{kt}"])
                        freed(dve.tensor_copy(xT[:, kt, :], b[:, :]), u[f"x{kt}"])
                    for kt in range(KT - 4, KT):
                        dve.wait_ge(free[u[f"x{kt}"][0]], u[f"x{kt}"][1] + 1)
                    dve.sem_inc(s_xt, KT)
                    for i in range(DEPTH):
                        up = u[f"par{i}"]
                        freed(dve.tensor_copy(pars[i][:, 0:ROWS], bank(dve, up)[:, 0:ROWS]), up)
                    for i in range(DEPTH):
                        dve.wait_ge(free[u[f"par{i}"][0]], u[f"par{i}"][1] + 1)
                    for i in range(DEPTH):
                        v = pars[i][:, ROW_MN:ROW_MN + 8]
                        start_link(dve.tensor_scalar(v, v, 0.5, None, ALU.mult))
                    dve.wait_ge(dchain, count[0])
                    dve.sem_inc(s_par, 1)
                elif k == "panel":
                    nx = next_panel(st)
                    if nx:
                        split(nx)
                    kind, p, c_, b_ = st["kind"], st["p"], st["c"], st["b"]
                    slot = p % 2
                    ts_ = cols(l)
                    src = pp[:, slot, :, ts_]
                    if kind == "ada":
                        dve.wait_ge(panel_done, p + 1)
                        i = c_ % NC
                        if i == 0 and l + c_:
                            dve.wait_ge(mod_ready, 6 * l + c_ // NC)
                        dve.tensor_copy(ada_rows[:, i * PC:(i + 1) * PC], pp[0:4, slot, 0, 0:PC]).then_inc(ada_copied, 1)
                        dve.wait_ge(ada_copied, 6 * NC * l + c_ + 1)
                        dve.sem_inc(slot_free[slot], 1)
                    elif kind in ("mv", "av"):
                        dve.wait_ge(panel_done, p + 1)
                        dst = vaug[:, :, c_, 0:MV] if kind == "mv" else v_a[:, :, :]
                        done = mv_ready if kind == "mv" else av_ready
                        dve.tensor_copy(dst, pp[:, slot, :, :].rearrange("p b (t n) -> p (b t) n", t=2)).then_inc(done, 1)
                        dve.wait_ge(done, MH * l + c_ + 1 if kind == "mv" else l + 1)
                        dve.sem_inc(slot_free[slot], 1)
                    elif kind == "proj":
                        dve.wait_ge(panel_done, p + 1)
                        dst = merged[:, 2 * c_:2 * c_ + 2, ts_] if b_ == 0 else gs[:, :, ts_]
                        dve.wait_ge(gate_exp, (l * 3 + b_) * NC + c_ + 1)
                        dve.scalar_tensor_tensor(out=dst, in0=gs[:, :, ts_], scalar=1.0, in1=src,
                                                 op0=ALU.add, op1=ALU.mult).then_inc(mt_ready, 1)
                        dve.wait_ge(mt_ready, (l * 3 + b_) * NC + c_ + 1)
                        dve.sem_inc(slot_free[slot], 1)
                    elif kind == "cu":
                        dve.wait_ge(panel_done, p + 1)
                        dve.wait_ge(cc_ready, l * NC + c_ + 1)
                        if c_ == 0:
                            dve.wait_ge(cpad, 2 * l + 2)
                        sg = slice(0, 2) if l < DEPTH - 1 else slice(1, 2)
                        n = sg.stop - sg.start
                        for b in range(NB):
                            i = dve.tensor_tensor(c_u[:, b, sg, 1:LAT + 1],
                                                  pp[:, slot, b, ts_].rearrange("p (s t) -> p s t", s=n),
                                                  c_sb[:, b, ts_].rearrange("p (s t) -> p s t", s=n), ALU.mult)
                            if b < NB - 1:
                                start_link(i)
                        i.then_inc(cu_ready, 1)
                        dve.wait_ge(dchain, count[0])
                        dve.wait_ge(cu_ready, l * NC + c_ + 1)
                        dve.sem_inc(slot_free[slot], 1)
                        dve.wait_ge(c1_ready, (l * NC + c_ + 1) * NB)
                        for tap in (1, 2):
                            for b in range(NB):
                                r = ROW_CONV + tap * 8 + 2 * c_ + b
                                start_link(dve.scalar_tensor_tensor(
                                    out=c_acc[:, b, sg, :], in0=c_u[:, b, sg, tap:tap + LAT], scalar=pars[l][:, r:r + 1],
                                    in1=c_acc[:, b, sg, :], op0=ALU.mult, op1=ALU.add))
                            dve.wait_ge(dchain, count[0])
                    elif kind == "cb":
                        dve.wait_ge(panel_done, p + 1)
                        no = y_no[l, "c", c_]
                        dve.wait_ge(y_ready, no)
                        sg = slice(0, 2) if l < DEPTH - 1 else slice(1, 2)
                        for b in range(NB):
                            i = dve.tensor_tensor(y_tmp[:, b, ts_], pp[:, slot, b, ts_],
                                                  c_acc[:, b, sg, :].rearrange("p s t -> p (s t)"), ALU.mult)
                            if b < NB - 1:
                                start_link(i)
                        dve.wait_ge(dchain, count[0])
                        i.then_inc(yf_ready, 1)
                        dve.wait_ge(yf_ready, yf_of[no] + 1)
                        dve.sem_inc(slot_free[slot], 1)
                    elif kind == "up":
                        dve.wait_ge(up_ready, (l * 4 + b_) * NC + c_ + 1)
                        dve.tensor_tensor(y_tmp[:, :, ts_], y_tmp[:, :, ts_], y_tmp[:, :, ts_], ALU.mult).then_inc(yf_ready, 1)
                        no = y_no[l, "up", b_, c_]
                        kts = slice(2 * c_, 2 * c_ + 2)
                        dve.wait_ge(yH_ready, no + 1)
                        dve.tensor_tensor(yL[:, kts, ts_], y_tmp[:, :, ts_], yH[:, kts, ts_].bitcast(F32),
                                          ALU.subtract).then_inc(y_ready, 1)
                    elif kind in ("wo", "down"):
                        dve.wait_ge(panel_done, p + 1)
                        g = 16 if kind == "wo" else 40
                        n = x_no[l, kind, b_, c_]
                        for b in range(NB):
                            kt = 2 * c_ + b
                            for hs, v in halves(l):
                                i = dve.scalar_tensor_tensor(out=xT[:, kt, hs], in0=pp[:, slot, b, hs],
                                                             scalar=modT[:, l, g + kt, v:v + 1], in1=xT[:, kt, hs],
                                                             op0=ALU.mult, op1=ALU.add)
                                if (b, v) != (NB - 1, halves(l)[-1][1]):
                                    start_link(i)
                        i.then_inc(x_ready, 1)
                        dve.wait_ge(dchain, count[0])
                        dve.wait_ge(x_ready, n + 1)
                        dve.sem_inc(slot_free[slot], 1)
                elif k == "adaturn":
                    m = st["m"]
                    b = bank(dve, u[0])
                    dst = modT[:, l, KT * m:KT * (m + 1), :]
                    bias = pars[l][:, ROW_ADA + KT * m:ROW_ADA + KT * (m + 1)].unsqueeze(2).to_broadcast([P, KT, 2])
                    freed(dve.tensor_tensor(dst, b[:, 0:2 * KT].rearrange("p (k v) -> p k v", v=2), bias, ALU.add), u[0])
                    dve.wait_ge(free[u[0][0]], u[0][1] + 1)
                    if m == 2:
                        dve.tensor_scalar(dst, dst, 0.5, None, ALU.mult).then_inc(mod_ready, 1)
                    else:
                        dve.sem_inc(mod_ready, 1)
                elif k == "squares":
                    if st["j"] == NC - 1:
                        n_norm += 1
                        ts_ = norm_cols(st)
                        dve.wait_ge(sd_ready, n_norm)
                        dve.sem_inc(free[u["ss"][0]], 1)
                        link(dve.reciprocal(n_r[:, ts_], n_r[:, ts_]))
                elif k == "apply":
                    n = st["n"]
                    full_ = not (l == DEPTH - 1 and n == 2)
                    ts_ = slice(0, TOK) if full_ else cols(l)
                    hv = [(slice(CTX, TOK), 0)] + ([(slice(0, CTX), 1)] if full_ else [])
                    sh, sc, r = (0, 8, ROW_N1) if n == 1 else (24, 32, ROW_N2)
                    if st["j"] == 0:
                        for v in range(2):
                            start_link(dve.scalar_tensor_tensor(out=gain[:, :, v], in0=modT[:, l, sc:sc + 8, v], scalar=1.0,
                                                                in1=pars[l][:, r:r + 8], op0=ALU.add, op1=ALU.mult))
                        dve.wait_ge(dchain, count[0])
                    for kt in (2 * st["j"], 2 * st["j"] + 1):
                        link(dve.tensor_tensor(n_t[:, kt % 2, ts_], xT[:, kt, ts_], n_r[:, ts_], ALU.mult))
                        if kt >= 4:
                            dve.wait_ge(h_ready, h_no[l, n] + kt - 3)
                        for hs, v in hv:
                            i = dve.tensor_scalar(n_h[:, kt % 4, hs], n_t[:, kt % 2, hs], gain[:, kt, v:v + 1],
                                                  modT[:, l, sh + kt, v:v + 1], ALU.mult, ALU.add)
                            if (hs, v) != hv[-1]:
                                start_link(i)
                        i.then_inc(hf_ready, 1)
                elif k == "gate_tok":
                    b = bank(dve, u["g"])
                    dve.tensor_copy(rows["g_rows"][:, :], b[0:16, :]).then_inc(gr_ready, 1)
                    dve.wait_ge(gr_ready, 3 * l + 1)
                    dve.sem_inc(free[u["g"][0]], 1)
                    dve.tensor_copy(rows["g_back"][:, 0:CTX], rows["g_rows"][:, CTX - 1::-1]).then_inc(gr_ready, 1)
                    dve.tensor_copy(rows["g_back"][:, CTX:TOK], rows["g_rows"][:, TOK - 1:CTX - 1:-1]).then_inc(gr_ready, 1)
                elif k == "gate_sel":
                    R = {n: t[0:8, :] for n, t in rows.items()}
                    dve.wait_ge(s_wg, 80 * (l + 1))
                    b = bank(dve, u["f"])
                    freed(dve.tensor_scalar(R["f_pre"], b[0:8, :], gb[0:8, 1:2], None, ALU.add), u["f"])
                    dve.wait_ge(free[u["f"][0]], u["f"][1] + 1)
                    dve.scalar_tensor_tensor(out=R["f_neg"], in0=R["f_pre"], scalar=-1.0, in1=R["f_pre"],
                                             op0=ALU.mult, op1=ALU.min).then_inc(fneg_ready, 1)
                elif k == "gate_scan":
                    R = {n: t[0:8, :] for n, t in rows.items()}
                    dve.wait_ge(fln_ready, 2 * l + 2)
                    link(dve.scalar_tensor_tensor(out=R["log_f"], in0=R["f_pre"], scalar=0.0, in1=R["f_exp"],
                                                  op0=ALU.min, op1=ALU.subtract))
                    dve.wait_ge(orow, l + 1)
                    link(dve.tensor_tensor_scan(R["F_run"], R["ones"], R["log_f"], 0.0, ALU.mult, ALU.add))
                    b = bank(dve, u["i"])
                    dve.scalar_tensor_tensor(out=R["a_run"], in0=b[0:8, :], scalar=gb[0:8, 0:1], in1=R["F_run"],
                                             op0=ALU.add, op1=ALU.subtract).then_inc(cols_in, 1)
                    dve.wait_ge(cols_in, 4 * l + 1)
                    dve.sem_inc(free[u["i"][0]], 1)
                    link(dve.tensor_tensor_scan(R["M_run"], R["a_run"], R["a_run"], 0.0, ALU.max, ALU.max))
                    dve.scalar_tensor_tensor(out=R["e_run"], in0=R["F_run"], scalar=-1.0, in1=R["M_run"],
                                             op0=ALU.mult, op1=ALU.subtract).then_inc(erow_ready, 1)
                    for nm, fr in (("M_back", "M_run"), ("a_back", "a_run")):
                        start_link(dve.tensor_copy(R[nm][:, 0:CTX], R[fr][:, CTX - 1::-1]))
                        i = dve.tensor_copy(R[nm][:, CTX:TOK], R[fr][:, TOK - 1:CTX - 1:-1])
                        if nm == "M_back":
                            start_link(i)
                        else:
                            i.then_inc(cols_in, 1)
                    dve.wait_ge(dchain, count[0])
                elif k == "gate_e2":
                    R = {n: t[0:8, :] for n, t in rows.items()}
                    dve.wait_ge(eexp_ready, l + 1)
                    dve.tensor_copy(R["e_back"][:, 0:CTX], R["e_run"][:, CTX - 1::-1]).then_inc(cols_in, 1)
                    dve.tensor_copy(R["e_back"][:, CTX:TOK], R["e_run"][:, TOK - 1:CTX - 1:-1]).then_inc(cols_in, 1)
                elif k == "gate_cols":
                    b = bank(dve, u["g"])
                    dve.tensor_copy(g_col[:, :, :, :], b[:, 0:4 * TT * 8].rearrange("p (i t n) -> p i t n", i=4, t=TT)
                                    ).then_inc(gc_ready, 1)
                    dve.wait_ge(gc_ready, l + 1)
                    dve.sem_inc(free[u["g"][0]], 1)
                elif k == "weigh":
                    h = st["h"]
                    for d in range(2):
                        dve.wait_ge(free[u[f"m{d}"][0]], u[f"m{d}"][1] + 1)
                    dve.wait_ge(E_ready, e_count(l, h))
                    for s in range(TT):
                        us = u[f"s{min(s, 2)}"]
                        b = bank(dve, us)
                        for d in range(2):
                            for a, e, off in packed(l, d)[s]:
                                src = b[:, a:e] if s < 2 else b[:, (s - 2) * LAT + a - CTX:(s - 2) * LAT + e - CTX]
                                v = EP[:, d, off:off + e - a]
                                i = dve.tensor_tensor(v, v, src, ALU.mult)
                                if not (s != 2 and (d, a) == (1, packed(l, 1)[s][-1][0])):
                                    start_link(i)
                        if s != 2:
                            freed(i, us)
                    for s in (0, 1, 3):
                        us = u[f"s{min(s, 2)}"]
                        dve.wait_ge(free[us[0]], us[1] + 1)
                    dve.wait_ge(dchain, count[0])
                    dve.sem_inc(P_ready, 1)
                elif k == "value":
                    h = st["h"]
                    tts = spans_tt(l)
                    for tt in tts:
                        bs = [bank(dve, u[tt, d]) for d in range(2)]
                        for d in range(2):
                            start_link(dve.tensor_scalar(mstat[:, tt, d:d + 1], bs[d][:, MV:MV + 1], -1.0,
                                                         g_col[:, 2 + d, tt, d * MH + h:d * MH + h + 1], ALU.mult, ALU.max))
                        dve.wait_ge(dchain, count[0])
                        for d in range(2):
                            start_link(dve.tensor_scalar(mstat[:, tt, 2 + d:3 + d], bs[d][:, MV:MV + 1],
                                                         mstat[:, tt, d:d + 1], None, ALU.max))
                        dve.wait_ge(dchain, count[0])
                        link(dve.reciprocal(mstat[:, tt, 4:6], mstat[:, tt, 2:4]))
                        dve.tensor_scalar(hM[:, h, tt, :], bs[0][:, 0:MV], mstat[:, tt, 4:5], None,
                                          ALU.mult).then_inc(free[u[tt, 0][0]], 1)
                        dve.wait_ge(free[u[tt, 0][0]], u[tt, 0][1] + 1)
                        dve.scalar_tensor_tensor(out=hM[:, h, tt, :], in0=bs[1][:, 0:MV], scalar=mstat[:, tt, 5:6],
                                                 in1=hM[:, h, tt, :], op0=ALU.mult, op1=ALU.add).then_inc(hraw_ready, 1)
                        dve.wait_ge(hraw_ready, h_count(l, h, tt))
                        dve.sem_inc(free[u[tt, 1][0]], 1)
                    dve.wait_ge(mrs_ready, l * MH + h + 1)
                    rs = mrs[:, tts[0]:TT]
                    link(dve.reciprocal(rs, rs))
                    for tt in tts:
                        i = dve.tensor_scalar(hM[:, h, tt, :], hM[:, h, tt, :], mrs[:, tt:tt + 1], None, ALU.mult)
                        if tt < TT - 1:
                            start_link(i)
                    i.then_inc(hn_ready, 1)
                elif k == "turn":
                    h = st["h"]
                    ts_ = cols(l)
                    dve.wait_ge(ot_ready, l * MH + h + 1)
                    v = y_tmp[:, :, ts_]
                    dve.scalar_tensor_tensor(out=v, in0=sig_o[:, h % 2, :, ts_], scalar=1.0, in1=v,
                                             op0=ALU.add, op1=ALU.mult).then_inc(yf_ready, 1)
                elif k == "qss":
                    j = st["j"]
                    t0 = 0 if j == 0 else cols(l).start // P
                    dve.wait_ge(qsd_ready, l * 5 + j + 1)
                    dve.sem_inc(free[u[0][0]], 1)
                    dve.reciprocal(q_rs.rearrange("p (b t) -> p b t", b=NB)[:, :, t0:TT],
                                   q_sd.rearrange("p (b t) -> p b t", b=NB)[:, :, t0:TT]).then_inc(qrs_ready, 1)
                elif k == "qbc":
                    j = st["j"]
                    ts_ = slice(0, TOK) if j == 0 else cols(l)
                    g = ROW_KN if j == 0 else ROW_QN
                    for b_ in range(NB):
                        b = bank(dve, u[b_])
                        dst = k_a[:, b_, ts_] if j == 0 else q_a[:, 2 * j - 2 + b_, ts_]
                        freed(dve.scalar_tensor_tensor(out=dst, in0=dst, scalar=pars[l][:, g:g + 1], in1=b[:, ts_],
                                                       op0=ALU.mult, op1=ALU.mult), u[b_])
                    for b_ in range(NB):
                        dve.wait_ge(free[u[b_][0]], u[b_][1] + 1)
                    dve.sem_inc(qn_ready, 1)
                elif k == "qrot":
                    j = st["j"]
                    b = bank(dve, u[0])
                    dst = [k_a[:, b_, CTX:TOK] if j == 0 else q_a[:, 2 * j - 2 + b_, CTX:TOK] for b_ in range(NB)]
                    for b_ in range(NB):
                        i = dve.tensor_tensor(q_t[:, b_, :], b[:, b_ * LAT:(b_ + 1) * LAT], ropeS, ALU.mult)
                        if b_ < NB - 1:
                            start_link(i)
                        else:
                            freed(i, u[0])
                        start_link(dve.tensor_tensor(dst[b_], dst[b_], ropeC, ALU.mult))
                    dve.wait_ge(dchain, count[0])
                    dve.wait_ge(free[u[0][0]], u[0][1] + 1)
                    start_link(dve.tensor_tensor(dst[0], dst[0], q_t[:, 0, :], ALU.add))
                    dve.tensor_tensor(dst[1], dst[1], q_t[:, 1, :], ALU.add).then_inc(qk_ready, 1)
                elif k == "scores":
                    h = st["h"]
                    nq = 4 if 2 in u else 2
                    for qt in range(2):
                        b = bank(dve, u[qt])
                        start_link(dve.reduce_max(amax[:, qt:qt + 1], b[:, :], AX))
                    if 2 in u:
                        b = bank(dve, u[2])
                        start_link(dve.reduce_max(amax[:, 2:4], b[:, :].rearrange("p (q k) -> p q k", q=2), AX))
                    dve.wait_ge(dchain, count[0])
                    dve.tensor_scalar(anb[:, 0:nq], amax[:, 0:nq], -float(AHD) ** -0.5, None, ALU.mult).then_inc(nb_ready, 1)
                    dve.wait_ge(p_exp, p_count(l, h))
                    for i in range(3 if 2 in u else 2):
                        dve.sem_inc(free[u[i][0]], 1)
                    link(dve.reciprocal(ars[:, 0:nq], asum[:, 0:nq]))
                    for qt in range(nq):
                        a = qt * TOK if qt < 2 else 2 * TOK + (qt - 2) * CTX
                        v = pr[:, a:a + (TOK if qt < 2 else CTX)]
                        i = dve.tensor_scalar(v, v, ars[:, qt:qt + 1], None, ALU.mult)
                        if qt < nq - 1:
                            start_link(i)
                    dve.wait_ge(dchain, count[0])
                    i.then_inc(p_ready, 1)
                elif k == "probs":
                    h = st["h"]
                    nb = 3 if 2 in u else 2
                    for i in range(nb):
                        b = bank(dve, u[i])
                        freed(dve.tensor_copy(prT[:, i * TOK:(i + 1) * TOK], b[:, :]), u[i])
                    for i in range(nb):
                        dve.wait_ge(free[u[i][0]], u[i][1] + 1)
                    dve.sem_inc(pT_ready, 1)
                elif k == "final":
                    ts_ = cols(DEPTH)
                    for kt in range(KT):
                        dve.scalar_tensor_tensor(out=xT[:, kt, ts_], in0=xT[:, kt, ts_],
                                                 scalar=pars[2][:, 16 + kt:17 + kt], in1=n_r[:, ts_],
                                                 op0=ALU.mult, op1=ALU.mult).then_inc(hf_ready, 1)
                    for i in range(4):
                        b = bank(dve, u[i])
                        j = dve.tensor_copy(f_out[:, i // 2, (i % 2) * 512:(i % 2 + 1) * 512], b[:, :])
                        if i % 2 == 0:
                            start_link(j)
                            dve.wait_ge(dchain, count[0])
                        else:
                            j.then_inc(f_ready, 1)


def e_count(l, h):
    per = [sum(len(r) for d in range(2) for r in packed(q, d)) - 2 for q in range(DEPTH)]
    return sum(per[q] * MH for q in range(l)) + per[l] * (h + 1)


def h_count(l, h, tt):
    n = [TT if q < DEPTH - 1 else TT - CTX // P for q in range(DEPTH)]
    first = TT - n[l]
    return sum(n[q] * MH for q in range(l)) + n[l] * h + tt - first + 1


def p_count(l, h):
    n = [4 if q < DEPTH - 1 else 2 for q in range(DEPTH)]
    return sum(n[q] * AH for q in range(l)) + n[l] * (h + 1)


_INS = ["x", "c", "ctx", "c_ctx", "w_ada", "b_ada", "norm1", "norm2", "w_in", "mlstm_gate_b", "mlstm_norm", "q_norm",
        "k_norm", "conv_w", "w_proj_m", "w_proj_a", "w_proj_c", "w_out", "w_up", "w_down", "final_norm"]


def kernel(**inputs):
    import numpy as _np
    import concourse.bacc as _bacc
    from concourse import mybir as _mybir
    from concourse.bass_utils import run_bass_kernel_spmd as _run

    nc = _bacc.Bacc("TRN2", target_bir_lowering=False, num_devices=1)
    arrays, args = {}, []
    for name in _INS:
        a = _np.ascontiguousarray(inputs[name])
        arrays[f"in_{name}"] = a
        args.append(nc.dram_tensor(f"in_{name}", a.shape, _mybir.dt.from_np(a.dtype), kind="ExternalInput").ap())
    arrays["constants"] = make_constants()
    args.append(nc.dram_tensor("constants", (P, CONST_COLS), F32, kind="ExternalInput").ap())
    args.append(nc.dram_tensor("out", (1, LAT, D), F32, kind="ExternalOutput").ap())
    trunk(nc, *args)
    return _run(nc, [arrays], core_ids=[0]).results[0]["out"]
```

```python
from contextlib import ExitStack

import numpy as np

import concourse.bass as bass
from concourse import mybir

F32 = mybir.dt.float32
F32R = mybir.dt.float32r
ALU = mybir.AluOpType
ACT = mybir.ActivationFunctionType
AX = mybir.AxisListType.X

P = 128
D = 1024
KT = D // P
DEPTH = 2
CTX = 256
LAT = 256
TOK = CTX + LAT
TT = TOK // P
GRID_W = 64
MH, MQK, MV = 4, 128, 256
AH, AKV, AHD = 8, 2, 128
FF = 4 * D
PC = 256
NB = PC // P
NC = D // PC
EPS = 1e-6
ROPE_THETA = 10000.0
ADAS = DEPTH * 6 * NC
EARLY = 2 * NC
MERGE = EARLY + 4 * NC
DIRECT = (0, 4, 6)
RAW = 4
AHEAD = 2
HIGH = 3
KH = KT // 2
KP = 2

SIZES = dict(mq=512, mk=512, mv=1024, mo=1024, mg=16, aq=1024, ak=256, av=256, cu=D, cb=D, cc=D, g0=D, g1=D, g2=D)
COL, _at = {}, 0
for _n, _s in SIZES.items():
    COL[_n] = _at
    _at += _s

ROW_ADA, ROW_N1, ROW_N2, ROW_MN, ROW_CONV, ROW_QN, ROW_KN = 0, 48, 56, 64, 72, 96, 97
ROWS = 98


def make_constants():
    ident = np.eye(P, dtype=np.float32)
    rot = np.zeros((P, P), np.float32)
    for m in range(P):
        if m % 64 < 32:
            rot[m + 32, m] = -1.0
        else:
            rot[m - 32, m] = 1.0
    nf = AHD // 4
    inv = (np.float32(ROPE_THETA) ** (-np.arange(nf, dtype=np.float32) / np.float32(nf))).astype(np.float32)
    t = np.arange(LAT)
    pos = np.stack([t // GRID_W, t % GRID_W]).astype(np.float32)
    d = np.arange(P)
    ang = (pos[d // 64][:, :] * inv[d % 32][:, None]).astype(np.float32)
    sel = np.zeros((P, 4, 8), np.float32)
    for g in range(2):
        for dr in range(2):
            for h in range(MH):
                for part in (0, 32):
                    sel[part + dr * 8 + g * 4 + h, g * 2 + dr, dr * 4 + h] = 1.0
    one_row = np.zeros((P, 8), np.float32)
    for r in range(8):
        one_row[r, r] = one_row[32 + r, r] = 1.0
    return np.concatenate([ident, rot, np.cos(ang), np.sin(ang), sel.reshape(P, 32), one_row], axis=1).astype(np.float32)


CONST_COLS = P + P + LAT + LAT + 32 + 8


def spans(l, d, s):
    if d == 0:
        out = [(P * s, TOK)]
    elif s < CTX // P:
        out = [(0, P * (s + 1)), (CTX, TOK)]
    else:
        out = [(CTX, P * (s + 1))]
    if l == DEPTH - 1:
        out = [(max(a, CTX), b) for a, b in out if b > CTX]
    if len(out) == 2 and out[0][1] == out[1][0]:
        out = [(out[0][0], out[1][1])]
    return out


def m_cols(l, d, a, b):
    o = 0 if l < DEPTH - 1 else d * LAT - CTX
    return slice(a + o, b + o)


def s_cols(l, s, a, b):
    o = (s - CTX // P) * LAT - CTX if s >= CTX // P else 0 if l < DEPTH - 1 else s * LAT - CTX
    return slice(a + o, b + o)


def packed(l, d):
    at, res = 0, []
    for s in range(TT):
        row = []
        for a, b in spans(l, d, s):
            row.append((a, b, at))
            at += b - a
        res.append(row)
    return res


EPW = max(sum(b - a for s in range(TT) for a, b in spans(0, d, s)) for d in range(2))


def make_plan():
    plan = []

    count = dict(panel=0, ada=0)
    owed = []

    def settle(now=True):
        while owed and (now or owed[0][0] <= count["panel"]):
            owed.pop(0)[1]()

    def panel(kind, l, c, b=0):
        plan.append(dict(k="panel", kind=kind, l=l, c=c, b=b))
        count["panel"] += 1
        settle(False)

    def step(k, l, **kw):
        plan.append(dict(k=k, l=l, **kw))

    def ada(n=1):
        for _ in range(n):
            a = count["ada"]
            if a == ADAS:
                return
            count["ada"] += 1
            step("ada", a // (6 * NC), a=a, at=count["panel"])
            owed.append((count["panel"] + 2, lambda a=a: step("adasum", a // (6 * NC), a=a)))
            if a % NC == NC - 1:
                owed.append((count["panel"] + 3, lambda a=a: step("modulation", a // (6 * NC), m=a // NC % 6)))

    def apply(l, n):
        settle()
        step("spread", l, n=n)
        for j in range(NC):
            step("apply", l, n=n, j=j)
        if (l, n) == (0, 1):
            step("first_split", l, p=1)

    for l in range(DEPTH):
        more = l < DEPTH - 1
        if l == 0:
            def add(*which):
                for a in which:
                    step("adasum", l, a=a)

            ada(2)
            add(0)
            step("turn_params", l)
            add(1)
            ada()
            step("turn_x", l, half=0)
            step("turn_x", l, half=1)
            for j in range(NC - 1):
                step("squares", l, n=1, j=j)
            ada()
            add(2)
            ada(2)
            step("squares", l, n=1, j=NC - 1)
            add(4, 3)
            ada(2)
            step("mean", l, n=1)
            step("first_split", l, p=0)
            step("modulation", l, m=0)
            add(6, 5, 7)
            step("modulation", l, m=1)
            owed.clear()
        apply(l, 1)
        panel("mk", l, 0)
        step("gate_tok", l)
        panel("mk", l, 1)
        step("gate_sel", l)
        panel("mq", l, 0)
        step("gate_exp", l)
        panel("mq", l, 1)
        step("gate_scan", l)
        panel("mv", l, 0)
        step("gate_e", l)
        panel("mv", l, 1)
        step("gate_e2", l)
        panel("mv", l, 2)
        step("gate_cols", l)
        panel("mv", l, 3)
        for h in range(MH):
            step("weigh", l, h=h)
            if h:
                step("norm_h", l, h=h - 1)
            panel("mo", l, h)
            if h:
                step("turn", l, h=h - 1)
            step("value", l, h=h)
        step("norm_h", l, h=MH - 1)
        panel("av", l, 0)
        step("turn", l, h=MH - 1)
        panel("ak", l, 0)
        panel("aq", l, 0)
        step("qss", l, j=0)
        panel("aq", l, 1)
        step("qbc", l, j=0)
        step("qss", l, j=1)
        step("qrot", l, j=1)
        panel("aq", l, 2)
        step("qrot", l, j=0)
        step("qss", l, j=2)
        step("qrot", l, j=2)
        beside = [("aq", NC - 1, 0)] + [(k, c, 0) for c in range(NC) for k in ("gate", "proj")] + [("gate", 0, 1)]
        for i in range(AH + 2):
            if i == AH + 1:
                for j in range(3):
                    step("ysplit", l, j=j)
            kind, c, b = beside[i]
            panel(kind, l, c, b)
            if i >= 2:
                step("attend", l, h=i - 2)
            if 1 <= i <= AH:
                step("probs", l, h=i - 1)
            if i < 2:
                step("qss", l, j=3 + i)
                step("qrot", l, j=3 + i)
            if i < AH:
                step("scores", l, h=i)
        step("ysplit", l, j=3)
        for c in range(NC):
            if c:
                panel("gate", l, c, 1)
            panel("proj", l, c, 1)
            if l == 0:
                ada()
        for c in range(NC):
            panel("cc", l, c)
            panel("cu", l, c)
            if l == 0:
                ada()
            panel("cb", l, c)
            if l == 0 and c:
                ada()
        for c in range(NC):
            panel("gate", l, c, 2)
            if l == 0 and c in (1, 2):
                ada()
            if c == NC - 1:
                for j in range(NC - 1):
                    step("msplit", l, j=j)
            panel("proj", l, c, 2)
            if l == 0 and c < NC - 1:
                ada()
        step("msplit", l, j=NC - 1)
        settle()
        for c in range(NC):
            panel("wo", l, c)
            if c:
                step("squares", l, n=2, j=c - 1)
        step("squares", l, n=2, j=NC - 1)
        step("mean", l, n=2)
        apply(l, 2)
        for g in range(FF // D):
            for c in range(NC):
                panel("up", l, c, g)
                ada()
            for c in range(NC):
                panel("down", l, c, g)
                ada()
                if g == FF // D - 1 and c:
                    step("squares", l + 1, n=1, j=c - 1)
                    if not more:
                        step("final_turn", DEPTH, n=1, j=c - 1)
        step("squares", l + 1, n=1, j=NC - 1)
        if more:
            step("mean", l + 1, n=1)
        else:
            step("final_mean", DEPTH, n=1)
            step("final_turn", DEPTH, n=1, j=NC - 1)
    step("final", DEPTH)
    assert count["ada"] == ADAS and not owed

    p = 0
    uses = [0, 0, 0, 0]
    sum_use = {}
    for st in plan:
        if st["k"] == "panel":
            st["p"] = p
            p += 1
        st["u"] = {}

    def use(st, name, bank):
        st["u"][name] = (bank, uses[bank])
        uses[bank] += 1

    start = dict(k="start", l=0, u={})
    use(start, "par2", 3)
    for st in plan:
        k = st["k"]
        if k == "mean":
            use(st, "ss", 3)
        elif k == "spread":
            use(st, "rs", 3)
            spread_use = st["u"]
        elif k == "apply":
            st["u"] = spread_use
        elif k == "final_turn":
            if st["j"] % 2 == 0:
                for tt in range(LAT // P):
                    use(st, tt, 2 * (st["j"] // 2) + tt)
                turn_use = st["u"]
            else:
                st["u"] = turn_use
        elif k == "turn_x":
            for kt in range(KT):
                use(st, kt, (0, 1)[kt % 2])
        elif k == "turn_params":
            for i in range(DEPTH):
                use(st, i, 0)
        elif k == "adasum":
            if st["a"] % NC == 0:
                use(st, 0, (2, 1)[st["a"] // NC % 2])
                sum_use[st["a"] // NC] = st["u"]
            else:
                st["u"] = sum_use[st["a"] // NC]
        elif k == "modulation":
            st["u"] = sum_use[6 * st["l"] + st["m"]]
        elif k == "gate_tok":
            use(st, "g", 1)
        elif k == "gate_sel":
            use(st, "i", 2)
            use(st, "f", 3)
        elif k == "gate_cols":
            use(st, "g", 0)
        elif k == "weigh":
            whole = st["l"] < DEPTH - 1
            for i, name in enumerate(("m0", "m1", "s0", "s1", "s2") if whole else ("m0", "s0", "s2")):
                use(st, name, i % 4)
            if not whole:
                st["u"]["m1"], st["u"]["s1"] = st["u"]["m0"], st["u"]["s0"]
        elif k == "value":
            for tt in range(TT) if st["l"] < DEPTH - 1 else range(CTX // P, TT):
                for d in range(2):
                    use(st, (tt, d), (2 * tt + d) % 4)
        elif k == "turn":
            use(st, 0, 2)
            use(st, 1, 3)
        elif k == "gate_scan":
            st["u"] = next(q for q in plan if q["k"] == "gate_sel" and q["l"] == st["l"])["u"]
        elif k == "qss":
            use(st, 0, 3)
        elif k == "qbc":
            use(st, 0, 0)
            use(st, 1, 1)
        elif k == "qrot":
            use(st, 0, 2)
        elif k in ("scores", "probs"):
            for b in range(3 if st["l"] < DEPTH - 1 else 2):
                use(st, b, b)
        elif k == "attend":
            use(st, 0, 3)
        elif k == "final":
            for j in (0, 2):
                q = next(q for q in plan if q["k"] == "final_turn" and q["j"] == j)
                for tt in range(LAT // P):
                    st["u"][j // 2, tt] = q["u"][tt]
    return [start] + plan, p


PLAN, NPANELS = make_plan()
PANELS = [st for st in PLAN if st["k"] == "panel"]


def panel_no(kind, l, c, b=0):
    return next(st["p"] for st in PANELS if (st["kind"], st["l"], st["c"], st["b"]) == (kind, l, c, b))


def trunk(nc, x, c, ctx_in, c_ctx, w_ada, b_ada, norm1, norm2, w_in, gate_b, mnorm, qnorm, knorm, conv_w,
          w_pm, w_pa, w_pc, w_out, w_up, w_down, fnorm, consts, out):
    ctx = ExitStack()
    with ctx:
        base = (nc.sbuf_base + 63) // 64 * 64

        def at(name, shape, dt, offset):
            return nc.alloc_sbuf_tensor_at(name, shape, dt, offset=base + offset)

        K16 = KT * TOK * 4
        o = 0
        xT = at("xT", [P, KT, TOK], F32, o); o += K16
        hH = at("hH", [P, KT, TOK], F32R, o); o += K16
        hL = at("hL", [P, KT, TOK], F32R, o); o += K16
        raw = at("raw", [P, RAW, KT, PC], F32, o); o += RAW * KT * PC * 4
        wL = at("wL", [P, RAW, KT, PC], F32R, o - RAW * KT * PC * 4)
        wH = at("wH", [P, HIGH, KT, PC], F32R, o); o += HIGH * KT * PC * 4
        Y = o
        yH = at("yH", [P, KT, TOK], F32R, o); o += K16
        yL = at("yL", [P, KT, TOK], F32R, o); o += K16
        names = ["g_rows", "g_back", "f_pre", "f_neg", "f_exp", "log_f", "F_run", "a_run", "e_run"]
        rows = {n: at(n, [16, TOK], F32, Y + i * TOK * 4) for i, n in enumerate(names)}
        rows["a_back"] = at("a_back", [16, TOK], F32, Y + 9 * TOK * 4)
        rows["e_back"] = at("e_back", [16, TOK], F32, Y + 10 * TOK * 4)
        rows["ones"] = at("ones_row", [16, TOK], F32, Y + 11 * TOK * 4)
        rows["M_run"] = at("M_run", [16, TOK], F32, Y + 12 * TOK * 4)
        rows["M_back"] = at("M_back", [16, TOK], F32, Y + 13 * TOK * 4)
        M_parts = [at(f"M_parts{i}", [40, TOK], F32R, Y + (14 + i) * TOK * 4) for i in range(2)]
        for n in ("g_rows", "g_back"):
            rows[n] = at(n + "_parts", [48, TOK], F32, Y + names.index(n) * TOK * 4)
        G = o
        merged = at("merged", [P, KT, TOK], F32, o); o += K16
        panel_bytes = KT * PC * 4
        early = [at(f"ada_early{i}", [P, 4, KT, PC], F32, a) for i, a in enumerate((K16, Y))]
        gaps = [at(f"ada_gap{i}", [P, KT, PC], F32, a)
                for i, a in enumerate((G + K16 + 12352, G + K16 + 22528, G, G + panel_bytes))]
        x_in = at("x_in", [P, TT, D], F32, G)
        qk = at("qk", [P, MH, 2, TOK], F32, G)
        hM = at("hM", [P, MH, TT, MV], F32, G)
        T = o
        vaug = at("vaug", [P, TT, MH, MV + 1], F32, T)
        EP = at("EP", [P, 2, EPW], F32, T + 16448)
        sig_o = at("sig_o", [P, 2, NB, TOK], F32, T + 26688)
        y_tmp = at("y_tmp", [P, NB, TOK], F32, T + 34944)
        junk = at("junk", [P, MV], F32, T + 39040)
        g_col = at("g_col", [P, 4, TT, 8], F32, T + 40320)
        mstat = at("mstat", [P, TT, 6], F32, T + 40832)
        mss = at("mss", [P, TT], F32, T + 40960)
        mrs = at("mrs", [P, TT], F32, T + 41024)
        w_gate = at("w_gate", [P, KT, 16], F32, T + 41088)
        wg = at("wg", [P, KT, P], F32R, T + 26688)
        gb = at("gb", [8, 2], F32, T + 41600)
        v_a = at("v_a", [P, TT, PC], F32, T)
        k_a = at("k_a", [P, NB, TOK], F32, T + 4096)
        q_a = at("q_a", [P, AH, TOK], F32, T + 8192)
        pr = at("pr", [P, 6 * 256], F32, T + 24576)
        prT = at("prT", [P, 6 * 256], F32, T + 30720)
        q_t = at("q_t", [P, NB, LAT], F32, T + 36864)
        c_sb = at("c_sb", [P, NB, TOK], F32, T)
        c_u = at("c_u", [P, NB, 2, LAT + 2], F32, T + 4096)
        c_acc = at("c_acc", [P, NB, 2, LAT], F32, T + 8256)
        n_sq = at("n_sq", [P, 2, 2, TOK], F32, T)
        n_sum = at("n_sum", [P, TOK], F32, T + 8192)
        n_t = at("n_t", [P, 2, TOK], F32, T + 10240)
        n_h = at("n_h", [P, 4, TOK], F32, T + 14336)
        f_out = at("f_out", [P, 2, D], F32, T + 22528)
        f_x = at("f_x", [P, 2, LAT], F32, T + 30720)
        par_rows = [at(f"par_rows{i}", [P, P], F32, T + 30720 + 512 * i) for i in range(3)]
        o = T + 41664
        gs = at("gs", [P, NB, TOK], F32, o); o += NB * TOK * 4
        con = at("con", [P, CONST_COLS], F32, o); o += (CONST_COLS * 4 + 31) // 32 * 32
        small = at("small", [P, 32], F32, o); o += 128
        mean_d, mean_h, eps, one = (small[:, i:i + 1] for i in range(4))
        eps_h = small[:, 12:13]
        n_sd, n_rs = small[:, 4:8], small[:, 8:12]
        q_sd, q_rs = small[:, 16:24], small[:, 24:32]
        pars = [at(f"pars{i}", [P, P if i < 2 else 24], F32, o + 512 * i) for i in range(3)]; o += 1120
        A = o
        acc = at("acc", [P, 2, 2, PC], F32, o); o += 2 * 2 * PC * 4
        modT = at("modT", [P, 2, 48, 2], F32, o); o += 768
        q_sq = at("q_sq", [P, NB, TOK], F32, A)
        q_sc = at("q_sc", [P, AH, TT], F32, o); o += AH * TT * 4
        one_row = at("one_row", [P, 8], F32R, o); o += 32
        c2 = at("c2", [P, KT, 2], F32, o); o += 64
        c2e = at("c2e", [P, KT, 2], F32, o); o += 64
        gain = at("gain", [P, KT, 2], F32, o); o += 64
        amax = at("amax", [P, 4], F32, o); o += 32
        anb = at("anb", [P, 4], F32, o); o += 32
        asum = at("asum", [P, 4], F32, o); o += 32
        ars = at("ars", [P, 4], F32, o); o += 32

        ident, rot = con[:, 0:P], con[:, P:2 * P]
        ropeC, ropeS = con[:, 2 * P:2 * P + LAT], con[:, 2 * P + LAT:2 * P + 2 * LAT]
        sel = con[:, 2 * P + 2 * LAT:CONST_COLS - 8].rearrange("p (g m) -> p g m", g=4)

        pp = ctx.enter_context(nc.psum_tensor("pp", [P, 2, NB, TOK], F32))
        pc = ctx.enter_context(nc.psum_tensor("pc", [P, 4, TOK], F32))

        def sem(name):
            return ctx.enter_context(nc.semaphore(name))

        s_small = sem("small_loaded")
        s_par_rows = sem("param_rows_loaded")
        s_x = [sem(f"x_loaded{i}") for i in range(2)]
        s_wg = sem("gate_weights_loaded")
        s_ada = [sem(f"ada_loaded{i}") for i in range(EARLY + len(gaps))]
        s_tables = sem("tables_loaded")
        acc_ready = sem("ada_sums_ready")
        acc_used = sem("ada_sums_used")
        s_raw = [sem(f"raw_loaded{i}") for i in range(RAW)]
        s_out = sem("out_stored")
        wH_ready = sem("weights_high_ready")
        wL_ready = sem("weights_rest_ready")
        panel_done = sem("panel_done")
        slot_free = [sem(f"slot_free{i}") for i in range(2)]
        full = [sem(f"bank_full{i}") for i in range(4)]
        free = [sem(f"bank_free{i}") for i in range(4)]
        s_const = sem("constants_ready")
        s_silu = sem("silu_ready")
        s_cexp = sem("c_exp_ready")
        s_xt = sem("x_turned")
        s_par = sem("params_ready")
        x_ready = sem("x_pair_ready")
        sd_ready = sem("deviation_ready")
        nrs_ready = sem("reciprocal_ready")
        nsum_ready = sem("square_sums_ready")
        fx_ready = sem("final_x_ready")
        fx_half = sem("final_x_first_tile")
        fa_ready = sem("final_first_half_ready")
        fx_used = sem("final_x_turned")
        wgz_ready = sem("gate_w_zeroed")
        qsd_ready = sem("q_deviation_ready")
        qrs_ready = sem("q_reciprocal_ready")
        mrs_ready = sem("h_deviation_ready")
        ot_ready = sem("h_turned_scaled")
        wLv_ready = sem("weights_rest_vector_ready")
        sq_ready = sem("squares_ready")
        x_half = sem("x_tile_ready")
        sq_half = sem("squares_tile_ready")
        sq_used = sem("squares_added")
        hf_ready = sem("h_float_ready")
        nt_ready = sem("normed_x_ready")
        hc_ready = sem("h_high_context_ready")
        hH_ready = sem("h_high_ready")
        h_ready = sem("h_ready")
        y_ready = sem("y_ready")
        yf_ready = sem("y_float_ready")
        yH_ready = sem("y_high_ready")
        wgH_ready = sem("gate_w_high_ready")
        wg_ready = sem("gate_w_ready")
        gr_ready = sem("gates_rows_ready")
        fneg_ready = sem("f_neg_ready")
        fln_ready = sem("f_ln_ready")
        erow_ready = sem("e_row_ready")
        eexp_ready = sem("e_exp_ready")
        cols_in = sem("gate_cols_inputs")
        gc_ready = sem("gate_cols_ready")
        mqk_ready = sem("mqk_ready")
        mv_ready = sem("mv_ready")
        E_ready = sem("E_ready")
        P_ready = sem("P_ready")
        mask_ready = sem("mask_ready")
        hraw_ready = sem("h_out_ready")
        hss_ready = sem("h_ss_ready")
        hn_ready = sem("h_norm_ready")
        so_exp = sem("sig_o_exp_ready")
        aqk_in = sem("aqk_copied")
        qsq_ready = sem("q_squares_ready")
        kn_ready = sem("k_normed")
        qk_ready = sem("qk_roped")
        av_ready = sem("av_ready")
        nb_ready = sem("neg_max_ready")
        p_exp = sem("p_exp_ready")
        p_ready = sem("p_scaled")
        pT_ready = sem("pT_ready")
        ya_ready = sem("ya_ready")
        gate_exp = sem("gate_exp_ready")
        mt_ready = sem("merge_term_ready")
        m_ready = sem("merged_ready")
        cc_ready = sem("cc_copied")
        cu_ready = sem("cu_ready")
        cpad = sem("conv_pad_zeroed")
        c1_ready = sem("conv_first_tap")
        up_ready = sem("up_relu_ready")
        f_ready = sem("final_rows_ready")
        Mz_ready = sem("M_parts_zeroed")
        MH_ready = sem("M_high_ready")
        Mp_ready = sem("M_parts_ready")
        one_row_ready = sem("one_row_ready")
        dback_ready = sem("M_back_ready")
        vones = sem("value_ones")
        orow = sem("ones_row_ready")

        def cols(l):
            return slice(0, TOK) if l < DEPTH - 1 else slice(CTX, TOK)

        def halves(l):
            return [(slice(CTX, TOK), 0)] + ([(slice(0, CTX), 1)] if l < DEPTH - 1 else [])

        def panel_source(st):
            kind, l, c, b = st["kind"], st["l"], st["c"], st["b"]
            if kind in COL:
                w, at_ = w_in[l], COL[kind]
            elif kind == "gate":
                w, at_ = w_in[l], COL[f"g{b}"]
            elif kind == "proj":
                w, at_ = (w_pm, w_pa, w_pc)[b][l], 0
            elif kind == "wo":
                w, at_ = w_out[l], 0
            elif kind == "up":
                w, at_ = w_up[l], b * D
            else:
                w, at_ = w_down[l][b * D:(b + 1) * D, :], 0
            return w.rearrange("(k p) n -> p k n", p=P)[:, :, at_ + c * PC:at_ + (c + 1) * PC]

        where, before, after = {}, {}, {}
        last_in = {}
        for a in range(ADAS):
            if a < EARLY:
                where[a] = (early[a // 4][:, a % 4, :, :], a)
            else:
                i = (a - EARLY) % 2 if a < MERGE else 1 + (a - MERGE) % 3
                where[a] = (gaps[i][:, :, :], EARLY + i)
            before[a] = last_in.get(where[a][1])
            last_in[where[a][1]] = a
        loads = {}
        for a in range(ADAS):
            loads[a] = 16 * sum(where[q][1] == where[a][1] for q in range(a + 1))
        ada_at = {st["a"]: st["at"] for st in PLAN if st["k"] == "ada"}

        def ada_load_at(a):
            if before[a] is not None:
                free_at = ada_at[before[a]] + 6
            elif a >= MERGE:
                free_at = panel_no("proj", 0, NC - 1, 2) + 5
            else:
                free_at = panel_no("proj", 0, 0, 1) + 4
            return min(free_at, ada_at[a] + 2)

        qk_order = [st["j"] for st in PLAN if st["k"] == "qrot" and st["l"] == 0]
        mean_use = [st["u"]["ss"] for st in PLAN if st["k"] == "mean"]
        summed = [a for a in range(ADAS) if a not in DIRECT]
        sum_no = {a: i for i, a in enumerate(summed)}
        sum_bank = {st["a"]: st["u"][0] for st in PLAN if st["k"] == "adasum"}

        def sums_added(eng, a):
            if a % NC == NC - 1:
                b, n = sum_bank[a]
                eng.wait_ge(full[b], n + 1)
            else:
                eng.wait_ge(acc_used, sum(q <= a and q % NC != NC - 1 for q in summed))

        y_no, h_no = {}, {}
        n_y = n_h_ = n_x = 0
        x_no = {}
        for st in PLAN:
            k, l = st["k"], st["l"]
            if k == "turn":
                y_no[l, "m", st["h"]] = n_y; n_y += 1
            elif k == "ysplit":
                y_no[l, "a", st["j"]] = n_y; n_y += 1
            elif k == "panel" and st["kind"] == "cb":
                y_no[l, "c", st["c"]] = n_y; n_y += 1
            elif k == "panel" and st["kind"] == "up":
                y_no[l, "up", st["b"], st["c"]] = n_y; n_y += 1
            elif k == "apply":
                h_no.setdefault((l, st["n"]), n_h_)
                n_h_ += 2
            elif k == "msplit":
                h_no[l, "m", st["j"]] = n_h_; n_h_ += 1
            elif k == "panel" and st["kind"] in ("wo", "down"):
                x_no[l, st["kind"], st["b"], st["c"]] = n_x; n_x += 1

        taken = [no for key, no in sorted(y_no.items(), key=lambda kv: kv[1]) if key[1] != "a"]
        yf_of = {no: i for i, no in enumerate(taken)}

        def x_needed(st):
            l, n, j = st["l"], st["n"], st["j"]
            if n == 2:
                return x_no[l, "wo", 0, j] + 1
            return x_no[l - 1, "down", FF // D - 1, j] + 1

        def halves_needed(st):
            last = [(q["l"], q["kind"], q["b"]) for q in PANELS if q["kind"] in ("wo", "down") and q["c"] == NC - 1]
            l, n = st["l"], st["n"]
            return last.index((l, "wo", 0) if n == 2 else (l - 1, "down", FF // D - 1)) + 1

        def shift_scale(n):
            return (0, 8) if n == 1 else (24, 32)

        def norm_halves(st):
            return [(slice(CTX, TOK), 0)] + ([(slice(0, CTX), 1)] if norm_cols(st).start == 0 else [])

        def operand(st):
            kind, l, c, b = st["kind"], st["l"], st["c"], st["b"]
            if kind == "proj":
                br = "mac"[b]
                return yH, yL, y_ready, lambda kt: y_no[l, br, kt // 2] + 1
            if kind == "wo":
                return hH, hL, h_ready, lambda kt: h_no[l, "m", kt // 2] + 1
            if kind == "down":
                return yH, yL, y_ready, lambda kt: y_no[l, "up", b, kt // 2] + 1
            n = 2 if kind == "up" else 1
            return hH, hL, h_ready, lambda kt: h_no[l, n] + kt + 1

        def next_panel(st):
            p = st["p"] + AHEAD
            return PANELS[p] if p < NPANELS else None

        def raw_arrived(eng, p):
            eng.wait_ge(s_raw[p % RAW], 16 * (p // RAW + 1))

        def bank(eng, u):
            b, n = u
            eng.wait_ge(full[b], n + 1)
            return pc[:, b, :]

        dchain = sem("vector_chain")

        def spans_tt(l):
            return list(range(TT)) if l < DEPTH - 1 else list(range(CTX // P, TT))

        def norm_cols(st):
            only_latent = st["l"] == DEPTH or (st["l"] == DEPTH - 1 and st["n"] == 2)
            return slice(CTX, TOK) if only_latent else slice(0, TOK)

        block = ctx.enter_context(nc.Block())

        @block.sync
        def _(sp):
            def load_ada(a):
                dst, place_ = where[a]
                l, c_ = a // (6 * NC), a % (6 * NC)
                if before[a] is not None:
                    sp.wait_ge(acc_ready, sum_no[before[a]] + 1)
                elif a >= MERGE:
                    sp.wait_ge(h_ready, h_no[0, "m", NC - 1] + 1)
                elif a >= EARLY:
                    sp.wait_ge(y_ready, y_no[0, "a", NC - 1] + 1)
                sp.dma_start(dst, w_ada[l].rearrange("(k p) n -> p k n", p=P)[:, :, c_ * PC:(c_ + 1) * PC]
                             ).then_inc(s_ada[place_], 16)

            sp.dma_start(con[:, 0:P], consts[:, 0:P]).then_inc(s_small, 16)
            sp.dma_start(par_rows[2][0:8, :], c.rearrange("a (r q) -> (a r) q", q=P)).then_inc(s_small, 16)
            sp.dma_start(par_rows[2][8:16, :], c_ctx.rearrange("(r q) -> r q", q=P)).then_inc(s_small, 16)
            sp.dma_start(par_rows[2][16:24, :], fnorm.rearrange("(r q) -> r q", q=P)).then_inc(s_small, 16)
            load_ada(0)
            load_ada(1)
            for l in range(DEPTH):
                pr_ = par_rows[l]
                for row, src, n in ((ROW_ADA, b_ada[l], 48), (ROW_N1, norm1[l], 8), (ROW_N2, norm2[l], 8),
                                    (ROW_MN, mnorm[l], 8), (ROW_QN, qnorm[l], 1), (ROW_KN, knorm[l], 1)):
                    sp.dma_start(pr_[row:row + n, :], src.rearrange("(r q) -> r q", q=P)).then_inc(s_par_rows, 16)
                sp.dma_start(pr_[ROW_CONV:ROW_CONV + 24, :],
                             conv_w[l].rearrange("k (r q) -> (k r) q", q=P)).then_inc(s_par_rows, 16)
            load_ada(2)
            sp.dma_start(x_in[:, 0:2, :], ctx_in[0].rearrange("(t p) d -> p t d", p=P)).then_inc(s_x[0], 16)
            sp.dma_start(x_in[:, 2:4, :], x[0].rearrange("(t p) d -> p t d", p=P)).then_inc(s_x[1], 16)
            for a in range(3, EARLY):
                load_ada(a)
            sp.dma_start(con[:, P:CONST_COLS], consts[:, P:CONST_COLS]).then_inc(s_tables, 16)
            next_ada = EARLY
            for st in PLAN:
                if st["k"] == "panel" and (st["kind"], st["c"]) == ("mq", 0):
                    l = st["l"]
                    if l:
                        sp.wait_ge(panel_done, panel_no("down", l - 1, NC - 1, FF // D - 1) + 1)
                    else:
                        sp.wait_ge(s_par, 3)
                    sp.dma_start(w_gate[:, :, :], w_in[l].rearrange("(k p) n -> p k n", p=P)[
                        :, :, COL["mg"]:COL["mg"] + 16]).then_inc(s_wg, 16)
                    for g in range(2):
                        for dr in range(2):
                            sp.dma_start(gb[dr * 4:dr * 4 + 4, g:g + 1],
                                         gate_b[l, dr, g].rearrange("(h a) -> h a", a=1)).then_inc(s_wg, 16)
                if st["k"] != "panel":
                    continue
                p = st["p"]
                while next_ada < ADAS and ada_load_at(next_ada) <= p:
                    load_ada(next_ada)
                    next_ada += 1
                if p >= RAW:
                    sp.wait_ge(panel_done, p - RAW + 1)
                sp.dma_start(raw[:, p % RAW, :, :], panel_source(st)).then_inc(s_raw[p % RAW], 16)
            ov = out[0].rearrange("(t p) d -> p t d", p=P)
            for tt in range(2):
                sp.wait_ge(fa_ready, tt + 1)
                sp.wait_ge(f_ready, tt + 1)
                sp.dma_start(ov[:, tt, :], f_out[:, tt, :]).then_inc(s_out, 16)
            sp.wait_ge(s_out, 32)

        @block.tensor
        def _(pe):
            def claim(u):
                b, n = u
                if n:
                    pe.wait_ge(free[b], n)
                return pc[:, b, :]

            def filled(ins, u):
                ins.then_inc(full[u[0]], 1)

            high_of = {h_ready: hH_ready, y_ready: yH_ready}

            def run_panel(st):
                p, kind, l = st["p"], st["kind"], st["l"]
                slot = p % 2
                if p >= 2:
                    pe.wait_ge(slot_free[slot], p // 2)
                hs_, ls_ = p % HIGH, p % RAW

                def split_ready(kt):
                    if kt % KH == 0:
                        pe.wait_ge(wL_ready, 2 * p + kt // KH + 1)
                        pe.wait_ge(wLv_ready, 2 * p + kt // KH + 1)

                hi, lo, ready, need = operand(st)
                if kind in ("mv", "av"):
                    pe.wait_ge(ready, need(KT - 1))
                    split_ready(0)
                    split_ready(KH)
                    for tt in range(TT):
                        dst = pp[:, slot, tt // 2, (tt % 2) * PC:(tt % 2 + 1) * PC]
                        ts_ = slice(tt * P, (tt + 1) * P)
                        for kt in range(KT):
                            pe.matmul(dst, hi[:, kt, ts_], wH[:, hs_, kt, :], start=kt == 0, stop=False)
                            pe.matmul(dst, hi[:, kt, ts_], wL[:, ls_, kt, :], start=False, stop=False)
                            last = pe.matmul(dst, lo[:, kt, ts_], wH[:, hs_, kt, :], start=False, stop=kt == KT - 1)
                    last.then_inc(panel_done, 1)
                    return
                ts_ = slice(0, TOK) if kind in ("mk", "ak") else cols(l)
                seen = 0
                for kt in range(KT):
                    split_ready(kt)
                    dsts = [pp[:, slot, b, ts_] for b in range(NB)]
                    wh = [wH[:, hs_, kt, b * P:(b + 1) * P] for b in range(NB)]
                    wl = [wL[:, ls_, kt, b * P:(b + 1) * P] for b in range(NB)]
                    first, end = kt == 0, kt == KT - 1
                    if need(kt) > seen:
                        seen = need(kt)
                        pe.wait_ge(high_of[ready], seen)
                        for b in range(NB):
                            pe.matmul(dsts[b], wh[b], hi[:, kt, ts_], start=first, stop=False)
                            pe.matmul(dsts[b], wl[b], hi[:, kt, ts_], start=False, stop=False)
                        pe.wait_ge(ready, seen)
                        for b in range(NB):
                            last = pe.matmul(dsts[b], wh[b], lo[:, kt, ts_], start=False, stop=end)
                        continue
                    for b in range(NB):
                        pe.matmul(dsts[b], wh[b], hi[:, kt, ts_], start=first, stop=False)
                        pe.matmul(dsts[b], wh[b], lo[:, kt, ts_], start=False, stop=False)
                        last = pe.matmul(dsts[b], wl[b], hi[:, kt, ts_], start=False, stop=end)
                last.then_inc(panel_done, 1)

            n_norm = 0
            for st in PLAN:
                k, l, u = st["k"], st["l"], st["u"]
                if k == "panel":
                    run_panel(st)
                elif k == "start":
                    pe.wait_ge(s_small, 64)
                    filled(pe.transpose(claim(u["par2"])[:, 0:24], par_rows[2][0:24, :], ident[0:24, 0:24]), u["par2"])
                elif k == "turn_x":
                    half = st["half"]
                    pe.wait_ge(s_x[half], 16)
                    for kt in range(KT):
                        b = claim(u[kt])
                        for i in range(2):
                            last = pe.transpose(b[:, i * P:(i + 1) * P], x_in[:, 2 * half + i, kt * P:(kt + 1) * P], ident)
                        filled(last, u[kt])
                elif k == "turn_params":
                    pe.wait_ge(s_par_rows, 16 * 7 * DEPTH)
                    for i in range(DEPTH):
                        b = claim(u[i])
                        filled(pe.transpose(b[:, 0:ROWS], par_rows[i][0:ROWS, :], ident[0:ROWS, 0:ROWS]), u[i])
                elif k in ("mean", "final_mean"):
                    if k == "mean":
                        b = claim(u["ss"])
                    else:
                        pe.wait_ge(slot_free[NPANELS % 2], NPANELS // 2)
                        b = pp[:, NPANELS % 2, 0, :]
                    n_norm += 1
                    pe.wait_ge(nsum_ready, n_norm)
                    for tt in range(norm_cols(st).start // P, TT):
                        last = pe.matmul(b[:, tt:tt + 1], n_sum[:, tt * P:(tt + 1) * P], mean_d, start=True, stop=True)
                    if k == "mean":
                        filled(last, u["ss"])
                    else:
                        last.then_inc(panel_done, 1)
                elif k == "spread":
                    b = claim(u["rs"])
                    pe.wait_ge(nrs_ready, n_norm)
                    for tt in range(norm_cols(st).start // P, TT):
                        last = pe.matmul(b[:, tt * P:(tt + 1) * P], n_rs[:, tt:tt + 1].to_broadcast([P, P]), ident,
                                         start=True, stop=True)
                    filled(last, u["rs"])
                elif k == "final_turn":
                    j = st["j"]
                    pe.wait_ge(fx_half, j + 1)
                    pe.wait_ge(fx_ready, j + 1)
                    for tt in range(LAT // P):
                        b = claim(u[tt]) if j % 2 == 0 else pc[:, u[tt][0], :]
                        for i in range(2):
                            at_ = (j % 2 * 2 + i) * P
                            last = pe.transpose(b[:, at_:at_ + P], f_x[:, i, tt * P:(tt + 1) * P], ident)
                        if j % 2:
                            filled(last, u[tt])
                        elif tt:
                            last.then_inc(fx_used, 1)
                elif k == "adasum":
                    a = st["a"]
                    b = claim(u[0]) if a % NC == 0 else pc[:, u[0][0], :]
                    if a in DIRECT:
                        w, place_ = where[a]
                        if a == DIRECT[0]:
                            pe.wait_ge(s_silu, 1)
                        pe.wait_ge(s_ada[place_], loads[a])
                        for i in range(NB):
                            n = 2 * (NB * (a % NC) + i)
                            for kt in range(KT):
                                last = pe.matmul(b[:, n:n + 2], w[:, kt, i * P:(i + 1) * P], c2[:, kt, :],
                                                 start=kt == 0, stop=kt == KT - 1)
                    else:
                        if a == summed[0]:
                            pe.wait_ge(s_const, 5)
                        m = sum_no[a]
                        pe.wait_ge(acc_ready, m + 1)
                        for i in range(NB):
                            for v in range(2):
                                n = 2 * (NB * (a % NC) + i) + v
                                last = pe.matmul(b[:, n:n + 1], acc[:, m % 2, v, i * P:(i + 1) * P], one,
                                                 start=True, stop=True)
                    if a % NC == NC - 1:
                        filled(last, u[0])
                    elif a not in DIRECT:
                        last.then_inc(acc_used, 1)
                elif k == "gate_tok":
                    b = claim(u["g"])
                    pe.wait_ge(wg_ready, l + 1)
                    for kt in range(KT):
                        pe.wait_ge(h_ready, h_no[l, 1] + kt + 1)
                        pe.matmul(b[:, :], wg[:, kt, :], hH[:, kt, :], start=kt == 0, stop=False)
                        last = pe.matmul(b[:, :], wg[:, kt, :], hL[:, kt, :], start=False, stop=kt == KT - 1)
                    filled(last, u["g"])
                elif k == "gate_sel":
                    if l == 0:
                        pe.wait_ge(s_tables, 16)
                    pe.wait_ge(gr_ready, 3 * l + 3)
                    for name, g in (("i", 0), ("f", 1)):
                        b = claim(u[name])
                        pe.matmul(b[0:8, :], sel[0:48, 2 * g, :], rows["g_rows"][:, :], start=True, stop=False)
                        last = pe.matmul(b[0:8, :], sel[0:48, 2 * g + 1, :], rows["g_back"][:, :], start=False, stop=True)
                        filled(last, u[name])
                elif k == "gate_cols":
                    b = claim(u["g"])
                    pe.wait_ge(cols_in, 4 * l + 4)
                    for i, name in enumerate(("a_run", "a_back", "e_run", "e_back")):
                        for tt in range(TT):
                            c0 = (i * TT + tt) * 8
                            last = pe.matmul(b[:, c0:c0 + 8], rows[name][0:8, tt * P:(tt + 1) * P], ident[0:8, 0:8],
                                             start=True, stop=True)
                    filled(last, u["g"])
                elif k == "weigh":
                    h = st["h"]
                    if h == 0:
                        pe.wait_ge(Mp_ready, l + 1)
                        pe.wait_ge(one_row_ready, 1)
                    whole = l < DEPTH - 1
                    ts_ = cols(l)
                    for d in range(2):
                        b = claim(u[f"m{d}"]) if whole or d == 0 else b
                        r = d * MH + h
                        last = pe.matmul(b[:, m_cols(l, d, ts_.start, TOK)], one_row[0:40, r:r + 1].to_broadcast([40, P]),
                                         M_parts[d][:, ts_], start=True, stop=True)
                        if whole or d:
                            filled(last, u[f"m{d}"])
                    pe.wait_ge(mqk_ready, 4 * l + 4)
                    for s in range(2):
                        b = claim(u[f"s{s}"]) if whole or s == 0 else b
                        last = pe.matmul(b[:, s_cols(l, s, ts_.start, TOK)], qk[:, h, 1, s * P:(s + 1) * P], qk[:, h, 0, ts_],
                                         start=True, stop=True)
                        if whole or s:
                            filled(last, u[f"s{s}"])
                    b = claim(u["s2"])
                    for s in range(2, 4):
                        last = pe.matmul(b[:, s_cols(l, s, CTX, TOK)], qk[:, h, 1, s * P:(s + 1) * P],
                                         qk[:, h, 0, CTX:TOK], start=True, stop=True)
                    filled(last, u["s2"])
                elif k == "value":
                    h = st["h"]
                    n = l * MH + h + 1
                    pe.wait_ge(P_ready, n)
                    pe.wait_ge(mask_ready, n)
                    pe.wait_ge(mv_ready, MH * l + h + 1)
                    pe.wait_ge(vones, l + 1)
                    for tt in sorted({key[0] for key in u}):
                        for d in range(2):
                            b = claim(u[tt, d])
                            terms = [(s, off + tt * P - a) for s, row in enumerate(packed(l, d)) for a, e, off in row
                                     if a <= tt * P < e]
                            for i, (s, off) in enumerate(terms):
                                last = pe.matmul(b[:, 0:MV + 1], EP[:, d, off:off + P], vaug[:, s, h, :],
                                                 start=i == 0, stop=i == len(terms) - 1)
                            filled(last, u[tt, d])
                elif k == "turn":
                    h = st["h"]
                    tts = range(TT) if l < DEPTH - 1 else range(CTX // P, TT)
                    pe.wait_ge(hn_ready, l * MH + h + 1)
                    for j in range(2):
                        b = claim(u[j])
                        for tt in tts:
                            last = pe.transpose(b[:, tt * P:(tt + 1) * P], hM[:, h, tt, j * P:(j + 1) * P], ident)
                        filled(last, u[j])
                elif k == "qss":
                    j = st["j"]
                    ts_ = slice(0, TOK) if j == 0 else cols(l)
                    pe.wait_ge(qsq_ready, l * 5 + j + 1)
                    b = claim(u[0])
                    for b_ in range(NB):
                        for tt in range(ts_.start // P, TT):
                            n = b_ * TT + (tt + 2) % TT
                            last = pe.matmul(b[:, n:n + 1], q_sq[:, b_, tt * P:(tt + 1) * P], mean_h,
                                             start=True, stop=True)
                    filled(last, u[0])
                elif k == "qbc":
                    j = st["j"]
                    pe.wait_ge(qrs_ready, l * 5 + j + 1)
                    for b_ in range(NB):
                        b = claim(u[b_])
                        for tt in range(TT):
                            n = b_ * TT + (tt + 2) % TT
                            last = pe.matmul(b[:, tt * P:(tt + 1) * P], q_rs[:, n:n + 1].to_broadcast([P, P]), ident,
                                             start=True, stop=True)
                        filled(last, u[b_])
                elif k == "qrot":
                    j = st["j"]
                    if j:
                        pe.wait_ge(aqk_in, l * 5 + j + 1)
                    else:
                        pe.wait_ge(kn_ready, l + 1)
                    b = claim(u[0])
                    for b_ in range(NB):
                        src = k_a[:, b_, CTX:TOK] if j == 0 else q_a[:, 2 * (j - 1) + b_, CTX:TOK]
                        last = pe.matmul(b[:, b_ * LAT:(b_ + 1) * LAT], rot, src, start=True, stop=True)
                    filled(last, u[0])
                elif k == "scores":
                    h = st["h"]
                    kv = h // (AH // AKV)
                    pe.wait_ge(qk_ready, l * 5 + qk_order.index(h // 2 + 1) + 1)
                    if h == 0:
                        pe.wait_ge(qk_ready, l * 5 + qk_order.index(0) + 1)
                    for i in range(2):
                        b = claim(u[i])
                        filled(pe.matmul(b[:, :], q_a[:, h, CTX + i * P:CTX + (i + 1) * P], k_a[:, kv, :],
                                         start=True, stop=True), u[i])
                    if 2 in u:
                        b = claim(u[2])
                        for i in range(2):
                            last = pe.matmul(b[:, i * CTX:(i + 1) * CTX], q_a[:, h, i * P:(i + 1) * P], k_a[:, kv, 0:CTX],
                                             start=True, stop=True)
                        filled(last, u[2])
                elif k == "probs":
                    h = st["h"]
                    pe.wait_ge(p_ready, l * AH + h + 1)
                    for i in range(2):
                        b = claim(u[i])
                        for kt in range(2 * i, 2 * i + 2):
                            for qt in range(2):
                                last = pe.transpose(b[:, (kt % 2) * 256 + qt * P:(kt % 2) * 256 + (qt + 1) * P],
                                                    pr[:, qt * TOK + kt * P:qt * TOK + (kt + 1) * P], ident)
                        filled(last, u[i])
                    if 2 in u:
                        b = claim(u[2])
                        for kt in range(2):
                            for qt in range(2):
                                last = pe.transpose(b[:, kt * 256 + qt * P:kt * 256 + (qt + 1) * P],
                                                    pr[:, 2 * TOK + qt * CTX + kt * P:2 * TOK + qt * CTX + (kt + 1) * P],
                                                    ident)
                        filled(last, u[2])
                elif k == "attend":
                    h = st["h"]
                    kv = h // (AH // AKV)
                    pe.wait_ge(pT_ready, l * AH + h + 1)
                    if h == 0:
                        pe.wait_ge(av_ready, l + 1)
                    b = claim(u[0])
                    if l < DEPTH - 1:
                        for kt in range(2):
                            pe.matmul(b[:, 0:CTX], v_a[:, kt, kv * P:(kv + 1) * P],
                                      prT[:, 2 * TOK + kt * 256:2 * TOK + (kt + 1) * 256], start=kt == 0, stop=kt == 1)
                    for kt in range(4):
                        last = pe.matmul(b[:, CTX:TOK], v_a[:, kt, kv * P:(kv + 1) * P], prT[:, kt * 256:(kt + 1) * 256],
                                         start=kt == 0, stop=kt == 3)
                    filled(last, u[0])

        @block.scalar
        def _(act):
            def split(st):
                p = st["p"]
                raw_arrived(act, p)
                if p >= HIGH:
                    act.wait_ge(panel_done, p - HIGH + 1)
                for a in (0, KH):
                    act.activation(wH[:, p % HIGH, a:a + KH, :], raw[:, p % RAW, a:a + KH, :], ACT.Copy).then_inc(wH_ready, 1)

            def y_high(no, src, kts, ts_):
                act.wait_ge(yf_ready, yf_of[no] + 1)
                act.activation(yH[:, kts, ts_], src, ACT.Copy).then_inc(yH_ready, 1)

            n_norm = n_hf = 0
            for st in PLAN:
                k, l, u = st["k"], st["l"], st["u"]
                if k == "start":
                    act.wait_ge(s_par, 2)
                    act.activation(c2e[:, :, :], c2[:, :, :], ACT.Exp, scale=-1.0).then_inc(s_cexp, 1)
                elif k == "first_split":
                    split(PANELS[st["p"]])
                    if st["p"]:
                        act.wait_ge(s_tables, 16)
                        act.activation(one_row[:, :], con[:, CONST_COLS - 8:CONST_COLS], ACT.Copy).then_inc(one_row_ready, 1)
                elif k == "turn_x":
                    half = st["half"]
                    for kt in range(KT):
                        b = bank(act, u[kt])
                        act.activation(xT[:, kt, half * LAT:(half + 1) * LAT], b[:, 0:LAT], ACT.Copy).then_inc(free[u[kt][0]], 1)
                    for kt in (KT - 2, KT - 1):
                        act.wait_ge(free[u[kt][0]], u[kt][1] + 1)
                    act.sem_inc(s_xt, 1)
                elif k == "panel":
                    nx = next_panel(st)
                    if nx:
                        split(nx)
                    kind, p, c_, b_ = st["kind"], st["p"], st["c"], st["b"]
                    slot = p % 2
                    ts_ = slice(0, TOK) if kind in ("mk", "ak") else cols(l)
                    src = pp[:, slot, :, ts_]
                    if kind in ("mk", "mq"):
                        act.wait_ge(panel_done, p + 1)
                        w = 1 if kind == "mk" else 0
                        act.activation(qk[:, 2 * c_:2 * c_ + 2, w, ts_], src, ACT.Copy,
                                       scale=1.0 if w else float(MQK) ** -0.5).then_inc(mqk_ready, 1)
                        act.wait_ge(mqk_ready, 4 * l + (c_ + 1 if w else 3 + c_))
                        act.sem_inc(slot_free[slot], 1)
                    elif kind == "mo":
                        act.wait_ge(panel_done, p + 1)
                        act.activation(sig_o[:, c_ % 2, :, ts_], src, ACT.Tanh, scale=0.5).then_inc(so_exp, 1)
                        act.wait_ge(so_exp, l * MH + c_ + 1)
                        act.sem_inc(slot_free[slot], 1)
                    elif kind in ("ak", "aq"):
                        j = 0 if kind == "ak" else c_ + 1
                        n = l * 5 + j + 1
                        dst = k_a[:, :, ts_] if kind == "ak" else q_a[:, 2 * c_:2 * c_ + 2, ts_]
                        act.wait_ge(panel_done, p + 1)
                        g = ROW_QN if j else ROW_KN
                        if j:
                            bk, un = next(q for q in PLAN if q["k"] == "qss" and q["l"] == l and q["j"] == j - 1)["u"][0]
                            act.wait_ge(full[bk], un + 1)
                        act.activation(q_sq[:, :, ts_], src, ACT.Square).then_inc(qsq_ready, 1)
                        act.activation(dst, src, ACT.Copy, scale=pars[l][:, g:g + 1]).then_inc(aqk_in, 1)
                        act.wait_ge(qsq_ready, n)
                        act.wait_ge(aqk_in, n)
                        act.sem_inc(slot_free[slot], 1)
                    elif kind == "gate":
                        n = (l * 3 + b_) * NC + c_
                        act.wait_ge(panel_done, p + 1)
                        if n:
                            act.wait_ge(m_ready, n)
                        act.activation(gs[:, :, ts_], src, ACT.Tanh, scale=0.5).then_inc(gate_exp, 1)
                        act.wait_ge(gate_exp, n + 1)
                        act.sem_inc(slot_free[slot], 1)
                    elif kind == "cc":
                        act.wait_ge(panel_done, p + 1)
                        if c_:
                            act.wait_ge(cu_ready, l * NC + c_)
                        act.activation(c_sb[:, :, ts_], src, ACT.Copy).then_inc(cc_ready, 1)
                        act.wait_ge(cc_ready, l * NC + c_ + 1)
                        act.sem_inc(slot_free[slot], 1)
                    elif kind == "cu":
                        act.wait_ge(cu_ready, l * NC + c_ + 1)
                        if c_:
                            act.wait_ge(yf_ready, yf_of[y_no[l, "c", c_ - 1]] + 1)
                        sg = slice(0, 2) if l < DEPTH - 1 else slice(1, 2)
                        for b in range(NB):
                            wt = pars[l][:, ROW_CONV + 2 * c_ + b:ROW_CONV + 2 * c_ + b + 1]
                            act.activation(c_acc[:, b, sg, :], c_u[:, b, sg, 0:LAT], ACT.Copy, scale=wt).then_inc(c1_ready, 1)
                    elif kind == "cb":
                        y_high(y_no[l, "c", c_], y_tmp[:, :, ts_], slice(2 * c_, 2 * c_ + 2), ts_)
                    elif kind == "up":
                        act.wait_ge(panel_done, p + 1)
                        no = y_no[l, "up", b_, c_]
                        act.wait_ge(y_ready, no)
                        act.activation(y_tmp[:, :, ts_], src, ACT.Relu).then_inc(up_ready, 1)
                        act.wait_ge(up_ready, (l * 4 + b_) * NC + c_ + 1)
                        act.sem_inc(slot_free[slot], 1)
                        y_high(no, y_tmp[:, :, ts_], slice(2 * c_, 2 * c_ + 2), ts_)
                elif k == "squares":
                    j, ts_ = st["j"], norm_cols(st)
                    if l == 0 and st["n"] == 1:
                        act.wait_ge(s_xt, 2)
                    elif j == NC - 1:
                        act.wait_ge(x_ready, x_needed(st) - 1)
                        act.wait_ge(x_half, halves_needed(st))
                    else:
                        act.wait_ge(x_ready, x_needed(st))
                    if l == 0 and st["n"] == 2 and j == 0:
                        act.wait_ge(acc_ready, sum_no[MERGE])
                    if j == 0 and n_norm:
                        act.wait_ge(sq_used, 5 * n_norm)
                    elif j == 1 and n_norm:
                        act.wait_ge(nsum_ready, n_norm)
                    elif j >= 2:
                        act.wait_ge(sq_used, 5 * n_norm + 2 * j - 3)
                    if j == NC - 1:
                        act.activation(n_sq[:, 1, 0, ts_], xT[:, KT - 2, ts_], ACT.Square).then_inc(sq_half, 1)
                        if not (l == 0 and st["n"] == 1):
                            act.wait_ge(x_ready, x_needed(st))
                        act.activation(n_sq[:, 1, 1, ts_], xT[:, KT - 1, ts_], ACT.Square).then_inc(sq_ready, 1)
                    else:
                        act.activation(n_sq[:, j % 2, :, ts_], xT[:, 2 * j:2 * j + 2, ts_], ACT.Square).then_inc(sq_ready, 1)
                elif k in ("mean", "final_mean"):
                    t0 = norm_cols(st).start // P
                    n_norm += 1
                    if n_norm == 1:
                        act.wait_ge(s_const, 5)
                    if k == "mean":
                        b = bank(act, u["ss"])
                    else:
                        act.wait_ge(panel_done, NPANELS + 1)
                        b = pp[:, NPANELS % 2, 0, :]
                    act.activation(n_sd[:, t0:TT], b[:, t0:TT], ACT.Sqrt, bias=eps).then_inc(sd_ready, 1)
                elif k == "final_turn":
                    j = st["j"]
                    act.wait_ge(x_ready, x_needed(st))
                    if j:
                        if j % 2:
                            act.wait_ge(fx_used, j // 2 + 1)
                        else:
                            for tt in range(LAT // P):
                                act.wait_ge(full[u0[tt][0]], u0[tt][1] + 1)
                    u0 = u
                    for i in range(2):
                        g = 16 + 2 * j + i
                        last = act.activation(f_x[:, i, :], xT[:, 2 * j + i, CTX:TOK], ACT.Copy, scale=pars[2][:, g:g + 1])
                        if i == 0:
                            last.then_inc(fx_half, 1)
                    last.then_inc(fx_ready, 1)
                elif k == "final":
                    act.wait_ge(nrs_ready, n_norm)
                    for tt in range(LAT // P):
                        b = bank(act, u[0, tt])
                        act.activation(f_out[:, tt, 0:D // 2], b[:, :], ACT.Copy,
                                       scale=n_rs[:, CTX // P + tt:CTX // P + tt + 1]).then_inc(fa_ready, 1)
                elif k == "qss":
                    j = st["j"]
                    b = bank(act, u[0])
                    t0 = 0 if j == 0 else cols(l).start // P
                    if l * 5 + j:
                        act.wait_ge(qrs_ready, l * 5 + j)
                    act.activation(q_sd.rearrange("p (b t) -> p b t", b=NB)[:, :, 0:TT - t0],
                                   b[:, 0:NB * TT].rearrange("p (b t) -> p b t", b=NB)[:, :, 0:TT - t0],
                                   ACT.Sqrt, bias=eps_h if j else eps, scale=float(AHD) if j else 1.0).then_inc(qsd_ready, 1)
                elif k == "apply":
                    ts_ = slice(0, TOK) if not (l == DEPTH - 1 and st["n"] == 2) else cols(l)
                    j = st["j"]
                    if j == 0 and st["n"] == 2:
                        act.wait_ge(panel_done, panel_no("wo", l, NC - 1) + 1)
                    elif j == 0 and l:
                        act.wait_ge(panel_done, panel_no("up", l - 1, NC - 1, 3) + 1)
                    for kt in (2 * j, 2 * j + 1):
                        act.wait_ge(nt_ready, n_hf + 1)
                        n_hf += 1
                        sh, _ = shift_scale(st["n"])
                        for hs, v in norm_halves(st):
                            i = act.activation(hH[:, kt, hs], n_t[:, kt % 2, hs], ACT.Identity,
                                               scale=gain[:, kt, v:v + 1], bias=modT[:, l, sh + kt, v:v + 1])
                            i.then_inc(hc_ready if v == 0 and len(norm_halves(st)) == 2 else hH_ready, 1)
                    if st["n"] == 1 and j == 0:
                        act.wait_ge(s_wg, 80 * (l + 1))
                        act.wait_ge(wgz_ready, l + 1)
                        act.activation(wg[:, :, 0:16], w_gate[:, :, :], ACT.Copy).then_inc(wgH_ready, 1)
                elif k == "gate_exp":
                    act.wait_ge(fneg_ready, l + 1)
                    act.activation(rows["f_exp"][0:8, :], rows["f_neg"][0:8, :], ACT.Exp).then_inc(fln_ready, 1)
                    act.wait_ge(fln_ready, 2 * l + 1)
                    act.activation(rows["f_exp"][0:8, :], rows["f_exp"][0:8, :], ACT.Ln, bias=1.0).then_inc(fln_ready, 1)
                elif k == "gate_e":
                    act.wait_ge(erow_ready, l + 1)
                    act.wait_ge(dback_ready, l + 1)
                    act.wait_ge(Mz_ready, 2 * l + 2)
                    for i, n in enumerate(("M_run", "M_back")):
                        act.activation(M_parts[i][0:8, :], rows[n][0:8, :], ACT.Copy).then_inc(MH_ready, 1)
                    act.activation(rows["e_run"][0:8, :], rows["e_run"][0:8, :], ACT.Exp).then_inc(eexp_ready, 1)
                elif k == "weigh":
                    h = st["h"]
                    act.wait_ge(gc_ready, l + 1)
                    if h:
                        bk, un = list(next(q for q in PLAN if q["k"] == "value" and q["l"] == l and q["h"] == h - 1)["u"].values())[-1]
                        act.wait_ge(full[bk], un + 1)
                    for d in range(2):
                        b = bank(act, u[f"m{d}"])
                        for s, row in enumerate(packed(l, d)):
                            for a, e, off in row:
                                last = act.activation(EP[:, d, off:off + e - a], b[:, m_cols(l, d, a, e)], ACT.Exp, scale=-1.0,
                                                      bias=g_col[:, d, s, d * MH + h:d * MH + h + 1])
                                frees = (s, a) == (TT - 1, row[-1][0]) and (l < DEPTH - 1 or d)
                                last.then_inc(free[u[f"m{d}"][0]] if frees else E_ready, 1)
                elif k in ("value", "norm_h"):
                    h, tts = st["h"], spans_tt(l)
                    for tt in tts[:-1] if k == "value" else tts[-1:]:
                        act.wait_ge(hraw_ready, h_count(l, h, tt))
                        if tt > tts[0]:
                            act.wait_ge(hss_ready, h_count(l, h, tt - 1))
                        act.activation(junk[:, :], hM[:, h, tt, :], ACT.Square, accum_out=mss[:, tt:tt + 1]).then_inc(hss_ready, 1)
                    if k == "value":
                        continue
                    act.wait_ge(hss_ready, h_count(l, h, TT - 1))
                    act.activation(mrs[:, tts[0]:TT], mss[:, tts[0]:TT], ACT.Sqrt, scale=1.0 / MV, bias=eps).then_inc(mrs_ready, 1)
                elif k == "turn":
                    h = st["h"]
                    act.wait_ge(y_ready, y_no[l, "m", h])
                    for j in range(2):
                        b = bank(act, u[j])
                        r = ROW_MN + 2 * h + j
                        act.activation(y_tmp[:, j, cols(l)], b[:, cols(l)], ACT.Copy,
                                       scale=pars[l][:, r:r + 1]).then_inc(free[u[j][0]], 1)
                    for j in range(2):
                        act.wait_ge(free[u[j][0]], u[j][1] + 1)
                    act.sem_inc(ot_ready, 1)
                    y_high(y_no[l, "m", h], y_tmp[:, :, cols(l)], slice(2 * h, 2 * h + 2), cols(l))
                elif k == "scores":
                    h = st["h"]
                    act.wait_ge(nb_ready, l * AH + h + 1)
                    for qt in range(2):
                        b = bank(act, u[qt])
                        act.activation(pr[:, qt * TOK:(qt + 1) * TOK], b[:, :], ACT.Exp, bias=anb[:, qt:qt + 1],
                                       scale=q_sc[:, h, qt:qt + 1], accum_out=asum[:, qt:qt + 1]).then_inc(p_exp, 1)
                    if 2 in u:
                        b = bank(act, u[2])
                        for qt in range(2):
                            act.activation(pr[:, 2 * TOK + qt * CTX:2 * TOK + (qt + 1) * CTX], b[:, qt * CTX:(qt + 1) * CTX],
                                           ACT.Exp, bias=anb[:, 2 + qt:3 + qt], scale=q_sc[:, h, 2 + qt:3 + qt],
                                           accum_out=asum[:, 2 + qt:3 + qt]).then_inc(p_exp, 1)
                elif k == "attend":
                    h = st["h"]
                    b = bank(act, u[0])
                    act.activation(q_a[:, h, cols(l)], b[:, cols(l)], ACT.Copy).then_inc(free[u[0][0]], 1)
                elif k == "ysplit":
                    j = st["j"]
                    no = y_no[l, "a", j]
                    bk, un = next(q for q in PLAN if q["k"] == "attend" and q["l"] == l and q["h"] == 2 * j + 1)["u"][0]
                    act.wait_ge(free[bk], un + 1)
                    act.wait_ge(panel_done, panel_no("proj", l, NC - 1, 0) + 1)
                    act.activation(yH[:, 2 * j:2 * j + 2, cols(l)], q_a[:, 2 * j:2 * j + 2, cols(l)],
                                   ACT.Copy).then_inc(yH_ready, 1)
                elif k == "msplit":
                    j = st["j"]
                    act.wait_ge(m_ready, (l * 3 + 2) * NC + j + 1)
                    act.wait_ge(panel_done, panel_no("gate", l, NC - 1, 2) + 1)
                    act.activation(hH[:, 2 * j:2 * j + 2, cols(l)], merged[:, 2 * j:2 * j + 2, cols(l)],
                                   ACT.Copy).then_inc(hH_ready, 1)

        @block.gpsimd
        def _(pool):
            pool.memset(one, 1.0).then_inc(s_const, 1)
            pool.memset(eps_h, EPS * AHD).then_inc(s_const, 1)
            pool.memset(mean_d, 1.0 / D).then_inc(s_const, 1)
            pool.memset(mean_h, 1.0 / AHD).then_inc(s_const, 1)
            pool.memset(eps, EPS).then_inc(s_const, 1)

            def split(st):
                p = st["p"]
                for i in range(2):
                    ks = slice(i * KH, i * KH + KP)
                    pool.wait_ge(wH_ready, 2 * p + i + 1)
                    pool.tensor_tensor(wL[:, p % RAW, ks, :], raw[:, p % RAW, ks, :], wH[:, p % HIGH, ks, :].bitcast(F32),
                                       ALU.subtract).then_inc(wL_ready, 1)

            def y_rest(no, src, kts, ts_):
                pool.wait_ge(yH_ready, no + 1)
                pool.tensor_tensor(yL[:, kts, ts_], src, yH[:, kts, ts_].bitcast(F32), ALU.subtract).then_inc(y_ready, 1)

            n_norm = n_hf = n_hc = 0
            for st in PLAN:
                k, l, u = st["k"], st["l"], st["u"]
                if k == "panel":
                    nx = next_panel(st)
                    if nx:
                        split(nx)
                    kind, c_, b_ = st["kind"], st["c"], st["b"]
                    ts_ = cols(l)
                    if kind == "proj":
                        n = (l * 3 + b_) * NC + c_
                        pool.wait_ge(mt_ready, n + 1)
                        if b_ == 0:
                            pool.sem_inc(m_ready, 1)
                        else:
                            m = merged[:, 2 * c_:2 * c_ + 2, ts_]
                            pool.tensor_tensor(m, m, gs[:, :, ts_], ALU.add).then_inc(m_ready, 1)
                    elif kind == "cc" and c_ == 0:
                        pool.wait_ge(y_ready, y_no[l, "a", 3] + 1)
                        pool.wait_ge(panel_done, panel_no("gate", l, 1, 1) + 1)
                        pool.memset(c_u[:, :, :, 0:1], 0.0).then_inc(cpad, 1)
                        pool.memset(c_u[:, :, :, LAT + 1:LAT + 2], 0.0).then_inc(cpad, 1)
                    elif kind == "cb":
                        y_rest(y_no[l, "c", c_], y_tmp[:, :, ts_], slice(2 * c_, 2 * c_ + 2), ts_)
                elif k == "first_split":
                    split(PANELS[st["p"]])
                elif k == "squares" and st["j"] < NC - 1:
                    j, ts_ = st["j"], norm_cols(st)
                    pool.wait_ge(sq_ready, NC * n_norm + j + 1)
                    sq, to = n_sq[:, j % 2, :, ts_], n_sum[:, ts_]
                    if j == 0:
                        if n_norm:
                            pool.wait_ge(full[mean_use[n_norm - 1][0]], mean_use[n_norm - 1][1] + 1)
                        pool.tensor_tensor(to, sq[:, 0, :], sq[:, 1, :], ALU.add).then_inc(sq_used, 1)
                    else:
                        pool.wait_ge(sq_used, 5 * n_norm + 2 * j - 1)
                        pool.tensor_tensor(to, to, sq[:, 0, :], ALU.add).then_inc(sq_used, 1)
                        pool.wait_ge(sq_used, 5 * n_norm + 2 * j)
                        pool.tensor_tensor(to, to, sq[:, 1, :], ALU.add).then_inc(sq_used, 1)
                elif k == "squares":
                    n_norm += 1
                elif k == "apply":
                    ts_ = slice(0, TOK) if not (l == DEPTH - 1 and st["n"] == 2) else cols(l)
                    j = st["j"]
                    if st["n"] == 1 and j == 0:
                        if l:
                            pool.wait_ge(panel_done, panel_no("down", l - 1, NC - 1, FF // D - 1) + 1)
                        else:
                            pool.wait_ge(s_par, 3)
                        pool.memset(wg[:, :, :].bitcast(F32), 0.0).then_inc(wgz_ready, 1)
                    for kt in (2 * j, 2 * j + 1):
                        n_hf += 1
                        pool.wait_ge(hf_ready, n_hf)
                        if norm_cols(st).start == 0:
                            n_hc += 1
                            pool.wait_ge(hc_ready, n_hc)
                        pool.wait_ge(hH_ready, h_no[l, st["n"]] + kt + 1)
                        pool.tensor_tensor(hL[:, kt, ts_], n_h[:, kt % 4, ts_], hH[:, kt, ts_].bitcast(F32),
                                           ALU.subtract).then_inc(h_ready, 1)
                    if st["n"] == 1 and j == 0:
                        pool.wait_ge(wgH_ready, l + 1)
                        pool.tensor_tensor(wg[:, :, 32:48], w_gate[:, :, :], wg[:, :, 0:16].bitcast(F32),
                                           ALU.subtract).then_inc(wg_ready, 1)
                    if st["n"] == 1 and j == NC - 1:
                        pool.wait_ge(h_ready, h_no[l, 1] + KT)
                        pool.memset(vaug[:, :, :, MV:MV + 1], 1.0).then_inc(vones, 1)
                        pool.memset(rows["ones"][0:8, :], 1.0).then_inc(orow, 1)
                        for t in M_parts:
                            pool.memset(t[:, :].bitcast(F32), 0.0).then_inc(Mz_ready, 1)
                elif k == "weigh":
                    h = st["h"]
                    pool.wait_ge(P_ready, l * MH + h + 1)
                    last = None
                    for d in range(2):
                        for s, row in enumerate(packed(l, d)):
                            for a, e, off in row:
                                if a <= s * P < e:
                                    v = EP[:, d, off + s * P - a:off + s * P - a + P]
                                    sign = 1 if d == 0 else -1
                                    last = pool.affine_select(out=v, in_=v, compare_op=ALU.is_ge, fill=0.0, base=0,
                                                              pattern=[[sign, P]], channel_multiplier=-sign)
                    last.then_inc(mask_ready, 1)
                elif k == "turn":
                    h = st["h"]
                    y_rest(y_no[l, "m", h], y_tmp[:, :, cols(l)], slice(2 * h, 2 * h + 2), cols(l))
                elif k == "ysplit":
                    j = st["j"]
                    y_rest(y_no[l, "a", j], q_a[:, 2 * j:2 * j + 2, cols(l)], slice(2 * j, 2 * j + 2), cols(l))
                elif k == "msplit":
                    j = st["j"]
                    pool.wait_ge(hH_ready, h_no[l, "m", j] + 1)
                    pool.tensor_tensor(hL[:, 2 * j:2 * j + 2, cols(l)], merged[:, 2 * j:2 * j + 2, cols(l)],
                                       hH[:, 2 * j:2 * j + 2, cols(l)].bitcast(F32), ALU.subtract).then_inc(h_ready, 1)


        @block.vector
        def _(dve):
            count = [0]

            def link(ins):
                count[0] += 1
                ins.then_inc(dchain, 1)
                dve.wait_ge(dchain, count[0])

            def start_link(ins):
                count[0] += 1
                ins.then_inc(dchain, 1)

            def freed(ins, u):
                ins.then_inc(free[u[0]], 1)

            def split(st):
                p = st["p"]
                for i in range(2):
                    ks = slice(i * KH + KP, (i + 1) * KH)
                    dve.wait_ge(wH_ready, 2 * p + i + 1)
                    dve.tensor_tensor(wL[:, p % RAW, ks, :], raw[:, p % RAW, ks, :], wH[:, p % HIGH, ks, :].bitcast(F32),
                                      ALU.subtract).then_inc(wLv_ready, 1)

            def sums(a):
                w, place_ = where[a]
                n = sum_no[a]
                if n == 0:
                    dve.wait_ge(s_silu, 1)
                dve.wait_ge(s_ada[place_], loads[a])
                if n >= 2:
                    sums_added(dve, summed[n - 2])
                for kt in range(KT):
                    for v in range(2):
                        to, cv = acc[:, n % 2, v, :], c2[:, kt, v:v + 1]
                        if kt == 0:
                            i = dve.tensor_scalar(to, w[:, kt, :], cv, None, ALU.mult)
                        else:
                            dve.wait_ge(dchain, count[0] - 1)
                            i = dve.scalar_tensor_tensor(out=to, in0=w[:, kt, :], scalar=cv, in1=to, op0=ALU.mult, op1=ALU.add)
                        if (kt, v) != (KT - 1, 1):
                            start_link(i)
                dve.wait_ge(dchain, count[0])
                i.then_inc(acc_ready, 1)

            n_norm = n_half = n_nt = 0
            for st in PLAN:
                k, l, u = st["k"], st["l"], st["u"]
                if k == "start":
                    up = u["par2"]
                    freed(dve.tensor_copy(pars[2][:, :], bank(dve, up)[:, 0:24]), up)
                    dve.wait_ge(free[up[0]], up[1] + 1)
                    dve.tensor_copy(c2[:, :, 0], pars[2][:, 0:8]).then_inc(s_par, 1)
                    dve.tensor_copy(c2[:, :, 1], pars[2][:, 8:16]).then_inc(s_par, 1)
                    dve.wait_ge(s_par, 2)
                    dve.wait_ge(s_cexp, 1)
                    link(dve.tensor_scalar(c2e[:, :, :], c2e[:, :, :], 1.0, None, ALU.add))
                    link(dve.reciprocal(c2e[:, :, :], c2e[:, :, :]))
                    dve.tensor_tensor(c2[:, :, :], c2[:, :, :], c2e[:, :, :], ALU.mult).then_inc(s_silu, 1)
                elif k == "ada":
                    if st["a"] not in DIRECT:
                        sums(st["a"])
                elif k == "first_split":
                    split(PANELS[st["p"]])
                elif k == "turn_params":
                    for i in range(DEPTH):
                        up = u[i]
                        freed(dve.tensor_copy(pars[i][:, 0:ROWS], bank(dve, up)[:, 0:ROWS]), up)
                    for i in range(DEPTH):
                        dve.wait_ge(free[u[i][0]], u[i][1] + 1)
                    for i in range(DEPTH):
                        v = pars[i][:, ROW_MN:ROW_MN + 8]
                        start_link(dve.tensor_scalar(v, v, 0.5, None, ALU.mult))
                    dve.wait_ge(dchain, count[0])
                    dve.sem_inc(s_par, 1)
                elif k == "panel":
                    nx = next_panel(st)
                    if nx:
                        split(nx)
                    kind, p, c_, b_ = st["kind"], st["p"], st["c"], st["b"]
                    slot = p % 2
                    ts_ = cols(l)
                    src = pp[:, slot, :, ts_]
                    if kind in ("mv", "av"):
                        dve.wait_ge(panel_done, p + 1)
                        dst = vaug[:, :, c_, 0:MV] if kind == "mv" else v_a[:, :, :]
                        done = mv_ready if kind == "mv" else av_ready
                        dve.tensor_copy(dst, pp[:, slot, :, :].rearrange("p b (t n) -> p (b t) n", t=2)).then_inc(done, 1)
                        dve.wait_ge(done, MH * l + c_ + 1 if kind == "mv" else l + 1)
                        dve.sem_inc(slot_free[slot], 1)
                    elif kind == "proj":
                        dve.wait_ge(panel_done, p + 1)
                        dst = merged[:, 2 * c_:2 * c_ + 2, ts_] if b_ == 0 else gs[:, :, ts_]
                        dve.wait_ge(gate_exp, (l * 3 + b_) * NC + c_ + 1)
                        dve.scalar_tensor_tensor(out=dst, in0=gs[:, :, ts_], scalar=1.0, in1=src,
                                                 op0=ALU.add, op1=ALU.mult).then_inc(mt_ready, 1)
                        dve.wait_ge(mt_ready, (l * 3 + b_) * NC + c_ + 1)
                        dve.sem_inc(slot_free[slot], 1)
                    elif kind == "cu":
                        dve.wait_ge(panel_done, p + 1)
                        dve.wait_ge(cc_ready, l * NC + c_ + 1)
                        if c_ == 0:
                            dve.wait_ge(cpad, 2 * l + 2)
                        sg = slice(0, 2) if l < DEPTH - 1 else slice(1, 2)
                        n = sg.stop - sg.start
                        for b in range(NB):
                            i = dve.tensor_tensor(c_u[:, b, sg, 1:LAT + 1],
                                                  pp[:, slot, b, ts_].rearrange("p (s t) -> p s t", s=n),
                                                  c_sb[:, b, ts_].rearrange("p (s t) -> p s t", s=n), ALU.mult)
                            if b < NB - 1:
                                start_link(i)
                        i.then_inc(cu_ready, 1)
                        dve.wait_ge(dchain, count[0])
                        dve.wait_ge(cu_ready, l * NC + c_ + 1)
                        dve.sem_inc(slot_free[slot], 1)
                        dve.wait_ge(c1_ready, (l * NC + c_ + 1) * NB)
                        for tap in (1, 2):
                            for b in range(NB):
                                r = ROW_CONV + tap * 8 + 2 * c_ + b
                                start_link(dve.scalar_tensor_tensor(
                                    out=c_acc[:, b, sg, :], in0=c_u[:, b, sg, tap:tap + LAT], scalar=pars[l][:, r:r + 1],
                                    in1=c_acc[:, b, sg, :], op0=ALU.mult, op1=ALU.add))
                            dve.wait_ge(dchain, count[0])
                    elif kind == "cb":
                        dve.wait_ge(panel_done, p + 1)
                        no = y_no[l, "c", c_]
                        dve.wait_ge(y_ready, no)
                        sg = slice(0, 2) if l < DEPTH - 1 else slice(1, 2)
                        for b in range(NB):
                            i = dve.tensor_tensor(y_tmp[:, b, ts_], pp[:, slot, b, ts_],
                                                  c_acc[:, b, sg, :].rearrange("p s t -> p (s t)"), ALU.mult)
                            if b < NB - 1:
                                start_link(i)
                        dve.wait_ge(dchain, count[0])
                        i.then_inc(yf_ready, 1)
                        dve.wait_ge(yf_ready, yf_of[no] + 1)
                        dve.sem_inc(slot_free[slot], 1)
                    elif kind == "up":
                        dve.wait_ge(up_ready, (l * 4 + b_) * NC + c_ + 1)
                        dve.tensor_tensor(y_tmp[:, :, ts_], y_tmp[:, :, ts_], y_tmp[:, :, ts_], ALU.mult).then_inc(yf_ready, 1)
                        no = y_no[l, "up", b_, c_]
                        kts = slice(2 * c_, 2 * c_ + 2)
                        dve.wait_ge(yH_ready, no + 1)
                        dve.tensor_tensor(yL[:, kts, ts_], y_tmp[:, :, ts_], yH[:, kts, ts_].bitcast(F32),
                                          ALU.subtract).then_inc(y_ready, 1)
                    elif kind in ("wo", "down"):
                        dve.wait_ge(panel_done, p + 1)
                        g = 16 if kind == "wo" else 40
                        n = x_no[l, kind, b_, c_]
                        for b in range(NB):
                            kt = 2 * c_ + b
                            for hs, v in halves(l):
                                i = dve.scalar_tensor_tensor(out=xT[:, kt, hs], in0=pp[:, slot, b, hs],
                                                             scalar=modT[:, l, g + kt, v:v + 1], in1=xT[:, kt, hs],
                                                             op0=ALU.mult, op1=ALU.add)
                                if (b, v) != (NB - 1, halves(l)[-1][1]):
                                    if c_ == NC - 1 and (b, v) == (0, halves(l)[-1][1]):
                                        i.then_inc(x_half, 1)
                                        n_half += 1
                                    else:
                                        start_link(i)
                        i.then_inc(x_ready, 1)
                        dve.wait_ge(x_half, n_half)
                        dve.wait_ge(dchain, count[0])
                        dve.wait_ge(x_ready, n + 1)
                        dve.sem_inc(slot_free[slot], 1)
                elif k == "modulation":
                    m = st["m"]
                    b = bank(dve, u[0])
                    dst = modT[:, l, KT * m:KT * (m + 1), :]
                    bias = pars[l][:, ROW_ADA + KT * m:ROW_ADA + KT * (m + 1)].unsqueeze(2).to_broadcast([P, KT, 2])
                    freed(dve.tensor_tensor(dst, b[:, 0:2 * KT].rearrange("p (k v) -> p k v", v=2), bias, ALU.add), u[0])
                    dve.wait_ge(free[u[0][0]], u[0][1] + 1)
                    if m == 2:
                        link(dve.tensor_scalar(dst, dst, 0.5, None, ALU.mult))
                elif k == "squares" and st["j"] == NC - 1:
                    ts_ = norm_cols(st)
                    sq, to = n_sq[:, 1, :, ts_], n_sum[:, ts_]
                    n_norm += 1
                    dve.wait_ge(sq_used, 5 * n_norm)
                    dve.wait_ge(sq_half, n_norm)
                    link(dve.tensor_tensor(to, to, sq[:, 0, :], ALU.add))
                    dve.wait_ge(sq_ready, NC * n_norm)
                    dve.tensor_tensor(to, to, sq[:, 1, :], ALU.add).then_inc(nsum_ready, 1)
                elif k in ("mean", "final_mean"):
                    t0 = norm_cols(st).start // P
                    dve.wait_ge(sd_ready, n_norm)
                    if k == "mean":
                        dve.sem_inc(free[u["ss"][0]], 1)
                    dve.reciprocal(n_rs[:, t0:TT], n_sd[:, t0:TT]).then_inc(nrs_ready, 1)
                elif k == "apply":
                    n = st["n"]
                    ts_, hv = norm_cols(st), norm_halves(st)
                    sh, sc = shift_scale(n)
                    r = ROW_N1 if n == 1 else ROW_N2
                    if st["j"] == 0:
                        for v in range(2):
                            start_link(dve.scalar_tensor_tensor(out=gain[:, :, v], in0=modT[:, l, sc:sc + 8, v], scalar=1.0,
                                                                in1=pars[l][:, r:r + 8], op0=ALU.add, op1=ALU.mult))
                        dve.wait_ge(dchain, count[0])
                    n_r = bank(dve, u["rs"])
                    for kt in (2 * st["j"], 2 * st["j"] + 1):
                        if kt >= 2:
                            dve.wait_ge(hH_ready, h_no[l, n] + kt - 1)
                        i = dve.tensor_tensor(n_t[:, kt % 2, ts_], xT[:, kt, ts_], n_r[:, ts_], ALU.mult)
                        i.then_inc(nt_ready, 1)
                        n_nt += 1
                        dve.wait_ge(nt_ready, n_nt)
                        if kt == KT - 1:
                            dve.sem_inc(free[u["rs"][0]], 1)
                        if kt >= 4:
                            dve.wait_ge(h_ready, h_no[l, n] + kt - 3)
                        for hs, v in hv:
                            i = dve.tensor_scalar(n_h[:, kt % 4, hs], n_t[:, kt % 2, hs], gain[:, kt, v:v + 1],
                                                  modT[:, l, sh + kt, v:v + 1], ALU.mult, ALU.add)
                            if (hs, v) != hv[-1]:
                                start_link(i)
                        i.then_inc(hf_ready, 1)
                elif k == "gate_tok":
                    b = bank(dve, u["g"])
                    dve.tensor_copy(rows["g_rows"][:, :], b[0:48, :]).then_inc(gr_ready, 1)
                    dve.wait_ge(gr_ready, 3 * l + 1)
                    dve.sem_inc(free[u["g"][0]], 1)
                    dve.tensor_copy(rows["g_back"][:, 0:CTX], rows["g_rows"][:, CTX - 1::-1]).then_inc(gr_ready, 1)
                    dve.tensor_copy(rows["g_back"][:, CTX:TOK], rows["g_rows"][:, TOK - 1:CTX - 1:-1]).then_inc(gr_ready, 1)
                elif k == "gate_sel":
                    R = {n: t[0:8, :] for n, t in rows.items()}
                    if l == 0:
                        dve.wait_ge(s_tables, 16)
                    dve.wait_ge(s_wg, 80 * (l + 1))
                    b = bank(dve, u["f"])
                    freed(dve.tensor_scalar(R["f_pre"], b[0:8, :], gb[0:8, 1:2], None, ALU.add), u["f"])
                    dve.wait_ge(free[u["f"][0]], u["f"][1] + 1)
                    dve.scalar_tensor_tensor(out=R["f_neg"], in0=R["f_pre"], scalar=-1.0, in1=R["f_pre"],
                                             op0=ALU.mult, op1=ALU.min).then_inc(fneg_ready, 1)
                elif k == "gate_scan":
                    R = {n: t[0:8, :] for n, t in rows.items()}
                    dve.wait_ge(fln_ready, 2 * l + 2)
                    link(dve.scalar_tensor_tensor(out=R["log_f"], in0=R["f_pre"], scalar=0.0, in1=R["f_exp"],
                                                  op0=ALU.min, op1=ALU.subtract))
                    dve.wait_ge(orow, l + 1)
                    link(dve.tensor_tensor_scan(R["F_run"], R["ones"], R["log_f"], 0.0, ALU.mult, ALU.add))
                    b = bank(dve, u["i"])
                    dve.scalar_tensor_tensor(out=R["a_run"], in0=b[0:8, :], scalar=gb[0:8, 0:1], in1=R["F_run"],
                                             op0=ALU.add, op1=ALU.subtract).then_inc(cols_in, 1)
                    dve.wait_ge(cols_in, 4 * l + 1)
                    dve.sem_inc(free[u["i"][0]], 1)
                    link(dve.tensor_tensor_scan(R["M_run"], R["a_run"], R["a_run"], 0.0, ALU.max, ALU.max))
                    dve.scalar_tensor_tensor(out=R["e_run"], in0=R["F_run"], scalar=-1.0, in1=R["M_run"],
                                             op0=ALU.mult, op1=ALU.subtract).then_inc(erow_ready, 1)
                    for nm, fr in (("M_back", "M_run"), ("a_back", "a_run")):
                        start_link(dve.tensor_copy(R[nm][:, 0:CTX], R[fr][:, CTX - 1::-1]))
                        i = dve.tensor_copy(R[nm][:, CTX:TOK], R[fr][:, TOK - 1:CTX - 1:-1])
                        if nm == "M_back":
                            start_link(i)
                        else:
                            i.then_inc(cols_in, 1)
                    dve.wait_ge(dchain, count[0])
                    dve.sem_inc(dback_ready, 1)
                elif k == "gate_e2":
                    R = {n: t[0:8, :] for n, t in rows.items()}
                    dve.wait_ge(MH_ready, 2 * l + 2)
                    for i, n in enumerate(("M_run", "M_back")):
                        start_link(dve.tensor_tensor(M_parts[i][32:40, :], R[n], M_parts[i][0:8, :].bitcast(F32), ALU.subtract))
                    dve.wait_ge(dchain, count[0])
                    dve.sem_inc(Mp_ready, 1)
                    dve.wait_ge(eexp_ready, l + 1)
                    dve.tensor_copy(R["e_back"][:, 0:CTX], R["e_run"][:, CTX - 1::-1]).then_inc(cols_in, 1)
                    dve.tensor_copy(R["e_back"][:, CTX:TOK], R["e_run"][:, TOK - 1:CTX - 1:-1]).then_inc(cols_in, 1)
                elif k == "gate_cols":
                    b = bank(dve, u["g"])
                    dve.tensor_copy(g_col[:, :, :, :], b[:, 0:4 * TT * 8].rearrange("p (i t n) -> p i t n", i=4, t=TT)
                                    ).then_inc(gc_ready, 1)
                    dve.wait_ge(gc_ready, l + 1)
                    dve.sem_inc(free[u["g"][0]], 1)
                elif k == "weigh":
                    h = st["h"]
                    whole = l < DEPTH - 1
                    for d in range(2):
                        dve.wait_ge(free[u[f"m{d}"][0]], u[f"m{d}"][1] + 1)
                    dve.wait_ge(E_ready, e_count(l, h))
                    for s in range(TT):
                        us = u[f"s{min(s, 2)}"]
                        b = bank(dve, us)
                        todo = [(d, a, e, off) for d in range(2) for a, e, off in packed(l, d)[s]]
                        for n, (d, a, e, off) in enumerate(todo):
                            v = EP[:, d, off:off + e - a]
                            i = dve.tensor_tensor(v, v, b[:, s_cols(l, s, a, e)], ALU.mult)
                            if n == len(todo) - 1 and (s in (1, 3) or whole and s == 0):
                                freed(i, us)
                            else:
                                start_link(i)
                    for name in ("s0", "s1", "s2"):
                        dve.wait_ge(free[u[name][0]], u[name][1] + 1)
                    dve.wait_ge(dchain, count[0])
                    dve.sem_inc(P_ready, 1)
                elif k == "value":
                    h = st["h"]
                    tts = spans_tt(l)
                    for tt in tts:
                        bs = [bank(dve, u[tt, d]) for d in range(2)]
                        for d in range(2):
                            start_link(dve.tensor_scalar(mstat[:, tt, d:d + 1], bs[d][:, MV:MV + 1], -1.0,
                                                         g_col[:, 2 + d, tt, d * MH + h:d * MH + h + 1], ALU.mult, ALU.max))
                        dve.wait_ge(dchain, count[0])
                        for d in range(2):
                            start_link(dve.tensor_scalar(mstat[:, tt, 2 + d:3 + d], bs[d][:, MV:MV + 1],
                                                         mstat[:, tt, d:d + 1], None, ALU.max))
                        dve.wait_ge(dchain, count[0])
                        link(dve.reciprocal(mstat[:, tt, 4:6], mstat[:, tt, 2:4]))
                        dve.tensor_scalar(hM[:, h, tt, :], bs[0][:, 0:MV], mstat[:, tt, 4:5], None,
                                          ALU.mult).then_inc(free[u[tt, 0][0]], 1)
                        dve.wait_ge(free[u[tt, 0][0]], u[tt, 0][1] + 1)
                        dve.scalar_tensor_tensor(out=hM[:, h, tt, :], in0=bs[1][:, 0:MV], scalar=mstat[:, tt, 5:6],
                                                 in1=hM[:, h, tt, :], op0=ALU.mult, op1=ALU.add).then_inc(hraw_ready, 1)
                        dve.wait_ge(hraw_ready, h_count(l, h, tt))
                        dve.sem_inc(free[u[tt, 1][0]], 1)
                elif k == "norm_h":
                    h, tts = st["h"], spans_tt(l)
                    dve.wait_ge(mrs_ready, l * MH + h + 1)
                    rs = mrs[:, tts[0]:TT]
                    link(dve.reciprocal(rs, rs))
                    for tt in tts:
                        i = dve.tensor_scalar(hM[:, h, tt, :], hM[:, h, tt, :], mrs[:, tt:tt + 1], None, ALU.mult)
                        if tt < TT - 1:
                            start_link(i)
                    i.then_inc(hn_ready, 1)
                elif k == "turn":
                    h = st["h"]
                    ts_ = cols(l)
                    dve.wait_ge(ot_ready, l * MH + h + 1)
                    v = y_tmp[:, :, ts_]
                    dve.scalar_tensor_tensor(out=v, in0=sig_o[:, h % 2, :, ts_], scalar=1.0, in1=v,
                                             op0=ALU.add, op1=ALU.mult).then_inc(yf_ready, 1)
                elif k == "qss":
                    j = st["j"]
                    t0 = 0 if j == 0 else cols(l).start // P
                    dve.wait_ge(qsd_ready, l * 5 + j + 1)
                    dve.sem_inc(free[u[0][0]], 1)
                    to = q_sc[:, 2 * j - 2:2 * j, :] if j else q_rs.rearrange("p (b t) -> p b t", b=NB)
                    dve.reciprocal(to[:, :, 0:TT - t0], q_sd.rearrange("p (b t) -> p b t", b=NB)[:, :, 0:TT - t0]
                                   ).then_inc(qrs_ready, 1)
                elif k == "qbc":
                    for b_ in range(NB):
                        b = bank(dve, u[b_])
                        freed(dve.tensor_tensor(k_a[:, b_, :], k_a[:, b_, :], b[:, :], ALU.mult), u[b_])
                    for b_ in range(NB):
                        dve.wait_ge(free[u[b_][0]], u[b_][1] + 1)
                    dve.sem_inc(kn_ready, 1)
                elif k == "qrot":
                    j = st["j"]
                    dve.wait_ge(dchain, count[0])
                    if l * 5 + qk_order.index(j):
                        dve.wait_ge(qk_ready, l * 5 + qk_order.index(j))
                    b = bank(dve, u[0])
                    dst = [k_a[:, b_, CTX:TOK] if j == 0 else q_a[:, 2 * j - 2 + b_, CTX:TOK] for b_ in range(NB)]
                    for b_ in range(NB):
                        i = dve.tensor_tensor(q_t[:, b_, :], b[:, b_ * LAT:(b_ + 1) * LAT], ropeS, ALU.mult)
                        if b_ < NB - 1:
                            start_link(i)
                        else:
                            freed(i, u[0])
                        start_link(dve.tensor_tensor(dst[b_], dst[b_], ropeC, ALU.mult))
                    dve.wait_ge(dchain, count[0])
                    dve.wait_ge(free[u[0][0]], u[0][1] + 1)
                    start_link(dve.tensor_tensor(dst[0], dst[0], q_t[:, 0, :], ALU.add))
                    dve.tensor_tensor(dst[1], dst[1], q_t[:, 1, :], ALU.add).then_inc(qk_ready, 1)
                elif k == "scores":
                    h = st["h"]
                    nq = 4 if 2 in u else 2
                    for qt in range(2):
                        b = bank(dve, u[qt])
                        start_link(dve.reduce_max(amax[:, qt:qt + 1], b[:, :], AX))
                    if 2 in u:
                        b = bank(dve, u[2])
                        start_link(dve.reduce_max(amax[:, 2:4], b[:, :].rearrange("p (q k) -> p q k", q=2), AX))
                    dve.wait_ge(dchain, count[0])
                    dve.wait_ge(qrs_ready, l * 5 + h // 2 + 2)
                    dve.scalar_tensor_tensor(out=anb[:, 0:nq], in0=amax[:, 0:nq], scalar=-1.0, in1=q_sc[:, h, 0:nq],
                                             op0=ALU.mult, op1=ALU.mult).then_inc(nb_ready, 1)
                    dve.wait_ge(p_exp, p_count(l, h))
                    for i in range(3 if 2 in u else 2):
                        dve.sem_inc(free[u[i][0]], 1)
                    link(dve.reciprocal(ars[:, 0:nq], asum[:, 0:nq]))
                    for qt in range(nq):
                        a = qt * TOK if qt < 2 else 2 * TOK + (qt - 2) * CTX
                        v = pr[:, a:a + (TOK if qt < 2 else CTX)]
                        i = dve.tensor_scalar(v, v, ars[:, qt:qt + 1], None, ALU.mult)
                        if qt < nq - 1:
                            start_link(i)
                    dve.wait_ge(dchain, count[0])
                    i.then_inc(p_ready, 1)
                elif k == "probs":
                    h = st["h"]
                    nb = 3 if 2 in u else 2
                    for i in range(nb):
                        b = bank(dve, u[i])
                        freed(dve.tensor_copy(prT[:, i * TOK:(i + 1) * TOK], b[:, :]), u[i])
                    for i in range(nb):
                        dve.wait_ge(free[u[i][0]], u[i][1] + 1)
                    dve.sem_inc(pT_ready, 1)
                elif k == "final":
                    dve.wait_ge(nrs_ready, n_norm)
                    for tt in range(LAT // P):
                        b = bank(dve, u[1, tt])
                        dve.tensor_scalar(f_out[:, tt, D // 2:D], b[:, :], n_rs[:, CTX // P + tt:CTX // P + tt + 1], None,
                                          ALU.mult).then_inc(f_ready, 1)


def e_count(l, h):
    per = [sum(len(r) for d in range(2) for r in packed(q, d)) - (2 if q < DEPTH - 1 else 1) for q in range(DEPTH)]
    return sum(per[q] * MH for q in range(l)) + per[l] * (h + 1)


def h_count(l, h, tt):
    n = [TT if q < DEPTH - 1 else TT - CTX // P for q in range(DEPTH)]
    first = TT - n[l]
    return sum(n[q] * MH for q in range(l)) + n[l] * h + tt - first + 1


def p_count(l, h):
    n = [4 if q < DEPTH - 1 else 2 for q in range(DEPTH)]
    return sum(n[q] * AH for q in range(l)) + n[l] * (h + 1)


_INS = ["x", "c", "ctx", "c_ctx", "w_ada", "b_ada", "norm1", "norm2", "w_in", "mlstm_gate_b", "mlstm_norm", "q_norm",
        "k_norm", "conv_w", "w_proj_m", "w_proj_a", "w_proj_c", "w_out", "w_up", "w_down", "final_norm"]


def kernel(**inputs):
    import numpy as _np
    import concourse.bacc as _bacc
    from concourse import mybir as _mybir
    from concourse.bass_utils import run_bass_kernel_spmd as _run

    nc = _bacc.Bacc("TRN2", target_bir_lowering=False, num_devices=1)
    arrays, args = {}, []
    for name in _INS:
        a = _np.ascontiguousarray(inputs[name])
        arrays[f"in_{name}"] = a
        args.append(nc.dram_tensor(f"in_{name}", a.shape, _mybir.dt.from_np(a.dtype), kind="ExternalInput").ap())
    arrays["constants"] = make_constants()
    args.append(nc.dram_tensor("constants", (P, CONST_COLS), F32, kind="ExternalInput").ap())
    args.append(nc.dram_tensor("out", (1, LAT, D), F32, kind="ExternalOutput").ap())
    trunk(nc, *args)
    return _run(nc, [arrays], core_ids=[0]).results[0]["out"]
```
